# Optimizing a Trainium2 kernel written in Bass

```python
import math
import jax, jax.numpy as jnp
from jax import lax
import numpy as np

D_MODEL = 1024
BATCH = 1
SEQ = 256
DEPTH = 1

MEM_LEN = 256
D_MIX = D_MODEL
HEAD_DIM = 64
NSA_HEADS = 8
NSA_KV_GROUPS = 2
NSA_HPG = NSA_HEADS // NSA_KV_GROUPS
CMP_BLOCK = 32
CMP_STRIDE = 16
SLC_BLOCK = 64
SLC_TOPK = 16
WINDOW = 512
Q_BLOCK = 128
RWKV_HEADS = 8
RWKV_DIM = RWKV_HEADS * HEAD_DIM
DECAY_LORA = 64
ICLR_LORA = 64
GATE_LORA = 128
GN_EPS = HEAD_DIM * 1e-5
X_HEADS = 4
X_HEAD_DIM = D_MODEL // X_HEADS
N_EXPERTS = 32
TOP_K = 4
D_EXPERT = D_MODEL
SWIGLU_LIMIT = 7.0
SWIGLU_ALPHA = 1.702
MOE_ROW_BLOCK = 256
RMS_EPS = 1e-6
NEG_INF = -1e30
BIG = 1e9

NSA_SPLITS = (NSA_HEADS * HEAD_DIM,) + (NSA_KV_GROUPS * HEAD_DIM,) * 6 + (NSA_HEADS * 3,)
RWKV_SPLITS = (RWKV_DIM, RWKV_DIM, RWKV_DIM, DECAY_LORA, ICLR_LORA, GATE_LORA)
NSA_PROJ = sum(NSA_SPLITS)
RWKV_PROJ = sum(RWKV_SPLITS)
P_TOTAL = NSA_PROJ + RWKV_PROJ

kernel_name = "nsa_rwkv7_hybrid_moe_block"

def rms_norm(x, g):
    xf = x.astype(jnp.float32)
    y = xf * lax.rsqrt(jnp.mean(xf * xf, axis=-1, keepdims=True) + RMS_EPS)
    return (y * g.astype(jnp.float32)).astype(x.dtype)

def split_cols(p, sizes):
    return jnp.split(p, np.cumsum(sizes)[:-1].tolist(), axis=-1)

def masked_softmax(s, mask):
    return jax.nn.softmax(jnp.where(mask, s, NEG_INF), axis=-1) * mask

def alibi_slopes(n):
    return (2.0 ** (-8.0 * np.arange(1, n + 1) / n)).astype(np.float32)

def nsa_mixer(p, q_g, kc_g, ks_g, kw_g, pe_k, pe_v, ck_w1, ck_w2, cv_w1, cv_w2):
    B, S, _ = p.shape
    H, G, HPG, Dh = NSA_HEADS, NSA_KV_GROUPS, NSA_HPG, HEAD_DIM
    scale = Dh ** -0.5
    n_sub = CMP_BLOCK // CMP_STRIDE
    n_cmp = S // CMP_STRIDE - n_sub + 1
    n_sel = S // SLC_BLOCK
    n_top = min(SLC_TOPK, n_sel)
    nq = S // Q_BLOCK

    q, kc, vc, ks, vs, kw, vw, gl = split_cols(p, NSA_SPLITS)
    q = rms_norm(q.reshape(B, S, H, Dh), q_g)

    def compress(t, pe, w1, w2):
        ch = t.reshape(B, S // CMP_STRIDE, CMP_STRIDE, G, Dh)
        blk = jnp.concatenate([ch[:, j:j + n_cmp] for j in range(n_sub)], axis=2)
        blk = blk + pe[None, None, :, None, :]
        blk = blk.transpose(0, 3, 1, 2, 4).reshape(B, G, n_cmp, CMP_BLOCK * Dh)
        return jax.nn.silu(blk @ w1) @ w2

    k_cmp = rms_norm(compress(kc.reshape(B, S, G, Dh), pe_k, ck_w1, ck_w2), kc_g)
    v_cmp = compress(vc.reshape(B, S, G, Dh), pe_v, cv_w1, cv_w2)
    k_slc = rms_norm(ks.reshape(B, S, G, Dh), ks_g).transpose(0, 2, 1, 3).reshape(B, G, n_sel, SLC_BLOCK, Dh)
    v_slc = vs.reshape(B, S, G, Dh).transpose(0, 2, 1, 3).reshape(B, G, n_sel, SLC_BLOCK, Dh)
    pad = ((0, 0), (0, 0), (WINDOW, 0), (0, 0))
    k_win = jnp.pad(rms_norm(kw.reshape(B, S, G, Dh), kw_g).transpose(0, 2, 1, 3), pad)
    v_win = jnp.pad(vw.reshape(B, S, G, Dh).transpose(0, 2, 1, 3), pad)
    gates = jax.nn.sigmoid(gl.astype(jnp.float32)).astype(p.dtype)

    q_blocks = q.reshape(B, nq, Q_BLOCK, G, HPG, Dh).transpose(1, 0, 3, 4, 2, 5)
    g_blocks = gates.reshape(B, nq, Q_BLOCK, G, HPG, 3).transpose(1, 0, 3, 4, 2, 5)
    t0s = jnp.arange(nq, dtype=jnp.int32) * Q_BLOCK

    slopes = jnp.asarray(alibi_slopes(H)).reshape(1, G, HPG, 1, 1)
    c_start = np.arange(n_cmp) * CMP_STRIDE
    c_end_np = c_start + CMP_BLOCK
    s_start = np.arange(n_sel) * SLC_BLOCK
    overlap = jnp.asarray((np.clip(np.minimum(c_end_np[:, None], s_start[None] + SLC_BLOCK)
                                   - np.maximum(c_start[:, None], s_start[None]), 0, None)
                           / CMP_BLOCK).astype(np.float32))
    c_last = jnp.asarray(c_end_np - 1, dtype=jnp.int32)
    b_ix = jnp.arange(B)[:, None, None, None]
    g_ix = jnp.arange(G)[None, :, None, None]
    bid = jnp.arange(n_sel, dtype=jnp.int32)
    win_off = jnp.arange(WINDOW + Q_BLOCK, dtype=jnp.int32)
    slc_off = jnp.arange(SLC_BLOCK, dtype=jnp.int32)

    def block(args):
        qb, gb, t0 = args
        t = t0 + jnp.arange(Q_BLOCK, dtype=jnp.int32)
        tq = t[:, None]
        dc = tq - c_last[None, :]
        s = jnp.einsum('bghqd,bgcd->bghqc', qb, k_cmp).astype(jnp.float32) * scale - slopes * dc.astype(jnp.float32)
        p_c = masked_softmax(s, dc >= 0)
        o_c = jnp.einsum('bghqc,bgcd->bghqd', p_c.astype(v_cmp.dtype), v_cmp)
        imp = jnp.einsum('bghqc,cn->bgqn', p_c, overlap)
        cur = tq // SLC_BLOCK
        forced = (bid[None] == 0) | (bid[None] == cur) | (bid[None] == cur - 1)
        score = jnp.where(forced, BIG, jnp.where(bid[None] * SLC_BLOCK <= tq, imp, -BIG))
        _, idx = lax.top_k(score, n_top)
        kg = k_slc[b_ix, g_ix, idx].reshape(B, G, Q_BLOCK, n_top * SLC_BLOCK, Dh)
        vg = v_slc[b_ix, g_ix, idx].reshape(B, G, Q_BLOCK, n_top * SLC_BLOCK, Dh)
        kpos = (idx[..., None] * SLC_BLOCK + slc_off).reshape(B, G, Q_BLOCK, n_top * SLC_BLOCK)
        ds = (t[None, None, :, None] - kpos)[:, :, None]
        s = jnp.einsum('bghqd,bgqkd->bghqk', qb, kg).astype(jnp.float32) * scale - slopes * ds.astype(jnp.float32)
        p_s = masked_softmax(s, ds >= 0)
        o_s = jnp.einsum('bghqk,bgqkd->bghqd', p_s.astype(vg.dtype), vg)
        kb = lax.dynamic_slice_in_dim(k_win, t0, WINDOW + Q_BLOCK, axis=2)
        vb = lax.dynamic_slice_in_dim(v_win, t0, WINDOW + Q_BLOCK, axis=2)
        spos = t0 - WINDOW + win_off
        dw = tq - spos[None]
        s = jnp.einsum('bghqd,bgkd->bghqk', qb, kb).astype(jnp.float32) * scale - slopes * dw.astype(jnp.float32)
        p_w = masked_softmax(s, (spos[None] >= 0) & (dw >= 0) & (dw < WINDOW))
        o_w = jnp.einsum('bghqk,bgkd->bghqd', p_w.astype(vb.dtype), vb)
        o = gb[..., 0:1] * o_c + gb[..., 1:2] * o_s + gb[..., 2:3] * o_w
        return o.astype(qb.dtype)

    outs = lax.map(block, (q_blocks, g_blocks, t0s))
    return outs.transpose(1, 0, 4, 2, 3, 5).reshape(B, S, H * Dh)

def wkv7_scan(r, w, k, v, a, b):
    B, S, H, N = r.shape
    xs = tuple(jnp.moveaxis(t.astype(jnp.float32), 1, 0) for t in (r, w, k, v, a, b))

    def step(state, inp):
        r_t, w_t, k_t, v_t, a_t, b_t = inp
        sa = jnp.einsum('bhij,bhj->bhi', state, a_t)
        state = state * w_t[:, :, None, :] + sa[..., None] * b_t[:, :, None, :] + v_t[..., None] * k_t[:, :, None, :]
        return state, jnp.einsum('bhij,bhj->bhi', state, r_t)

    _, ys = lax.scan(step, jnp.zeros((B, H, N, N), jnp.float32), xs)
    return jnp.moveaxis(ys, 0, 1)

def rwkv7_mixer(p, mu, w0, w_up, a0, a_up, g_up, k_k, k_a, r_k, ln_w, ln_b):
    B, S, _ = p.shape
    H, N = RWKV_HEADS, HEAD_DIM
    prev = jnp.pad(p, ((0, 0), (1, 0), (0, 0)))[:, :-1]
    p = p + (prev - p) * mu
    r, k, v, wd, ad, gd = split_cols(p, RWKV_SPLITS)
    w = -jax.nn.softplus(-(w0 + jnp.tanh(wd) @ w_up)) - 0.5
    a = jax.nn.sigmoid(a0 + ad @ a_up)
    g = jax.nn.sigmoid(gd) @ g_up
    hs = lambda t: t.reshape(B, S, H, N)
    kk = hs(k * k_k).astype(jnp.float32)
    kk = kk / jnp.maximum(jnp.sqrt(jnp.sum(kk * kk, axis=-1, keepdims=True)), 1e-12)
    k = k * (1.0 + (a - 1.0) * k_a)
    decay = jnp.exp(-jnp.exp(w.astype(jnp.float32)))
    r_, k_, v_, a_ = hs(r), hs(k), hs(v), hs(a).astype(jnp.float32)
    y = wkv7_scan(r_, hs(decay), k_, v_, -kk, kk * a_)
    mean = jnp.mean(y, axis=-1, keepdims=True)
    var = jnp.mean(jnp.square(y - mean), axis=-1, keepdims=True)
    y = ((y - mean) * lax.rsqrt(var + GN_EPS)).reshape(B, S, RWKV_DIM).astype(p.dtype) * ln_w + ln_b
    y = y + (jnp.sum(r_ * k_ * r_k, axis=-1, keepdims=True) * v_).reshape(B, S, RWKV_DIM)
    return y * g

def memory_cross_attention(hn, memn, xq_w, xk_w, xv_w, xq_g, xk_g, xo_w):
    B, S, D = hn.shape
    M = memn.shape[1]
    q = rms_norm((hn @ xq_w).reshape(B, S, X_HEADS, X_HEAD_DIM), xq_g)
    k = rms_norm((memn @ xk_w).reshape(B, M, X_HEADS, X_HEAD_DIM), xk_g)
    v = (memn @ xv_w).reshape(B, M, X_HEADS, X_HEAD_DIM)
    s = jnp.einsum('bshd,bmhd->bhsm', q, k).astype(jnp.float32) * (X_HEAD_DIM ** -0.5)
    pr = jax.nn.softmax(s, axis=-1)
    o = jnp.einsum('bhsm,bmhd->bshd', pr.astype(v.dtype), v).reshape(B, S, D)
    return o @ xo_w

def clamped_swiglu(h):
    hg = jnp.minimum(h[..., ::2], SWIGLU_LIMIT)
    hl = jnp.clip(h[..., 1::2], -SWIGLU_LIMIT, SWIGLU_LIMIT)
    return hg * jax.nn.sigmoid(SWIGLU_ALPHA * hg) * (hl + 1.0)

def moe_ffn(x, router_w, router_b, mlp1_w, mlp1_b, mlp2_w, mlp2_b):
    B, S, D = x.shape
    T = B * S
    A = T * TOP_K
    M = MOE_ROW_BLOCK
    xt = x.reshape(T, D)
    logits = (xt @ router_w + router_b).astype(jnp.float32)
    top_v, top_i = lax.top_k(logits, TOP_K)
    gate = jax.nn.softmax(top_v, axis=-1)
    e_flat = top_i.reshape(A)
    order = jnp.argsort(e_flat, stable=True)
    e_sorted = e_flat[order]
    counts = jnp.bincount(e_flat, length=N_EXPERTS)
    starts = jnp.cumsum(counts) - counts
    padded = (counts + M - 1) // M * M
    pends = jnp.cumsum(padded)
    pstarts = pends - padded
    dest = pstarts[e_sorted] + jnp.arange(A) - starts[e_sorted]
    n_blocks = -(-A // M) + N_EXPERTS
    R = n_blocks * M
    row_tok = jnp.full((R,), T, jnp.int32).at[dest].set((order // TOP_K).astype(jnp.int32))
    row_w = jnp.zeros((R,), jnp.float32).at[dest].set(gate.reshape(A)[order])
    blk_e = jnp.minimum(jnp.searchsorted(pends, jnp.arange(n_blocks) * M, side='right'), N_EXPERTS - 1)
    xpad = jnp.concatenate([xt, jnp.zeros((1, D), xt.dtype)], axis=0)

    def expert_block(args):
        tok, wr, e = args
        hb = xpad[tok] @ mlp1_w[e] + mlp1_b[e]
        yb = clamped_swiglu(hb) @ mlp2_w[e] + mlp2_b[e]
        return yb * wr[:, None].astype(yb.dtype)

    ys = lax.map(expert_block, (row_tok.reshape(n_blocks, M), row_w.reshape(n_blocks, M), blk_e))
    y = jax.ops.segment_sum(ys.reshape(R, D), row_tok, num_segments=T + 1)[:T]
    return y.reshape(B, S, D).astype(x.dtype)

def hybrid_layer(h, mem, norm_mix_g, w_in, q_norm_g, k_cmp_norm_g, k_slc_norm_g, k_win_norm_g,
                 cmp_pe_k, cmp_pe_v, cmp_k_w1, cmp_k_w2, cmp_v_w1, cmp_v_w2,
                 rwkv_mu, rwkv_w0, rwkv_w_up, rwkv_a0, rwkv_a_up, rwkv_g_up, rwkv_k_k, rwkv_k_a,
                 rwkv_r_k, rwkv_ln_w, rwkv_ln_b, w_out,
                 norm_x_g, norm_mem_g, xq_w, xk_w, xv_w, xq_norm_g, xk_norm_g, xo_w,
                 norm_ffn_g, router_w, router_b, mlp1_w, mlp1_b, mlp2_w, mlp2_b):
    p = rms_norm(h, norm_mix_g) @ w_in
    o_nsa = nsa_mixer(p[..., :NSA_PROJ], q_norm_g, k_cmp_norm_g, k_slc_norm_g, k_win_norm_g,
                      cmp_pe_k, cmp_pe_v, cmp_k_w1, cmp_k_w2, cmp_v_w1, cmp_v_w2)
    o_rwkv = rwkv7_mixer(p[..., NSA_PROJ:], rwkv_mu, rwkv_w0, rwkv_w_up, rwkv_a0, rwkv_a_up, rwkv_g_up,
                         rwkv_k_k, rwkv_k_a, rwkv_r_k, rwkv_ln_w, rwkv_ln_b)
    h = h + jnp.concatenate([o_nsa, o_rwkv], axis=-1) @ w_out
    h = h + memory_cross_attention(rms_norm(h, norm_x_g), rms_norm(mem, norm_mem_g),
                                   xq_w, xk_w, xv_w, xq_norm_g, xk_norm_g, xo_w)
    h = h + moe_ffn(rms_norm(h, norm_ffn_g), router_w, router_b, mlp1_w, mlp1_b, mlp2_w, mlp2_b)
    return h

def setup_inputs(seed: int = 0) -> dict:
    key = jax.random.key(seed)
    ks = iter(jax.random.split(key, 64))
    f32 = jnp.float32

    def nrm(shape, scale):
        return scale * jax.random.normal(next(ks), (DEPTH,) + shape, f32)

    def gain(n):
        return 1.0 + 0.02 * jax.random.normal(next(ks), (DEPTH, n), f32)

    def unif(shape, lo, hi):
        return jax.random.uniform(next(ks), (DEPTH,) + shape, f32, lo, hi)

    Dh, L, G = HEAD_DIM, CMP_BLOCK, NSA_KV_GROUPS
    return {
        "x": jax.random.normal(next(ks), (BATCH, SEQ, D_MODEL), f32),
        "mem": jax.random.normal(next(ks), (BATCH, MEM_LEN, D_MODEL), f32),
        "norm_mix_g": gain(D_MODEL),
        "w_in": nrm((D_MODEL, P_TOTAL), D_MODEL ** -0.5),
        "q_norm_g": gain(Dh),
        "k_cmp_norm_g": gain(Dh),
        "k_slc_norm_g": gain(Dh),
        "k_win_norm_g": gain(Dh),
        "cmp_pe_k": nrm((L, Dh), 0.1),
        "cmp_pe_v": nrm((L, Dh), 0.1),
        "cmp_k_w1": nrm((L * Dh, Dh), (L * Dh) ** -0.5),
        "cmp_k_w2": nrm((Dh, Dh), Dh ** -0.5),
        "cmp_v_w1": nrm((L * Dh, Dh), (L * Dh) ** -0.5),
        "cmp_v_w2": nrm((Dh, Dh), Dh ** -0.5),
        "rwkv_mu": unif((RWKV_PROJ,), 0.0, 1.0),
        "rwkv_w0": unif((RWKV_DIM,), -6.0, -1.0),
        "rwkv_w_up": nrm((DECAY_LORA, RWKV_DIM), 0.1 * DECAY_LORA ** -0.5),
        "rwkv_a0": nrm((RWKV_DIM,), 0.1),
        "rwkv_a_up": nrm((ICLR_LORA, RWKV_DIM), 0.5 * ICLR_LORA ** -0.5),
        "rwkv_g_up": nrm((GATE_LORA, RWKV_DIM), GATE_LORA ** -0.5),
        "rwkv_k_k": 0.85 + nrm((RWKV_DIM,), 0.02),
        "rwkv_k_a": gain(RWKV_DIM),
        "rwkv_r_k": nrm((RWKV_HEADS, HEAD_DIM), 0.1),
        "rwkv_ln_w": gain(RWKV_DIM),
        "rwkv_ln_b": nrm((RWKV_DIM,), 0.02),
        "w_out": nrm((D_MIX, D_MODEL), D_MIX ** -0.5),
        "norm_x_g": gain(D_MODEL),
        "norm_mem_g": gain(D_MODEL),
        "xq_w": nrm((D_MODEL, D_MODEL), D_MODEL ** -0.5),
        "xk_w": nrm((D_MODEL, D_MODEL), D_MODEL ** -0.5),
        "xv_w": nrm((D_MODEL, D_MODEL), D_MODEL ** -0.5),
        "xq_norm_g": gain(X_HEAD_DIM),
        "xk_norm_g": gain(X_HEAD_DIM),
        "xo_w": nrm((D_MODEL, D_MODEL), D_MODEL ** -0.5),
        "norm_ffn_g": gain(D_MODEL),
        "router_w": nrm((D_MODEL, N_EXPERTS), D_MODEL ** -0.5),
        "router_b": nrm((N_EXPERTS,), 0.01),
        "mlp1_w": nrm((N_EXPERTS, D_MODEL, 2 * D_EXPERT), D_MODEL ** -0.5),
        "mlp1_b": nrm((N_EXPERTS, 2 * D_EXPERT), 0.02),
        "mlp2_w": nrm((N_EXPERTS, D_EXPERT, D_MODEL), D_EXPERT ** -0.5),
        "mlp2_b": nrm((N_EXPERTS, D_MODEL), 0.02),
    }

def reference(x, mem, norm_mix_g, w_in, q_norm_g, k_cmp_norm_g, k_slc_norm_g, k_win_norm_g,
              cmp_pe_k, cmp_pe_v, cmp_k_w1, cmp_k_w2, cmp_v_w1, cmp_v_w2,
              rwkv_mu, rwkv_w0, rwkv_w_up, rwkv_a0, rwkv_a_up, rwkv_g_up, rwkv_k_k, rwkv_k_a,
              rwkv_r_k, rwkv_ln_w, rwkv_ln_b, w_out,
              norm_x_g, norm_mem_g, xq_w, xk_w, xv_w, xq_norm_g, xk_norm_g, xo_w,
              norm_ffn_g, router_w, router_b, mlp1_w, mlp1_b, mlp2_w, mlp2_b):
    layer_params = (norm_mix_g, w_in, q_norm_g, k_cmp_norm_g, k_slc_norm_g, k_win_norm_g,
                    cmp_pe_k, cmp_pe_v, cmp_k_w1, cmp_k_w2, cmp_v_w1, cmp_v_w2,
                    rwkv_mu, rwkv_w0, rwkv_w_up, rwkv_a0, rwkv_a_up, rwkv_g_up, rwkv_k_k, rwkv_k_a,
                    rwkv_r_k, rwkv_ln_w, rwkv_ln_b, w_out,
                    norm_x_g, norm_mem_g, xq_w, xk_w, xv_w, xq_norm_g, xk_norm_g, xo_w,
                    norm_ffn_g, router_w, router_b, mlp1_w, mlp1_b, mlp2_w, mlp2_b)
    h = x
    for l in range(DEPTH):
        h = hybrid_layer(h, mem, *[prm[l] for prm in layer_params])
    return h


_drawn_inputs = setup_inputs


def setup_inputs(seed=0):
    import zlib

    import numpy as np

    out = dict(_drawn_inputs(seed))
    spreads = {}
    factors = {'q_norm_g': 8.0,
     'k_cmp_norm_g': 8.0,
     'k_slc_norm_g': 6.669,
     'k_win_norm_g': 4.642,
     'cmp_pe_k': 8.0,
     'rwkv_w_up': 4.516,
     'rwkv_k_a': 2.891,
     'rwkv_ln_w': 3.033,
     'norm_x_g': 4.262,
     'norm_mem_g': 4.241,
     'xq_norm_g': 3.064,
     'xk_norm_g': 5.304,
     'mlp1_b': 19.101,
     'mlp2_b': 21.788,
     'rwkv_ln_b': 2.9,
     'norm_ffn_g': 5.816,
     'router_b': 6.856}
    for name, (base, spread) in spreads.items():
        noise = np.random.default_rng([zlib.crc32(name.encode()), seed]).standard_normal(out[name].shape)
        drawn = base * np.exp(spread * noise) if base else spread * noise
        out[name] = __import__('jax').numpy.asarray(drawn.astype(out[name].dtype))
    for name, factor in factors.items():
        out[name] = (out[name] * factor).astype(out[name].dtype)
    return out
```

```python
from contextlib import ExitStack

import numpy as np

import concourse.bass as bass
from concourse import mybir

P = 128
F32 = mybir.dt.float32
I32 = mybir.dt.int32
ALU = mybir.AluOpType
ACT = mybir.ActivationFunctionType
AX = mybir.AxisListType.X

T = 256
TT = T // P
D = 1024
KD = D // P
MEM = 256
HD = 64
NSA_H, NSA_G = 8, 2
RW_H = 8
CMP, STRIDE = 32, 16
NCMP = T // STRIDE - CMP // STRIDE + 1
X_H, X_HD = 4, 256
NE, TOPK = 32, 4
DE = 1024
SLOTS = 64
EXTRA = (T * TOPK) // (SLOTS + 1)
ITEMS = NE + EXTRA
ICOLS = ITEMS + 1
CH = 64
EPS = 1e-6
GN_EPS = HD * 1e-5
NEG = -1e30
KAPPA = float(np.exp(-0.5))

C_Q, C_KC, C_VC, C_KS, C_VS, C_KW, C_VW, C_GL = 0, 512, 640, 768, 896, 1024, 1152, 1280
C_R, C_K, C_V, C_WD = 1304, 1816, 2328, 2840

JOBS = [("w_in", C_WD), ("w_in", C_K), ("w_in", C_K + 256), ("w_in", C_R), ("w_in", C_R + 256),
        ("w_in", C_V), ("w_in", C_V + 256),
        ("w_in", C_KC), ("w_in", C_KS), ("w_in", C_KW), ("q", 0), ("q", 1), ("gl", C_GL),
        ("cmp_k_w1", 0), ("cmp_v_w1", 0)] + \
    [("xk_w", 256 * j) for j in range(4)] + [("xv_w", 256 * j) for j in range(4)] + \
    [("w_out", 256 * j) for j in range(4)] + [("xq_w", 256 * j) for j in range(4)] + \
    [("xo_w", 256 * j) for j in range(4)]
WSLOTS = 3
J_LORA, J_K, J_R, J_V, J_KC, J_KS, J_KW, J_Q, J_GL, J_CK, J_CV, J_XK, J_XV, J_OUT, J_XQ, J_XO = \
    0, 1, 3, 5, 7, 8, 9, 10, 12, 13, 14, 15, 19, 23, 27, 31

VROWS = [("norm_mix_g", 8), ("norm_x_g", 8), ("norm_mem_g", 8), ("norm_ffn_g", 8), ("rwkv_mu", 14),
         ("rwkv_w0", 4), ("rwkv_a0", 4), ("rwkv_k_k", 4), ("rwkv_k_a", 4), ("rwkv_r_k", 4),
         ("rwkv_ln_w", 4), ("rwkv_ln_b", 4), ("xq_norm_g", 2), ("xk_norm_g", 2),
         ("q_norm_g", 1), ("k_slc_norm_g", 1), ("k_win_norm_g", 1), ("k_cmp_norm_g", 1)]
VCOL = {}
for _name, _rows in VROWS:
    VCOL[_name] = sum(r for n, r in VROWS[:len(VCOL)])
NV = sum(r for _, r in VROWS)


def view(buf, off, *dims):
    n = int(np.prod(dims))
    flat = buf[:, off:off + n]
    if len(dims) == 1:
        return flat
    names = "abcd"[:len(dims)]
    return flat.rearrange(f"p ({' '.join(names)}) -> p {' '.join(names)}",
                          **{c: d for c, d in zip(names[1:], dims[1:])})


def bcast(ap, *shape):
    return ap.to_broadcast(list(shape))


def build(nc, a, out):
    ctx = ExitStack()
    with ctx:
        sems = {}

        def sem(name):
            if name not in sems:
                sems[name] = ctx.enter_context(nc.semaphore(name))
            return sems[name]

        def sb(name, *dims, dt=F32, rows=P):
            return ctx.enter_context(nc.sbuf_tensor("sb_" + name, [rows, *dims], dt))

        ring = sb("ring", 24576)
        h = sb("h", TT, D)
        hnT = sb("hnT", KD, T)
        hn = sb("hn", 2048)
        wsl = sb("wsl", WSLOTS * 2048)
        kxT = sb("kxT", KD, T)
        vx = sb("vx", 2048)
        qx = sb("qx", 2048)
        ox = sb("ox", 2048)
        orT = sb("orT", 4, T)
        onT = sb("onT", 4, T)
        ident = sb("ident", P)
        blk = sb("blk", P)
        blk64 = sb("blk64", P)
        o256 = sb("o256", P)
        before = sb("before", P)
        ones = sb("ones", P)
        masks4 = sb("masks4", 4, P)
        masks3 = sb("masks3", 3, P)
        lowers = sb("lowers", 2, P)
        dist = sb("dist", 384)
        distc = sb("distc", TT, 16)
        maskc = sb("maskc", TT, 16)
        mreset = sb("mreset", T)
        vrows = sb("vrows", P)
        vecs = sb("vecs", P)
        omka = sb("omka", 4)
        eps_col = sb("eps_col", 2)
        perow = sb("perow", 2, P)
        peT = sb("peT", 2, CMP)
        cw2 = sb("cw2", 2, HD)
        rw = sb("rw", KD, NE)
        rb = sb("rb", NE)
        wend = sb("wend", 4, 4)
        kcmpT = sb("kcmpT", 16)
        vcmp = sb("vcmp", 2, HD)
        h1T = sb("h1T", 2, 16)
        csq = sb("csq", 16)
        crs = sb("crs", 16)
        gates = sb("gates", TT, 24)
        sc_c = sb("sc_c", TT, 8, 16)
        ptc = sb("ptc", 2, P)
        st = sb("st", 64)
        rank = sb("rank", TT, ICOLS)
        gate = sb("gate", TT, ICOLS)
        tabi = sb("tabi", 64, dt=I32)
        psum = ctx.enter_context(nc.psum_tensor("ps", [P, 8, 512], F32))

        GM = view(ring, 0, 8, 4, P)
        DT3 = view(ring, 4096, 8, 3, P)
        B1, B2, B3, B4, PP = (view(ring, 7168 + 1024 * i, 8, P) for i in range(5))
        QT = view(ring, 12288, 4, P)
        AKV, Z, U = (view(ring, 12800 + 512 * i, 512) for i in range(3))
        AR = view(ring, 14336, 4, 2, 2, P)
        bhT = view(ring, 16384, 4, T)
        khT = view(ring, 17408, 4, T)
        gT = view(ring, 18432, 4, T)
        bonus = view(ring, 19456, 4, T)
        vT = view(ring, 20480, 4, T)
        tok = view(ring, 21504, 4, 512)
        SH = view(ring, 23552, 4, 4, HD)
        (kT, rT, sig, cum, W, Wi, Wp, kkr, sqr, kk, aT, k2, tmp) = \
            (view(ring, 1024 * i, 4, T) for i in range(13))
        wdad = view(ring, 13312, T)
        gd = view(ring, 13568, T)
        Y, YC, SQ = view(ring, 10240, 512), view(ring, 10752, 512), view(ring, 9216, 512)
        shifted = view(kxT[:, :, :].rearrange("p a b -> p (a b)"), 0, 2, 2, 257)
        diff = view(vx, 0, 2, 2, T)
        lora = view(vx, 1024, 2, 512)
        qT = view(hn, 0, 4, T)
        ksT, kwT = view(hn, 1024, T), view(hn, 1280, T)
        vs, vw = view(hn, 1536, TT, P), view(hn, 1792, TT, P)
        kcT = view(onT[:, :, :].rearrange("p a b -> p (a b)"), 0, 2, T)
        nsq = view(onT[:, :, :].rearrange("p a b -> p (a b)"), 512, 2, T)
        orf = orT[:, :, :].rearrange("p a b -> p (a b)")
        XC = view(orf, 0, CMP, NCMP)
        nrs = view(orf, 512, 2, T)
        memx = view(qx, 0, TT, D)
        S2 = view(qx, 0, 2, 2, T)
        PT = view(qx, 1024, 2, 4, P)
        memT = view(ox, 0, KD, T)
        qxT = view(qx, 0, KD, T)
        oxT = view(ox, 0, KD, T)
        vxm = view(vx, 0, TT, D)

        xsq = sb("xsq", 2, T)
        xrs = sb("xrs", T)
        xs = view(hn, 0, 2, MEM)
        xpt = view(hn, 512, 2, 2, P)
        hf = hnT[:, :, :].rearrange("p a b -> p (a b)")
        xgT, actv, actT, yb = view(hf, 0, KD, SLOTS), view(hf, 512, 512), view(hf, 1024, 4, P), view(hf, 1536, 512)
        gl, ll, sg = (view(wsl, 512 * i, 2, 256) for i in range(3))
        selg, sel, selgT = view(wsl, 1536, TT, P), view(wsl, 1792, TT, SLOTS), view(wsl, 1920, TT, P)
        bias, zrow = view(wsl, 2176, 3 * DE), view(wsl, 5248, 512)
        kf = kxT[:, :, :].rearrange("p a b -> p (a b)")
        lw, le, key, pick = (view(kf, 64 * i, TT, NE) for i in range(4))
        chosen, place = view(kf, 256, TT, NE), view(kf, 320, TT, NE)
        gsm, first = view(kf, 384, TT, NE), view(kf, 448, TT)
        extra, upto, off = (view(kf, 512 + NE * i, NE) for i in range(3))
        top = view(kf, 640, TT)
        it1, it2, it3 = (view(vx, 512 * i, EXTRA, NE) for i in range(3))
        blk_of, exp_of, it4 = view(vx, 1536, EXTRA), view(vx, 1552, EXTRA), view(vx, 1568, EXTRA)
        tabf = view(vx, 1600, 64)
        iotas = sb("iotas", P)
        reve = sb("reve", NE)
        w1 = view(ring, 0, KD, 2 * DE)
        w2 = view(ring, 16384, KD, D)

        def vec(name, i=0, n=1):
            return vecs[:, VCOL[name] + i:VCOL[name] + i + n]

        def slot(j):
            return wsl[:, (j % WSLOTS) * 2048:(j % WSLOTS + 1) * 2048]

        def wjob(j, n=256):
            return slot(j)[:, 0:8 * n].rearrange("p (k n) -> p k n", k=8)

        INV = [("D2", "copy", "DT", "D", "B1"), ("D2T", "copy", "D", "DT", "B2"),
               ("D4", "copy", "B2", "B1", "B3"), ("D4T", "copy", "B1", "B2", "B4"),
               ("P2", "add", "B2", "PP", "PP"), ("D8T", "copy", "B3", "B4", "B1"),
               ("P4", "add", "B4", "PP", "PP"), ("P8", "add", "B1", "PP", "PP"),
               ("P8T", "turn", "PP", None, "B2"), ("T1", "copy", "E1T", "PP", "B3"),
               ("M1", "add", "B2", "B3", "PP"), ("M1T", "turn", "PP", None, "B2"),
               ("T2", "copy", "E2T", "PP", "B3"), ("M2", "add", "B2", "B3", "PP")]
        COPIES = [n for n, kind, *_ in INV if kind != "add"]
        ADDS = [n for n, kind, *_ in INV if kind == "add"]
        NEEDS = {"D2": ["G"], "D2T": ["G"], "D4": ["D2", "D2T"], "D4T": ["D2T"], "P2": ["P1", "D2T"],
                 "D8T": ["D4", "D4T"], "P4": ["P2", "D4T"], "P8": ["P4", "D8T"], "P8T": ["P8"],
                 "T1": ["P8"], "M1": ["P8T", "T1"], "M1T": ["M1"], "T2": ["M1"], "M2": ["M1T", "T2"]}
        PART = {"D": lambda i: GM[:, i, 0, :], "DT": lambda i: DT3[:, i, 0, :],
                "E1T": lambda i: DT3[:, i, 1, :], "E2T": lambda i: DT3[:, i, 2, :],
                "B1": lambda i: B1[:, i, :], "B2": lambda i: B2[:, i, :], "B3": lambda i: B3[:, i, :],
                "B4": lambda i: B4[:, i, :], "PP": lambda i: PP[:, i, :]}
        BUF = {"B1": B1, "B2": B2, "B3": B3, "B4": B4, "PP": PP}

        def inv_done(name, tt, g):
            if name == "G":
                return "p1_made", 2 * tt + g + 1
            if name == "P1":
                return "p1_made", 2 * tt + g + 1
            own, group = ("inv_added", ADDS) if name in ADDS else ("inv_copied", COPIES)
            return own, 2 * (len(group) * tt + group.index(name)) + g + 1

        core = []
        for tt in range(TT):
            core += [("tok", tt), ("parts", tt)]
            core += [("inv", tt, i) for i in range(len(INV))]
            core += [("qt", tt), ("akv", tt), ("z", tt)]
            core += [("chunk", c) for c in (2 * tt, 2 * tt + 1)]
            core += [("y", tt), ("ynorm", tt)]
        units = [(tt, hd) for tt in range(TT) for hd in range(NSA_H)]
        fill = [("xk", 0), ("cmpsc", 0)]
        for u in range(len(units) + 2):
            if u < len(units):
                fill.append(("score", u))
            if 1 <= u <= len(units):
                fill.append(("turnp", u - 1))
            if u >= 2:
                fill.append(("pv", u - 2))
            if u % 2 == 1 and u // 2 + 1 < 8:
                fill.append(("xk", u // 2 + 1) if u // 2 + 1 < 4 else ("xv", u // 2 - 3))
        order = []
        for i, step in enumerate(core):
            order.append(step)
            order += fill[i * len(fill) // len(core):(i + 1) * len(fill) // len(core)]
        SLOPE = [float(2.0 ** (-8.0 * (i + 1) / NSA_H)) for i in range(NSA_H)]

        tiles = {}
        block = ctx.enter_context(nc.Block())

        def ready(eng, *name):
            bank, number = tiles[name]
            eng.wait_ge(sem("tile_ready"), number + 1)
            return bank

        NORMS = ["x", "mem", "cross", "ffn"]

        @block.tensor
        def _(pe):
            owners = {}

            def tile(*name, freed, bank=None):
                n = sum(1 for b, _ in tiles.values() if b != 7)
                if bank is None:
                    bank = n % 7
                if bank in owners:
                    own, value = owners[bank]
                    pe.wait_ge(sem(own), value)
                owners[bank] = freed
                tiles[name] = (bank, n)
                return psum[:, bank, :]

            def loaded(j):
                transfers = sum({"q": 4, "cmp_k_w1": 2, "cmp_v_w1": 2}.get(JOBS[i][0], 1)
                                for i in range(j % WSLOTS, j + 1, WSLOTS))
                pe.wait_ge(sem(f"weights_in_{j % WSLOTS}"), 16 * transfers)

            def turn_norm(which, src, freed):
                for tt in range(TT):
                    pe.wait_ge(sem("rows_normed"), 2 * NORMS.index(which) + tt + 1)
                    for half in range(2):
                        t = tile("turn", which, tt, half, freed=(freed, 2 * tt + half + 1))
                        for k in range(4):
                            c = (4 * half + k) * P
                            mm = pe.transpose(t[:, k * P:(k + 1) * P], src[:, tt, c:c + P], ident[:, :])
                        mm.then_inc(sem("tile_ready"), 1)

            def project(t, w, act, cols=2):
                for g in range(cols):
                    for k in range(KD):
                        mm = pe.matmul(t[:, g * T:(g + 1) * T], w[:, k, g * P:(g + 1) * P], act[:, k, :],
                                       start=k == 0, stop=k == KD - 1)
                return mm

            pe.wait_ge(sem("consts"), 1)
            pe.wait_ge(sem("rows_in"), 16 * len(VROWS) + 16 * 8)
            t = tile("vecs", freed=("vecs", 1))
            pe.transpose(t[:, 0:NV], vrows[0:NV, :], ident[0:NV, 0:NV])
            for kind in range(2):
                mm = pe.transpose(t[:, P + CMP * kind:P + CMP * (kind + 1)], perow[0:CMP, kind, :],
                                  ident[0:CMP, 0:CMP])
            mm.then_inc(sem("tile_ready"), 1)
            hn3 = view(hn, 0, TT, D)
            turn_norm("x", hn3, "xT")
            turn_norm("mem", memx, "memT")

            def rwkv_job(j):
                loaded(j)
                t = tile("job", j, freed=("job_taken", j + 1))
                project(t, wjob(j), hnT).then_inc(sem("tile_ready"), 1)

            pe.wait_ge(sem("xT"), 4)
            for j in range(J_LORA, J_R + 2):
                rwkv_job(j)
            pe.wait_ge(sem("small_in"), 16 * 9)
            pe.wait_ge(sem("lora_in"), 2)
            pe.wait_ge(sem("mixed"), 1)
            for name, rows, w, act in (("zw", slice(0, 64), 0, wdad), ("az", slice(64, 128), 0, wdad),
                                       ("gg", slice(0, 128), 1, gd)):
                for i in range(2):
                    t = tile(name, i, freed=(name, i + 1))
                    for p in (2 * i, 2 * i + 1):
                        mm = pe.matmul(t[:, (p % 2) * T:(p % 2 + 1) * T], lora[rows, w, p * P:(p + 1) * P],
                                       act[rows, :], start=True, stop=True)
                    mm.then_inc(sem("tile_ready"), 1)
            rwkv_job(J_V)
            rwkv_job(J_V + 1)
            for i in range(2):
                pe.wait_ge(sem("key_squares"), i + 1)
                t = tile("kks", i, freed=("key_norms", i + 1))
                pe.matmul(t, blk[:, :], sqr[:, 2 * i:2 * i + 2, :], start=True, stop=True) \
                  .then_inc(sem("tile_ready"), 1)

            loaded(J_KC)
            t = tile("kc", freed=("kc_copied", 1))
            project(t, wjob(J_KC), hnT).then_inc(sem("tile_ready"), 1)
            for n, j in enumerate((J_KS, J_KW)):
                loaded(j)
                t = tile("kv", n, freed=("keys_normed", n + 1))
                w = wjob(j)
                project(t, w, hnT, cols=1)
                for tt in range(TT):
                    for k in range(KD):
                        mm = pe.matmul(t[:, T + tt * P:T + (tt + 1) * P], hnT[:, k, tt * P:(tt + 1) * P],
                                       w[:, k, P:2 * P], start=k == 0, stop=k == KD - 1)
                mm.then_inc(sem("tile_ready"), 1)
                pe.wait_ge(sem("nsa_squares"), n + 1)
                t = tile("kvn", n, freed=("nsa_rs", n + 1))
                pe.matmul(t[:, 0:T], blk64[:, :], nsq[:, 0, :], start=True, stop=True) \
                  .then_inc(sem("tile_ready"), 1)
            for n in range(2):
                loaded(J_Q + n)
                t = tile("q", n, freed=("queries_normed", n + 1))
                project(t, wjob(J_Q + n), hnT).then_inc(sem("tile_ready"), 1)
                pe.wait_ge(sem("nsa_squares"), n + 3)
                t = tile("qn", n, freed=("nsa_rs", n + 3))
                pe.matmul(t, blk64[:, :], nsq[:, :, :], start=True, stop=True).then_inc(sem("tile_ready"), 1)
            loaded(J_GL)
            t = tile("gl", freed=("gates", 1))
            w = wjob(J_GL, 24)
            for tt in range(TT):
                for k in range(KD):
                    mm = pe.matmul(t[:, tt * 24:(tt + 1) * 24], hnT[:, k, tt * P:(tt + 1) * P], w[:, k, :],
                                   start=k == 0, stop=k == KD - 1)
            mm.then_inc(sem("tile_ready"), 1)

            for kind in range(2):
                loaded(J_CK + kind)
                pe.wait_ge(sem("cmp_in"), kind + 1)
                t = tile("cmp", kind, freed=("cmp_hidden", kind + 1))
                w = slot(J_CK + kind)[:, 0:2048].rearrange("p (l e) -> p l e", l=CMP)
                for g in range(NSA_G):
                    r = slice(64 * g, 64 * g + 64)
                    for l in range(CMP):
                        mm = pe.matmul(t[r, 0:NCMP], w[r, l, :], XC[r, l, :], start=l == 0, stop=l == CMP - 1)
                mm.then_inc(sem("tile_ready"), 1)
            pe.wait_ge(sem("cmp_hidden"), 2)
            t = tile("kcmp", freed=("kcmp", 1))
            for g in range(NSA_G):
                r = slice(64 * g, 64 * g + 64)
                mm = pe.matmul(t[r, 0:NCMP], cw2[r, 0, :], h1T[r, 0, 0:NCMP], start=True, stop=True)
            mm.then_inc(sem("tile_ready"), 1)
            for g in range(NSA_G):
                t = tile("vcmp", g, freed=("vcmp", g + 1))
                r = slice(64 * g, 64 * g + 64)
                pe.matmul(t[0:NCMP, 0:HD], h1T[r, 1, 0:NCMP], cw2[r, 1, :], start=True, stop=True) \
                  .then_inc(sem("tile_ready"), 1)
            pe.wait_ge(sem("kcmp_squares"), 1)
            t = tile("kcn", freed=("kcmp_rs", 1))
            pe.matmul(t[:, 0:NCMP], blk64[:, :], csq[:, 0:NCMP], start=True, stop=True) \
              .then_inc(sem("tile_ready"), 1)
            for i in range(2):
                pe.wait_ge(sem("bonus_in"), i + 1)
                t = tile("bo", i, freed=("bonus", i + 1))
                pe.matmul(t, blk[:, :], tmp[:, 2 * i:2 * i + 2, :], start=True, stop=True) \
                  .then_inc(sem("tile_ready"), 1)

            def tok_step(tt):
                pe.wait_ge(sem("rwkv_ready"), 1)
                for kind in range(4):
                    t = tile("tok", tt, kind, freed=("tok", 4 * tt + kind + 1))
                    for p in range(4):
                        src = AR[:, p, tt, 0, :] if kind == 0 else \
                            (bhT, khT, vT)[kind - 1][:, p, tt * P:(tt + 1) * P]
                        mm = pe.transpose(t[:, p * P:(p + 1) * P], src, ident[:, :])
                    mm.then_inc(sem("tile_ready"), 1)

            def parts_step(tt):
                for g in range(2):
                    for i in range(4 * g, 4 * g + 4):
                        p, r = i // 2, slice(64 * (i % 2), 64 * (i % 2) + 64)
                        t = tile("gm", tt, i, freed=("gm_masked", 8 * tt + i + 1))
                        rhs = AR[r, p, tt, :, :]
                        pe.matmul(t[:, 0:T], bhT[r, p, tt * P:(tt + 1) * P], rhs, start=True, stop=True)
                        pe.matmul(t[:, T:2 * T], khT[r, p, tt * P:(tt + 1) * P], rhs, start=True, stop=True) \
                          .then_inc(sem("tile_ready"), 1)
                    for q in range(2):
                        t = tile("g3", tt, g, q, freed=("g3_masked", 4 * tt + 2 * g + q + 1))
                        r = slice(64 * q, 64 * q + 64)
                        for n, p in enumerate((2 * g, 2 * g + 1)):
                            mm = pe.matmul(t[:, n * P:(n + 1) * P], AR[r, p, tt, 0, :],
                                           bhT[r, p, tt * P:(tt + 1) * P], start=True, stop=True)
                        mm.then_inc(sem("tile_ready"), 1)

            def inv_step(tt, s):
                name, kind, lhs, rhs, _ = INV[s]
                for g in range(2):
                    own, value = inv_done(name, tt, g)
                    for need in NEEDS[name]:
                        own_need, at = inv_done(need, tt, g)
                        pe.wait_ge(sem(own_need), at)
                    t = tile("inv", tt, s, g, freed=(own, value))
                    for i in range(4 * g, 4 * g + 4):
                        o = t[:, (i % 4) * P:(i % 4 + 1) * P]
                        if kind == "turn":
                            mm = pe.transpose(o, PART[lhs](i), ident[:, :])
                        else:
                            mm = pe.matmul(o, PART[lhs](i), PART[rhs](i), start=True, stop=True)
                    mm.then_inc(sem("tile_ready"), 1)

            def qt_step(tt):
                own, value = inv_done("M2", tt, 1)
                pe.wait_ge(sem(own), value)
                pe.wait_ge(sem("tok"), 4 * tt + 4)
                t = tile("qt", tt, freed=("qt", tt + 1))
                for i in range(RW_H):
                    mm = pe.matmul(t[64 * (i % 2):64 * (i % 2) + 64, (i // 2) * P:(i // 2 + 1) * P],
                                   tok[:, 0, i * HD:(i + 1) * HD], PP[:, i, :], start=True, stop=True)
                mm.then_inc(sem("tile_ready"), 1)

            def akv_step(tt):
                t = tile("akv", tt, freed=("akv", tt + 1))
                for i in range(RW_H):
                    mm = pe.matmul(t[:, i * HD:(i + 1) * HD], GM[:, i, 2, :], tok[:, 3, i * HD:(i + 1) * HD],
                                   start=True, stop=True)
                mm.then_inc(sem("tile_ready"), 1)

            def z_step(tt):
                pe.wait_ge(sem("akv"), tt + 1)
                t = tile("z", tt, freed=("z", tt + 1))
                for i in range(RW_H):
                    mm = pe.matmul(t[:, i * HD:(i + 1) * HD], PP[:, i, :], AKV[:, i * HD:(i + 1) * HD],
                                   start=True, stop=True)
                mm.then_inc(sem("tile_ready"), 1)

            def chunk_step(c):
                tt, rows = c // 2, slice(64 * (c % 2), 64 * (c % 2) + 64)
                if c == 2:
                    pe.wait_ge(sem("qt"), 2)
                if c > 0:
                    pe.wait_ge(sem("state"), c)
                    for q in range(2):
                        t = tile("u", c, q, freed=("u", 2 * c + q + 1))
                        r = slice(64 * q, 64 * q + 64)
                        for p in range(4):
                            mm = pe.matmul(t[rows, p * HD:(p + 1) * HD], QT[r, p, rows], SH[r, c, p, :],
                                           start=True, stop=True)
                        mm.then_inc(sem("tile_ready"), 1)
                if c < 3:
                    pe.wait_ge(sem("u"), 2 * c + 2)
                    t = tile("ds", c, freed=("state", c + 1))
                    for i in range(RW_H):
                        r, cols = slice(64 * (i % 2), 64 * (i % 2) + 64), slice(i * HD, (i + 1) * HD)
                        o = t[r, (i // 2) * HD:(i // 2 + 1) * HD]
                        pe.matmul(o, tok[rows, 2, cols], tok[rows, 3, cols], start=True, stop=False)
                        mm = pe.matmul(o, tok[rows, 1, cols], U[rows, cols], start=False, stop=True)
                    mm.then_inc(sem("tile_ready"), 1)

            def y_step(tt):
                pe.wait_ge(sem("u"), 4 * tt + 4)
                t = tile("y", tt, freed=("y", tt + 1))
                for i in range(RW_H):
                    p, r, cols = i // 2, slice(64 * (i % 2), 64 * (i % 2) + 64), slice(i * HD, (i + 1) * HD)
                    o = t[r, p * P:(p + 1) * P]
                    pe.matmul(o, tok[:, 3, cols], GM[:, i, 3, :], start=True, stop=False)
                    mm = pe.matmul(o, U[:, cols], GM[:, i, 1, :], start=False, stop=False)
                    for c in (2 * tt, 2 * tt + 1):
                        if c > 0:
                            mm = pe.matmul(o[:, 64 * (c % 2):64 * (c % 2) + 64], SH[r, c, p, :],
                                           AR[r, p, tt, 1, 64 * (c % 2):64 * (c % 2) + 64],
                                           start=False, stop=c % 2 == 1)
                mm.then_inc(sem("tile_ready"), 1)

            def ynorm_step(tt):
                pe.wait_ge(sem("y"), tt + 1)
                t = tile("ymean", tt, freed=("y_centred", tt + 1))
                pe.matmul(t, blk64[:, :], Y, start=True, stop=True).then_inc(sem("tile_ready"), 1)
                pe.wait_ge(sem("y_squared"), tt + 1)
                t = tile("yvar", tt, freed=("y_rs", tt + 1))
                pe.matmul(t, blk64[:, :], SQ, start=True, stop=True).then_inc(sem("tile_ready"), 1)

            def xk_step(j):
                if j == 0:
                    pe.wait_ge(sem("memT"), 4)
                loaded(J_XK + j)
                t = tile("xk", j, freed=("kx_normed", j + 1))
                project(t, wjob(J_XK + j), memT).then_inc(sem("tile_ready"), 1)
                xnorm("xk", j, "kx_squares", "kx_rs")

            def xnorm(name, j, squares, freed):
                pe.wait_ge(sem(squares), j + 1)
                t = tile(name + "n", j, freed=(freed, j + 1))
                pe.matmul(t[:, 0:T], o256[:, :], xsq[:, 0, :], start=True, stop=False)
                pe.matmul(t[:, 0:T], o256[:, :], xsq[:, 1, :], start=False, stop=True) \
                  .then_inc(sem("tile_ready"), 1)

            def rows_job(t, j, lhs):
                w = wjob(j)
                for tt in range(TT):
                    for k in range(KD):
                        mm = pe.matmul(t[:, tt * T:(tt + 1) * T], lhs(k, tt), w[:, k, :],
                                       start=k == 0, stop=k == KD - 1)
                return mm

            def xv_step(j):
                loaded(J_XV + j)
                t = tile("xv", j, freed=("vx", j + 1))
                rows_job(t, J_XV + j, lambda k, tt: memT[:, k, tt * P:(tt + 1) * P]) \
                    .then_inc(sem("tile_ready"), 1)

            def cmpsc_step(_):
                pe.wait_ge(sem("queries_normed"), 2)
                pe.wait_ge(sem("kcmp"), 1)
                for tt in range(TT):
                    for g in range(NSA_G):
                        t = tile("cmpsc", tt, g, freed=("cmp_scores", 2 * tt + g + 1))
                        r = slice(64 * g, 64 * g + 64)
                        for i in range(4):
                            mm = pe.matmul(t[:, i * 16:i * 16 + NCMP], qT[r, i, tt * P:(tt + 1) * P],
                                           kcmpT[r, 0:NCMP], start=True, stop=True)
                        mm.then_inc(sem("tile_ready"), 1)

            def score_step(u):
                tt, i = units[u]
                r, nk = slice(64 * (i // 4), 64 * (i // 4) + 64), P * (tt + 1)
                if u == 0:
                    pe.wait_ge(sem("keys_normed"), 2)
                t = tile("score", u, freed=("scores", u + 1))
                for b, keys in enumerate((ksT, kwT)):
                    mm = pe.matmul(t[:, b * T:b * T + nk], qT[r, i % 4, tt * P:(tt + 1) * P], keys[r, 0:nk],
                                   start=True, stop=True)
                mm.then_inc(sem("tile_ready"), 1)

            def turnp_step(u):
                tt, i = units[u]
                if i == 0:
                    pe.wait_ge(sem("cmp_probs"), tt + 1)
                t = tile("pc", u, freed=("ptc", u + 1))
                pe.transpose(t[0:NCMP, 0:P], sc_c[:, tt, i, 0:NCMP], ident[:, :]).then_inc(sem("tile_ready"), 1)
                pe.wait_ge(sem("probs"), u + 1)
                t = tile("pt", u, freed=("pt", u + 1))
                for b in range(2):
                    for kt in range(tt + 1):
                        n = b * (tt + 1) + kt
                        mm = pe.transpose(t[:, n * P:(n + 1) * P], S2[:, u % 2, b, kt * P:(kt + 1) * P],
                                          ident[:, :])
                mm.then_inc(sem("tile_ready"), 1)

            def pv_step(u):
                tt, i = units[u]
                g = i // 4
                if u == 0:
                    pe.wait_ge(sem("vcmp"), 2)
                if i == 0:
                    out_tile[0] = tile("o", tt, freed=("on", tt + 1), bank=7)
                pe.wait_ge(sem("ptc"), u + 1)
                pe.wait_ge(sem("pt"), u + 1)
                o = out_tile[0][64 * (i % 2):64 * (i % 2) + 64, (i // 2) * P:(i // 2 + 1) * P]
                pe.matmul(o, vcmp[0:NCMP, g, :], ptc[0:NCMP, u % 2, :], start=True, stop=False)
                for b, values in enumerate((vs, vw)):
                    for kt in range(tt + 1):
                        mm = pe.matmul(o, values[:, kt, g * HD:(g + 1) * HD], PT[:, u % 2, b * (tt + 1) + kt, :],
                                       start=False, stop=b == 1 and kt == tt)
                mm.then_inc(sem("pv_done"), 1)

            out_tile = [None]
            steps = {"tok": tok_step, "parts": parts_step, "inv": inv_step, "qt": qt_step, "akv": akv_step,
                     "z": z_step, "chunk": chunk_step, "y": y_step, "ynorm": ynorm_step, "xk": xk_step,
                     "xv": xv_step, "cmpsc": cmpsc_step, "score": score_step, "turnp": turnp_step,
                     "pv": pv_step}
            for step, *args in order:
                steps[step](*args)

            pe.wait_ge(sem("on"), 2)
            pe.wait_ge(sem("rwkv_out"), 2)
            for j in range(4):
                loaded(J_OUT + j)
                t = tile("wout", j, freed=("h_mixed", j + 1))
                rows_job(t, J_OUT + j, lambda k, tt: (onT if k < 4 else orT)[:, k % 4, tt * P:(tt + 1) * P]) \
                    .then_inc(sem("tile_ready"), 1)
            turn_norm("cross", hn3, "hT")
            pe.wait_ge(sem("hT"), 4)
            for j in range(4):
                loaded(J_XQ + j)
                t = tile("xq", j, freed=("qx_normed", j + 1))
                project(t, wjob(J_XQ + j), hnT).then_inc(sem("tile_ready"), 1)
                xnorm("xq", j, "qx_squares", "qx_rs")

            def xscore(n):
                tt, i = n % 2, n // 2
                pe.wait_ge(sem("qx_normed"), i + 1)
                t = tile("xs", n, freed=("xscores", n + 1))
                for c in range(2):
                    mm = pe.matmul(t[:, 0:MEM], qxT[:, 2 * i + c, tt * P:(tt + 1) * P], kxT[:, 2 * i + c, :],
                                   start=c == 0, stop=c == 1)
                mm.then_inc(sem("tile_ready"), 1)

            def xturn(n):
                pe.wait_ge(sem("xprobs"), n + 1)
                t = tile("xp", n, freed=("xpt", n + 1))
                for m in range(2):
                    mm = pe.transpose(t[:, m * P:(m + 1) * P], xs[:, n % 2, m * P:(m + 1) * P], ident[:, :])
                mm.then_inc(sem("tile_ready"), 1)

            def xpv(n):
                tt, i = n % 2, n // 2
                pe.wait_ge(sem("xpt"), n + 1)
                t = tile("xo", n, freed=("ox", n + 1))
                for c in range(2):
                    for m in range(2):
                        mm = pe.matmul(t[:, c * P:(c + 1) * P], vxm[:, m, i * X_HD + c * P:i * X_HD + (c + 1) * P],
                                       xpt[:, n % 2, m, :], start=m == 0, stop=m == 1)
                mm.then_inc(sem("tile_ready"), 1)

            for n in range(2 * X_H + 2):
                if n < 2 * X_H:
                    xscore(n)
                if 1 <= n <= 2 * X_H:
                    xturn(n - 1)
                if n >= 2:
                    xpv(n - 2)
            pe.wait_ge(sem("ox"), 8)
            for j in range(4):
                loaded(J_XO + j)
                t = tile("xout", j, freed=("h_crossed", j + 1))
                rows_job(t, J_XO + j, lambda k, tt: oxT[:, k, tt * P:(tt + 1) * P]).then_inc(sem("tile_ready"), 1)
            turn_norm("ffn", hn3, "hfT")
            pe.wait_ge(sem("hfT"), 4)
            t = tile("logits", freed=("logits", 1))
            for tt in range(TT):
                o = t[:, tt * NE:(tt + 1) * NE]
                pe.matmul(o, ones[0:1, :], rb[0:1, :], start=True, stop=False)
                for k in range(KD):
                    mm = pe.matmul(o, hnT[:, k, tt * P:(tt + 1) * P], rw[:, k, :], start=False, stop=k == KD - 1)
            mm.then_inc(sem("tile_ready"), 1)
            pe.wait_ge(sem("chosen"), 1)
            t = tile("places", freed=("places", 1))
            pe.matmul(t[:, 0:NE], before[:, :], chosen[:, 0, :], start=True, stop=True)
            pe.matmul(t[:, NE:2 * NE], ones[:, :], chosen[:, 0, :], start=True, stop=False)
            pe.matmul(t[:, NE:2 * NE], before[:, :], chosen[:, 1, :], start=False, stop=True)
            pe.matmul(t[:, 2 * NE:3 * NE], ones[:, :], chosen[:, 0, :], start=True, stop=False)
            pe.matmul(t[:, 2 * NE:3 * NE], ones[:, :], chosen[:, 1, :], start=False, stop=True) \
              .then_inc(sem("tile_ready"), 1)

            def gather():
                for k in range(KD):
                    for tt in range(TT):
                        mm = pe.matmul(psum[:, 4, k * SLOTS:(k + 1) * SLOTS], hn3[:, tt, k * P:(k + 1) * P],
                                       sel[:, tt, :], start=tt == 0, stop=tt == 1)
                mm.then_inc(sem("gathered"), 1)

            pe.wait_ge(sem("tabled"), 1)
            pe.wait_ge(sem("zeroed"), 1)
            for b in range(4):
                mm = pe.matmul(psum[:, b, :], zrow[0:1, 0:P], zrow[0:1, :], start=True, stop=True)
            pe.wait_ge(sem("selected"), 1)
            gather()
            n_items = pe.value_load(tabi[0:1, 0:1], min_val=NE, max_val=ITEMS)
            with pe.Fori(0, n_items) as i:
                pe.wait_ge(sem("slots_in"), i + 1)
                pe.wait_ge(sem("bias_in"), (i + 1) * 32)
                pe.wait_ge(sem("swiglu"), i * 2 + 1)
                for n in range(2):
                    for half in range(2):
                        o = psum[64 * half:64 * half + 64, 4 + n, :]
                        c = half * DE + n * 512
                        mm = pe.matmul(o, ones[0:1, 0:SLOTS], bias[0:1, c:c + 512], start=True, stop=False)
                    for kq in range(2):
                        for half in range(2):
                            pe.wait_ge(sem(f"w1_in_{4 * n + 2 * kq + half}"), (i + 1) * 16)
                        for k in range(4 * kq, 4 * kq + 4):
                            for half in range(2):
                                o = psum[64 * half:64 * half + 64, 4 + n, :]
                                c = half * DE + n * 512
                                mm = pe.matmul(o, xgT[:, k, :], w1[:, k, c:c + 512],
                                               start=False, stop=k == KD - 1)
                                if k % 4 == 3:
                                    mm.then_inc(sem("piece_used"), 1)
                pe.wait_ge(sem("gated"), i + 1)
                pe.wait_ge(sem("y_out"), i + 1)
                for tt in range(TT):
                    mm = pe.transpose(psum[:, 7, tt * P:(tt + 1) * P], selg[:, tt, :], ident[:, :])
                mm.then_inc(sem("gated_turned"), 1)
                pe.wait_ge(sem("selected"), i + 2)
                pe.wait_ge(sem("swiglu"), i * 2 + 2)
                gather()
                for n in range(2):
                    pe.wait_ge(sem("swiglu"), i * 2 + 2 + n)
                    if n == 0:
                        pe.wait_ge(sem("act_out"), i * 2 + 1)
                    for m in (2 * n, 2 * n + 1):
                        mm = pe.transpose(psum[:, 6, m * P:(m + 1) * P], actv[:, m * P:(m + 1) * P], ident[:, :])
                    mm.then_inc(sem("act_turned"), 1)
                    if n == 0:
                        pe.wait_ge(sem("selgT"), i + 1)
                        for o2 in range(2):
                            pe.matmul(psum[64 * o2:64 * o2 + 64, 7, :], ones[0:1, 0:SLOTS],
                                      bias[0:1, 2 * DE + o2 * 512:2 * DE + (o2 + 1) * 512],
                                      start=True, stop=False)
                    pe.wait_ge(sem("act_out"), i * 2 + 2 + n)
                    for q in range(2):
                        pe.wait_ge(sem(f"w2_in_{2 * n + q}"), (i + 1) * 16)
                        for m in (2 * n, 2 * n + 1):
                            for o2 in range(2):
                                mm = pe.matmul(psum[64 * o2:64 * o2 + 64, 7, :],
                                               actT[:, m, 64 * q:64 * q + 64],
                                               w2[:, 4 * q + m, o2 * 512:(o2 + 1) * 512],
                                               start=False, stop=(n == 1 and q == 1 and m == 3))
                        mm.then_inc(sem("piece_used"), 1)
                pe.wait_ge(sem("y_out"), i + 2)
                for tt in range(TT):
                    for o2 in range(2):
                        r = slice(64 * o2, 64 * o2 + 64)
                        mm = pe.matmul(psum[:, 2 * tt + o2, :], selgT[r, tt, :], yb[r, :],
                                       start=False, stop=False, skip_group_check=True)
                mm.then_inc(sem("scattered"), 1)

        @block.vector
        def _(dve):
            counts = {}

            def link(ins, name="vector_step"):
                counts[name] = counts.get(name, 0) + 1
                ins.then_inc(sem(name), 1)
                dve.wait_ge(sem(name), counts[name])

            def stt(o, x, s, y, op0, op1):
                return dve.scalar_tensor_tensor(out=o, in0=x, scalar=s, in1=y, op0=op0, op1=op1)

            def norm_rows(which, src, dst):
                n = 2 * NORMS.index(which)
                for tt in range(TT):
                    dve.wait_ge(sem("row_rs"), n + tt + 1)
                    c = st[:, n + tt:n + tt + 1]
                    link(dve.tensor_scalar(dst[:, tt, :], src[:, tt, :], c, None, ALU.mult), "rows_normed")

            def turned(which, dst, gain, name):
                for tt in range(TT):
                    for half in range(2):
                        b = ready(dve, "turn", which, tt, half)
                        g = vec(gain, 4 * half, 4).unsqueeze(2)
                        link(dve.tensor_tensor(dst[:, 4 * half:4 * half + 4, tt * P:(tt + 1) * P],
                                               view(psum[:, b, :], 0, 4, P), bcast(g, P, 4, P), ALU.mult), name)

            hn3 = view(hn, 0, TT, D)
            dve.wait_ge(sem("consts"), 1)
            norm_rows("x", h, hn3)
            b = ready(dve, "vecs")
            link(dve.tensor_copy(vecs[:, 0:NV], psum[:, b, 0:NV]))
            link(dve.tensor_copy(peT[:, :, :], view(psum[:, b, P:P + 64], 0, 2, CMP)), "vecs")
            link(dve.tensor_scalar(omka[:, :], vec("rwkv_k_a", 0, 4), -1.0, 1.0, ALU.mult, ALU.add))
            turned("x", hnT, "norm_mix_g", "xT")
            norm_rows("mem", memx, memx)
            turned("mem", memT, "norm_mem_g", "memT")
            link(dve.memset(shifted[:, :, :, 0:1], 0.0), "shift_zeroed")

            MIXED = {J_LORA: (12, lambda g: (wdad, gd)[g])}
            for jj in range(2):
                MIXED[J_K + jj] = (4 + 2 * jj, lambda g, jj=jj: kT[:, 2 * jj + g, :])
                MIXED[J_R + jj] = (2 * jj, lambda g, jj=jj: rT[:, 2 * jj + g, :])
                MIXED[J_V + jj] = (8 + 2 * jj, lambda g, jj=jj: vT[:, 2 * jj + g, :])

            def mix(j):
                at, dst = MIXED[j]
                dve.wait_ge(sem("differenced"), j + 1)
                stt(dst(0), diff[:, j % 2, 0, :], vec("rwkv_mu", at), shifted[:, j % 2, 0, 1:T + 1],
                    ALU.mult, ALU.add)
                link(stt(dst(1), diff[:, j % 2, 1, :], vec("rwkv_mu", at + 1), shifted[:, j % 2, 1, 1:T + 1],
                         ALU.mult, ALU.add), "mixed")

            mix(J_LORA)
            mix(J_K)
            mix(J_K + 1)
            for i in range(2):
                for p in (2 * i, 2 * i + 1):
                    link(dve.tensor_scalar(kkr[:, p, :], kT[:, p, :], vec("rwkv_k_k", p), None, ALU.mult),
                         "kkr" if p % 2 else "vector_step")
            mix(J_R)
            mix(J_R + 1)
            dve.wait_ge(sem("zw"), 2)
            for p in range(4):
                link(dve.tensor_tensor_scan(cum[:, p, :], mreset[:, :], sig[:, p, :], 0.0, ALU.mult, ALU.add))
            link(dve.tensor_tensor(tmp[:, :, :], cum[:, :, :], sig[:, :, :], ALU.subtract), "cum")
            dve.wait_ge(sem("az"), 2)
            for p in range(4):
                link(dve.tensor_scalar(k2[:, p, :], aT[:, p, :], vec("rwkv_k_a", p), omka[:, p:p + 1],
                                       ALU.mult, ALU.add))
            link(dve.tensor_tensor(k2[:, :, :], k2[:, :, :], kT[:, :, :], ALU.mult))
            mix(J_V)
            mix(J_V + 1)
            dve.wait_ge(sem("decays"), 3)
            for i in range(2):
                for p in (2 * i, 2 * i + 1):
                    link(stt(tmp[:, p, :], rT[:, p, :], vec("rwkv_r_k", p), k2[:, p, :], ALU.mult, ALU.mult),
                         "bonus_in" if p % 2 else "vector_step")
            for i in range(2):
                b = ready(dve, "kks", i)
                link(dve.tensor_scalar(kk[:, 2 * i:2 * i + 2, :], view(psum[:, b, :], 0, 2, T), 1e-24, None,
                                       ALU.max), "key_norms")
            dve.wait_ge(sem("key_roots"), 2)
            link(dve.reciprocal(kk[:, :, :], kk[:, :, :]))
            link(dve.tensor_tensor(kk[:, :, :], kk[:, :, :], kkr[:, :, :], ALU.mult))

            def halves(x):
                return x.rearrange("p a (b c) -> p a b c", b=2)

            link(stt(AR[:, :, :, 0, :], halves(kk), -1.0, halves(Wp), ALU.mult, ALU.mult))
            link(dve.tensor_tensor(AR[:, :, :, 1, :], halves(rT), halves(W), ALU.mult))
            link(dve.tensor_tensor(bhT[:, :, :], kk[:, :, :], aT[:, :, :], ALU.mult))
            link(dve.tensor_tensor(bhT[:, :, :], bhT[:, :, :], Wi[:, :, :], ALU.mult))
            link(dve.tensor_copy(wend[:, :, :], W.rearrange("p a (c t) -> p a c t", c=4)[:, :, :, CH - 1]))
            link(dve.tensor_tensor(khT[:, :, :], k2[:, :, :], Wi[:, :, :], ALU.mult), "rwkv_ready")

            for n in range(2):
                dve.wait_ge(sem("nsa_rs"), n + 1)
                b = tiles["kv", n][0]
                link(stt((ksT, kwT)[n], psum[:, b, 0:T], vec(("k_slc_norm_g", "k_win_norm_g")[n]), nrs[:, 0, :],
                         ALU.mult, ALU.mult), "keys_normed")
            for n in range(2):
                dve.wait_ge(sem("nsa_rs"), n + 3)
                b = tiles["q", n][0]
                for j in range(2):
                    link(stt(qT[:, 2 * n + j, :], psum[:, b, j * T:(j + 1) * T], vec("q_norm_g"), nrs[:, j, :],
                             ALU.mult, ALU.mult), "queries_normed" if j else "vector_step")
            dve.wait_ge(sem("kc_copied"), 1)
            for kind in range(2):
                if kind:
                    ready(dve, "cmp", 0)
                kc = kcT[:, kind, :].rearrange("p (c l) -> p c l", l=STRIDE)
                for l1 in range(2):
                    pos = peT[:, kind, STRIDE * l1:STRIDE * (l1 + 1)].unsqueeze(2)
                    link(dve.tensor_tensor(XC[:, STRIDE * l1:STRIDE * (l1 + 1), :],
                                           kc[:, l1:l1 + NCMP, :].rearrange("p c l -> p l c"),
                                           bcast(pos, P, STRIDE, NCMP), ALU.add), "cmp_in" if l1 else "vector_step")
                if kind:
                    for kd in range(2):
                        b = ready(dve, "cmp", kd)
                        dve.wait_ge(sem("cmp_sig"), kd + 1)
                        link(dve.tensor_tensor(h1T[:, kd, 0:NCMP], psum[:, b, 0:NCMP], csq[:, 0:NCMP], ALU.mult),
                             "cmp_hidden")
            dve.wait_ge(sem("kcmp_rs"), 1)
            b = tiles["kcmp",][0]
            link(stt(kcmpT[:, 0:NCMP], psum[:, b, 0:NCMP], vec("k_cmp_norm_g"), crs[:, 0:NCMP],
                     ALU.mult, ALU.mult), "kcmp")
            for i in range(2):
                b = ready(dve, "bo", i)
                link(dve.tensor_tensor(bonus[:, 2 * i:2 * i + 2, :], view(psum[:, b, :], 0, 2, T),
                                       vT[:, 2 * i:2 * i + 2, :], ALU.mult), "bonus")

            def parts_step(tt):
                if tt:
                    ready(dve, "y", 0)
                for g in range(2):
                    for i in range(4 * g, 4 * g + 4):
                        b = ready(dve, "gm", tt, i)
                        dve.tensor_tensor(GM[:, i, :, :], view(psum[:, b, :], 0, 4, P), masks4[:, :, :],
                                          ALU.mult).then_inc(sem("gm_masked"), 1)
                    for q in range(2):
                        b = ready(dve, "g3", tt, g, q)
                        for n in range(2):
                            part = psum[:, b, n * P:(n + 1) * P].unsqueeze(1)
                            link(dve.tensor_tensor(DT3[:, 4 * g + 2 * n + q, :, :], bcast(part, P, 3, P),
                                                   masks3[:, :, :], ALU.mult), "g3_masked" if n else "vector_step")
                    link(dve.tensor_tensor(PP[:, 4 * g:4 * g + 4, :], GM[:, 4 * g:4 * g + 4, 0, :],
                                           bcast(ident[:, :].unsqueeze(1), P, 4, P), ALU.add), "p1_made")

            def inv_step(tt, s):
                if INV[s][1] != "add":
                    return
                for g in range(2):
                    b = ready(dve, "inv", tt, s, g)
                    link(dve.tensor_tensor(PP[:, 4 * g:4 * g + 4, :], view(psum[:, b, :], 0, 4, P),
                                           PP[:, 4 * g:4 * g + 4, :], ALU.add), "inv_added")

            def akv_step(tt):
                b = ready(dve, "akv", tt)
                link(dve.tensor_copy(AKV, psum[:, b, :]), "akv")

            def chunk_step(c):
                tt, rows = c // 2, slice(64 * (c % 2), 64 * (c % 2) + 64)
                dve.wait_ge(sem("z"), tt + 1)
                if c == 0:
                    for q in range(2):
                        link(dve.tensor_copy(U[rows, 256 * q:256 * q + 256], Z[rows, 256 * q:256 * q + 256]), "u")
                else:
                    u4, z4 = (x.rearrange("p (a q v) -> p q a v", q=2, v=HD) for x in (U, Z))
                    for q in range(2):
                        b = ready(dve, "u", c, q)
                        link(dve.tensor_tensor(u4[rows, q], view(psum[rows, b, :], 0, 4, HD), z4[rows, q],
                                               ALU.add), "u")
                if c < 3:
                    b = ready(dve, "ds", c)
                    grown = psum[:, b, 0:256]
                    if c > 0:
                        link(dve.tensor_tensor(AKV[:, 0:256], grown, SH[:, c, :, :].rearrange("p a b -> p (a b)"),
                                               ALU.add))
                        grown = AKV[:, 0:256]
                    link(dve.tensor_tensor(SH[:, c + 1, :, :], view(grown, 0, 4, HD),
                                           bcast(wend[:, :, c:c + 1], P, 4, HD), ALU.mult), "state")

            def ynorm_step(tt):
                b = ready(dve, "ymean", tt)
                dve.wait_ge(sem("y"), tt + 1)
                link(dve.tensor_tensor(YC, Y, psum[:, b, :], ALU.subtract), "y_centred")
                dve.wait_ge(sem("y_rs"), tt + 1)
                link(dve.tensor_tensor(YC, YC, Y, ALU.mult))
                for p in range(4):
                    c = slice(p * P, (p + 1) * P)
                    link(dve.tensor_scalar(YC[:, c], YC[:, c], vec("rwkv_ln_w", p), vec("rwkv_ln_b", p),
                                           ALU.mult, ALU.add))
                yc = view(YC, 0, 4, P)
                now = slice(tt * P, (tt + 1) * P)
                link(dve.tensor_tensor(yc, yc, bonus[:, :, now], ALU.add))
                link(dve.tensor_tensor(orT[:, :, now], yc, gT[:, :, now], ALU.mult), "rwkv_out")

            def xk_step(j):
                xnormed("xk", j, "kx_squares", "kx_rs", kxT, "xk_norm_g", "kx_normed")

            def xnormed(name, j, squares, rs, dst, gain, done):
                dve.wait_ge(sem(rs), j + 1)
                b = tiles[name, j][0]
                for c in range(2):
                    link(stt(dst[:, 2 * j + c, :], psum[:, b, c * T:(c + 1) * T], vec(gain, c), xrs[:, :],
                             ALU.mult, ALU.mult), done if c else "vector_step")

            def cmpsc_step(_):
                dve.wait_ge(sem("cmp_bias"), 1)
                dve.wait_ge(sem("gates"), 1)
                for tt in range(TT):
                    s = sc_c[:, tt, :, 0:NCMP]
                    for g in range(NSA_G):
                        b = ready(dve, "cmpsc", tt, g)
                        part = sc_c[:, tt, 4 * g:4 * g + 4, 0:NCMP]
                        link(dve.tensor_tensor(part, view(psum[:, b, :], 0, 4, 16)[:, :, 0:NCMP], part, ALU.add),
                             "cmp_scores")
                    link(dve.reduce_max(st[:, 8:16], s, AX))
                    link(dve.tensor_tensor(s, s, bcast(st[:, 8:16].unsqueeze(2), P, 8, NCMP), ALU.subtract),
                         "cmp_shifted")
                    dve.wait_ge(sem("cmp_exp"), tt + 1)
                    link(dve.reduce_sum(st[:, 16:24], s, AX))
                    link(dve.reciprocal(st[:, 16:24], st[:, 16:24]))
                    link(dve.tensor_tensor(st[:, 16:24], gates[:, tt, 0:24:3], st[:, 16:24], ALU.mult))
                    link(dve.tensor_tensor(s, s, bcast(maskc[:, tt, 0:NCMP].unsqueeze(1), P, 8, NCMP), ALU.mult))
                    link(dve.tensor_tensor(s, s, bcast(st[:, 16:24].unsqueeze(2), P, 8, NCMP), ALU.mult),
                         "cmp_probs")

            def score_step(u):
                tt, i = units[u]
                nk = P * (tt + 1)
                b = ready(dve, "score", u)
                if u >= 2:
                    ready(dve, "pt", u - 2)
                d = dist[:, T - nk:T].unsqueeze(1)
                link(stt(S2[:, u % 2, :, 0:nk], bcast(d, P, 2, nk), 8.0 * SLOPE[i],
                         view(psum[:, b, :], 0, 2, T)[:, :, 0:nk], ALU.mult, ALU.add), "scores")
                m = st[:, 24 + 2 * (u % 2):26 + 2 * (u % 2)]
                link(dve.reduce_max(m, S2[:, u % 2, :, 0:nk], AX))
                link(dve.tensor_scalar(st[:, 28 + 2 * (u % 2):30 + 2 * (u % 2)], m, -0.125, None, ALU.mult),
                     "score_max")

            def turnp_step(u):
                tt, i = units[u]
                dve.wait_ge(sem("exped"), u + 1)
                if u >= 2:
                    dve.wait_ge(sem("probs"), u - 1)
                c = st[:, 36 + 2 * (u % 2):38 + 2 * (u % 2)]
                link(dve.reciprocal(c, st[:, 32 + 2 * (u % 2):34 + 2 * (u % 2)]))
                link(dve.tensor_tensor(c, gates[:, tt, 3 * i + 1:3 * i + 3], c, ALU.mult), "coef")

            steps = {"parts": parts_step, "inv": inv_step, "akv": akv_step, "chunk": chunk_step,
                     "ynorm": ynorm_step, "xk": xk_step, "cmpsc": cmpsc_step, "score": score_step,
                     "turnp": turnp_step}
            for step, *args in order:
                if step in steps:
                    steps[step](*args)

            def residual(name, done):
                for j in range(4):
                    b = ready(dve, name, j)
                    cols = h[:, :, j * T:(j + 1) * T]
                    link(dve.tensor_tensor(cols, view(psum[:, b, :], 0, 2, T), cols, ALU.add), done)

            residual("wout", "h_mixed")
            norm_rows("cross", h, hn3)
            turned("cross", hnT, "norm_x_g", "hT")
            for j in range(4):
                xnormed("xq", j, "qx_squares", "qx_rs", qxT, "xq_norm_g", "qx_normed")
            for n in range(2 * X_H + 1):
                if n < 2 * X_H:
                    b = ready(dve, "xs", n)
                    link(dve.reduce_max(st[:, 40 + n % 2:41 + n % 2], psum[:, b, 0:MEM], AX))
                    link(dve.tensor_scalar(st[:, 42 + n % 2:43 + n % 2], st[:, 40 + n % 2:41 + n % 2],
                                           -float(X_HD) ** -0.5, None, ALU.mult), "xmax")
                if n >= 1:
                    q = (n - 1) % 2
                    dve.wait_ge(sem("xscores"), n)
                    link(dve.reciprocal(st[:, 46 + q:47 + q], st[:, 44 + q:45 + q]))
                    link(dve.tensor_scalar(xs[:, q, :], xs[:, q, :], st[:, 46 + q:47 + q], None, ALU.mult), "xprobs")
            residual("xout", "h_crossed")
            norm_rows("ffn", h, hn3)
            turned("ffn", hnT, "norm_ffn_g", "hfT")

            def wide(x):
                return bcast(x.unsqueeze(2), P, TT, NE)

            b = ready(dve, "logits")
            link(dve.tensor_copy(lw, view(psum[:, b, 0:2 * NE], 0, TT, NE)), "logits")
            link(dve.tensor_copy(le, lw))
            link(dve.memset(chosen, 0.0))
            for n in range(TOPK):
                link(dve.reduce_max(top, lw, AX))
                if n == 0:
                    link(dve.tensor_copy(first, top))
                link(dve.tensor_tensor(key, lw, wide(top), ALU.is_equal))
                link(dve.tensor_tensor(key, key, bcast(reve[:, :].unsqueeze(1), P, TT, NE), ALU.mult))
                link(dve.reduce_max(top, key, AX))
                link(dve.tensor_tensor(pick, key, wide(top), ALU.is_equal))
                link(dve.tensor_tensor(chosen, chosen, pick, ALU.add), "chosen" if n == TOPK - 1 else "vector_step")
                if n < TOPK - 1:
                    link(stt(lw, pick, -3e38, lw, ALU.mult, ALU.add))
            link(dve.tensor_tensor(le, le, wide(first), ALU.subtract), "logits_shifted")
            dve.wait_ge(sem("logits_exp"), 1)
            link(dve.tensor_tensor(gsm, le, chosen, ALU.mult))
            link(dve.reduce_sum(top, gsm, AX))
            link(dve.reciprocal(top, top))
            link(dve.memset(rank[:, :, :], -1.0))
            link(dve.memset(gate[:, :, :], 0.0))
            link(dve.tensor_tensor(gate[:, :, 0:NE], gsm, wide(top), ALU.mult))
            b = ready(dve, "places")
            pl = psum[:, b, 0:3 * NE]
            link(dve.tensor_scalar(place, view(pl, 0, TT, NE), 1.0, None, ALU.add))
            link(dve.tensor_tensor(place, place, chosen, ALU.mult))
            link(dve.tensor_scalar(rank[:, :, 0:NE], place, -1.0, None, ALU.add))
            count = pl[:, 2 * NE:3 * NE]
            link(dve.tensor_scalar(extra, count, float(SLOTS), None, ALU.is_gt))
            for m in range(2, T // SLOTS):
                link(stt(extra, count, float(SLOTS * m), extra, ALU.is_gt, ALU.add))
            link(dve.tensor_tensor_scan(upto, ones[:, 0:NE], extra, 0.0, ALU.mult, ALU.add), "places")
            link(dve.tensor_tensor(off, upto, extra, ALU.subtract))
            dve.wait_ge(sem("item_iota"), 1)

            def items(x):
                return bcast(x.unsqueeze(1), P, EXTRA, NE)

            link(dve.tensor_tensor(it2, items(off), it1, ALU.is_le))
            link(dve.tensor_tensor(it3, items(upto), it1, ALU.is_gt))
            link(dve.tensor_tensor(it2, it2, it3, ALU.mult))
            link(dve.tensor_tensor(it3, it2, items(off), ALU.mult))
            link(dve.reduce_sum(blk_of, it3, AX))
            link(dve.tensor_tensor(blk_of, it1[:, :, 0], blk_of, ALU.subtract))
            link(dve.tensor_scalar(blk_of, blk_of, float(SLOTS), float(SLOTS), ALU.mult, ALU.add))
            link(dve.tensor_tensor(it3, it2, items(reve[:, :]), ALU.mult))
            link(dve.reduce_sum(exp_of, it3, AX))
            link(dve.tensor_scalar(exp_of, exp_of, -1.0, 64.0, ALU.mult, ALU.add))
            for tt in range(TT):
                link(dve.tensor_tensor(it3, it2, items(rank[:, tt, 0:NE]), ALU.mult))
                link(dve.reduce_sum(it4, it3, AX))
                link(dve.tensor_tensor(rank[:, tt, NE:ITEMS], it4, blk_of, ALU.subtract))
                link(dve.tensor_tensor(it3, it2, items(gate[:, tt, 0:NE]), ALU.mult))
                link(dve.reduce_sum(gate[:, tt, NE:ITEMS], it3, AX))
            link(dve.tensor_scalar(tabf[:, 0:1], upto[:, NE - 1:NE], float(NE), None, ALU.add))
            link(dve.tensor_scalar(tabf[:, 1:1 + NE], reve[:, :], -1.0, 64.0, ALU.mult, ALU.add))
            link(dve.tensor_scalar(tabf[:, 1 + NE:1 + ITEMS], exp_of, float(NE - 1), None, ALU.min))
            link(dve.memset(tabf[:, 1 + ITEMS:64], 0.0))
            link(dve.tensor_copy(tabi[:, :], tabf), "tabled")
            link(dve.memset(zrow, 0.0), "zeroed")

            def choose(i):
                for tt in range(TT):
                    ins = dve.tensor_scalar(sel[:, tt, :], iotas[:, 0:SLOTS], rank[:, tt, bass.ds(i, 1)], None,
                                            ALU.is_equal)
                ins.then_inc(sem("selected"), 1)

            def fill_slots():
                g = vec("norm_ffn_g", 0, KD).unsqueeze(2)
                dve.tensor_tensor(xgT, view(psum[:, 4, :], 0, KD, SLOTS), bcast(g, P, KD, SLOTS), ALU.mult) \
                   .then_inc(sem("slots_in"), 1)

            for tt in range(TT):
                ins = dve.tensor_scalar(sel[:, tt, :], iotas[:, 0:SLOTS], rank[:, tt, 0:1], None, ALU.is_equal)
            ins.then_inc(sem("selected"), 1)
            dve.sem_inc(sem("swiglu"), 1)
            dve.sem_inc(sem("gated_turned"), 1)
            dve.wait_ge(sem("gathered"), 1)
            fill_slots()
            n_items = dve.value_load(tabi[0:1, 0:1], min_val=NE, max_val=ITEMS)
            with dve.Fori(0, n_items) as i:
                dve.wait_ge(sem("gated_turned"), i + 1)
                for tt in range(TT):
                    ins = dve.tensor_scalar(selg[:, tt, :], iotas[:, :], rank[:, tt, bass.ds(i, 1)],
                                            gate[:, tt, bass.ds(i, 1)], ALU.is_equal, ALU.mult)
                ins.then_inc(sem("gated"), 1)
                dve.wait_ge(sem("gathered"), i + 1)
                choose(i + 1)
                for n in range(2):
                    dve.wait_ge(sem("piece_used"), i * 12 + 4 + 4 * n)
                    if n == 1:
                        dve.wait_ge(sem("gated_turned"), i + 2)
                        dve.tensor_copy(selgT, view(psum[:, 7, 0:256], 0, TT, P)).then_inc(sem("selgT"), 1)
                    hid = view(psum[:, 4 + n, :], 0, 256, 2)
                    dve.tensor_scalar(gl[:, n, :], hid[:, :, 0], 7.0, None, ALU.min).then_inc(sem("glu"), 1)
                    dve.tensor_scalar(ll[:, n, :], hid[:, :, 1], 7.0, -7.0, ALU.min, ALU.max) \
                       .then_inc(sem("lin"), 1)
                    dve.wait_ge(sem("lin"), i * 2 + n + 1)
                    stt(ll[:, n, :], ll[:, n, :], 1.0, gl[:, n, :], ALU.add, ALU.mult).then_inc(sem("glin"), 1)
                    dve.wait_ge(sem("glin"), i * 2 + n + 1)
                    dve.wait_ge(sem("sig"), i * 2 + n + 1)
                    dve.tensor_tensor(actv[:, n * 256:(n + 1) * 256], ll[:, n, :], sg[:, n, :], ALU.mult) \
                       .then_inc(sem("swiglu"), 1)
                dve.wait_ge(sem("gathered"), i + 2)
                fill_slots()
            dve.wait_ge(sem("scattered"), n_items)
            for tt in range(TT):
                for o2 in range(2):
                    cols = h[:, tt, o2 * 512:(o2 + 1) * 512]
                    link(dve.tensor_tensor(cols, psum[:, 2 * tt + o2, :], cols, ALU.add), "out_ready")

        @block.scalar
        def _(act):
            counts = {}

            def link(ins, name="scalar_step"):
                counts[name] = counts.get(name, 0) + 1
                ins.then_inc(sem(name), 1)
                act.wait_ge(sem(name), counts[name])

            def f(o, x, func, **kw):
                return act.activation(o, x, func, **kw)

            hn3 = view(hn, 0, TT, D)
            junk = kxT[:, :, :].rearrange("p a b -> p (a b)")

            def inv_root(dst, src, name, scale=1.0, eps=EPS):
                link(f(dst, src, ACT.Ln, scale=scale, bias=eps_col[:, 0:1] if eps == EPS else eps_col[:, 1:2]))
                link(f(dst, dst, ACT.Exp, scale=-0.5), name)

            def squares(which, src, dst):
                n = 2 * NORMS.index(which)
                for tt in range(TT):
                    c = st[:, n + tt:n + tt + 1]
                    link(f(dst[:, tt, :], src[:, tt, :], ACT.Square, accum_out=c))
                    inv_root(c, c, "row_rs", scale=1.0 / D)

            act.wait_ge(sem("consts"), 1)
            act.wait_ge(sem("x_in"), 16)
            squares("x", h, hn3)
            act.wait_ge(sem("mem_in"), 16)
            squares("mem", memx, view(junk, 0, TT, D))
            act.wait_ge(sem("shift_zeroed"), 1)

            def take(j):
                if j >= 2:
                    act.wait_ge(sem("mixed"), j - 1)
                b = ready(act, "job", j)
                link(f(shifted[:, j % 2, :, 1:T + 1], view(psum[:, b, :], 0, 2, T), ACT.Copy), "job_taken")

            take(J_LORA)
            act.wait_ge(sem("mixed"), 1)
            link(f(wdad[0:64, :], wdad[0:64, :], ACT.Tanh), "lora_in")
            link(f(gd, gd, ACT.Sigmoid), "lora_in")
            take(J_K)
            take(J_K + 1)
            take(J_R)
            take(J_R + 1)
            for name, dst in (("zw", sig), ("az", aT), ("gg", gT)):
                for i in range(2):
                    b = ready(act, name, i)
                    for p in (2 * i, 2 * i + 1):
                        src = psum[:, b, (p % 2) * T:(p % 2 + 1) * T]
                        if name == "gg":
                            ins = f(dst[:, p, :], src, ACT.Copy)
                        else:
                            ins = f(dst[:, p, :], src, ACT.Sigmoid,
                                    bias=vec("rwkv_w0" if name == "zw" else "rwkv_a0", p))
                        link(ins, name if p % 2 else "scalar_step")
            take(J_V)
            take(J_V + 1)
            for i in range(2):
                act.wait_ge(sem("kkr"), i + 1)
                link(f(sqr[:, 2 * i:2 * i + 2, :], kkr[:, 2 * i:2 * i + 2, :], ACT.Square), "key_squares")
            act.wait_ge(sem("cum"), 1)
            link(f(W[:, :, :], cum[:, :, :], ACT.Exp, scale=-KAPPA), "decays")
            link(f(Wi[:, :, :], cum[:, :, :], ACT.Exp, scale=KAPPA), "decays")
            link(f(Wp[:, :, :], tmp[:, :, :], ACT.Exp, scale=-KAPPA), "decays")
            act.wait_ge(sem("key_norms"), 2)
            for i in range(2):
                link(f(kk[:, 2 * i:2 * i + 2, :], kk[:, 2 * i:2 * i + 2, :], ACT.Sqrt), "key_roots")
            b = ready(act, "kc")
            link(f(kcT[:, :, :], view(psum[:, b, :], 0, 2, T), ACT.Copy), "kc_copied")
            for n in range(2):
                b = ready(act, "kv", n)
                link(f((vs, vw)[n], view(psum[:, b, T:2 * T], 0, TT, P), ACT.Copy))
                link(f(nsq[:, 0, :], psum[:, b, 0:T], ACT.Square), "nsa_squares")
                b = ready(act, "kvn", n)
                if n:
                    act.wait_ge(sem("keys_normed"), n)
                inv_root(nrs[:, 0, :], psum[:, b, 0:T], "nsa_rs")
            for n in range(2):
                b = ready(act, "q", n)
                link(f(nsq[:, :, :], view(psum[:, b, :], 0, 2, T), ACT.Square), "nsa_squares")
                b = ready(act, "qn", n)
                act.wait_ge(sem("queries_normed" if n else "keys_normed"), 1 if n else 2)
                inv_root(nrs[:, :, :], view(psum[:, b, :], 0, 2, T), "nsa_rs")
            b = ready(act, "gl")
            link(f(gates[:, :, :], view(psum[:, b, 0:48], 0, 2, 24), ACT.Sigmoid), "gates")
            for kind in range(2):
                b = ready(act, "cmp", kind)
                if kind:
                    act.wait_ge(sem("cmp_hidden"), 1)
                link(f(csq[:, 0:NCMP], psum[:, b, 0:NCMP], ACT.Sigmoid), "cmp_sig")
            act.wait_ge(sem("cmp_hidden"), 2)
            b = ready(act, "kcmp")
            link(f(csq[:, 0:NCMP], psum[:, b, 0:NCMP], ACT.Square), "kcmp_squares")
            for g in range(NSA_G):
                b = ready(act, "vcmp", g)
                link(f(vcmp[0:NCMP, g, :], psum[0:NCMP, b, 0:HD], ACT.Copy), "vcmp")
            b = ready(act, "kcn")
            inv_root(crs[:, 0:NCMP], psum[:, b, 0:NCMP], "kcmp_rs")

            def tok_step(tt):
                for kind in range(4):
                    b = ready(act, "tok", tt, kind)
                    if tt and kind == 0:
                        ready(act, "y", 0)
                    link(f(tok[:, kind, :], psum[:, b, :], ACT.Copy), "tok")

            def inv_step(tt, s):
                name, kind, _, _, dst = INV[s]
                if kind == "add":
                    return
                for g in range(2):
                    b = ready(act, "inv", tt, s, g)
                    if tt and name == "D4T" and g == 0:
                        act.wait_ge(sem("rwkv_out"), 1)
                    link(f(BUF[dst][:, 4 * g:4 * g + 4, :], view(psum[:, b, :], 0, 4, P), ACT.Copy), "inv_copied")

            def qt_step(tt):
                b = ready(act, "qt", tt)
                link(f(QT, view(psum[:, b, :], 0, 4, P), ACT.Copy), "qt")

            def z_step(tt):
                b = ready(act, "z", tt)
                link(f(Z, psum[:, b, :], ACT.Copy), "z")

            def y_step(tt):
                b = ready(act, "y", tt)
                link(f(Y, psum[:, b, :], ACT.Copy), "y")

            def ynorm_step(tt):
                act.wait_ge(sem("y_centred"), tt + 1)
                link(f(SQ, YC, ACT.Square), "y_squared")
                b = ready(act, "yvar", tt)
                inv_root(Y, psum[:, b, :], "y_rs", eps=GN_EPS)

            def xk_step(j):
                xsquares("xk", j, "kx_squares", "kx_rs", "kx_normed")

            def xsquares(name, j, done, rs, used):
                b = ready(act, name, j)
                link(f(xsq[:, :, :], view(psum[:, b, :], 0, 2, T), ACT.Square), done)
                b = ready(act, name + "n", j)
                if j:
                    act.wait_ge(sem(used), j)
                inv_root(xrs[:, :], psum[:, b, 0:T], rs)

            def xv_step(j):
                b = ready(act, "xv", j)
                link(f(vxm[:, :, j * T:(j + 1) * T], view(psum[:, b, :], 0, 2, T), ACT.Copy), "vx")

            def cmpsc_step(_):
                for tt in range(TT):
                    act.wait_ge(sem("cmp_shifted"), tt + 1)
                    s = sc_c[:, tt, :, 0:NCMP]
                    link(f(s, s, ACT.Exp, scale=0.125), "cmp_exp")

            def score_step(u):
                tt, i = units[u]
                nk = P * (tt + 1)
                act.wait_ge(sem("score_max"), u + 1)
                if u >= 2:
                    act.wait_ge(sem("coef"), u - 1)
                for b in range(2):
                    s = S2[:, u % 2, b, 0:nk]
                    q = 2 * (u % 2) + b
                    link(f(s, s, ACT.Exp, bias=st[:, 28 + q:29 + q], scale=0.125, accum_out=st[:, 32 + q:33 + q]),
                         "exped" if b else "scalar_step")

            def turnp_step(u):
                tt, i = units[u]
                n = 2 * (tt + 1)
                b = ready(act, "pc", u)
                if u >= 2:
                    act.wait_ge(sem("pv_done"), u - 1)
                link(f(ptc[0:NCMP, u % 2, :], psum[0:NCMP, b, 0:P], ACT.Copy), "ptc")
                b = ready(act, "pt", u)
                link(f(PT[:, u % 2, 0:n, :], view(psum[:, b, 0:n * P], 0, n, P), ACT.Copy), "pt")

            def pv_step(u):
                tt, i = units[u]
                if i == NSA_H - 1:
                    act.wait_ge(sem("pv_done"), NSA_H * (tt + 1))
                    link(f(onT[:, :, tt * P:(tt + 1) * P], view(psum[:, 7, :], 0, 4, P), ACT.Copy), "on")

            steps = {"tok": tok_step, "inv": inv_step, "qt": qt_step, "z": z_step, "y": y_step,
                     "ynorm": ynorm_step, "xk": xk_step, "xv": xv_step, "cmpsc": cmpsc_step,
                     "score": score_step, "turnp": turnp_step, "pv": pv_step}
            for step, *args in order:
                if step in steps:
                    steps[step](*args)

            act.wait_ge(sem("h_mixed"), 4)
            squares("cross", h, hn3)
            for j in range(4):
                xsquares("xq", j, "qx_squares", "qx_rs", "qx_normed")
            for n in range(2 * X_H + 2):
                if n < 2 * X_H:
                    b = ready(act, "xs", n)
                    act.wait_ge(sem("xmax"), n + 1)
                    if n >= 2:
                        ready(act, "xp", n - 2)
                    link(f(xs[:, n % 2, :], psum[:, b, 0:MEM], ACT.Exp, bias=st[:, 42 + n % 2:43 + n % 2],
                           scale=float(X_HD) ** -0.5, accum_out=st[:, 44 + n % 2:45 + n % 2]), "xscores")
                if 1 <= n <= 2 * X_H:
                    b = ready(act, "xp", n - 1)
                    if n >= 3:
                        ready(act, "xo", n - 3)
                    link(f(xpt[:, (n - 1) % 2, :, :], view(psum[:, b, 0:256], 0, 2, P), ACT.Copy), "xpt")
                if n >= 2:
                    tt, i = (n - 2) % 2, (n - 2) // 2
                    b = ready(act, "xo", n - 2)
                    link(f(oxT[:, 2 * i:2 * i + 2, tt * P:(tt + 1) * P], view(psum[:, b, 0:256], 0, 2, P),
                           ACT.Copy), "ox")
            act.wait_ge(sem("h_crossed"), 4)
            squares("ffn", h, hn3)
            act.wait_ge(sem("logits_shifted"), 1)
            link(f(le, le, ACT.Exp), "logits_exp")

            act.sem_inc(sem("act_out"), 1)
            act.sem_inc(sem("y_out"), 1)
            act.wait_ge(sem("tabled"), 1)
            n_items = act.value_load(tabi[0:1, 0:1], min_val=NE, max_val=ITEMS)
            with act.Fori(0, n_items) as i:
                for n in range(2):
                    act.wait_ge(sem("glu"), i * 2 + n + 1)
                    f(sg[:, n, :], gl[:, n, :], ACT.Sigmoid, scale=1.702).then_inc(sem("sig"), 1)
                for n in range(2):
                    act.wait_ge(sem("act_turned"), i * 2 + n + 1)
                    f(actT[:, 2 * n:2 * n + 2, :], view(psum[:, 6, n * 256:(n + 1) * 256], 0, 2, P),
                      ACT.Copy).then_inc(sem("act_out"), 1)
                act.wait_ge(sem("piece_used"), i * 12 + 12)
                f(yb, psum[:, 7, :], ACT.Copy).then_inc(sem("y_out"), 1)

        @block.gpsimd
        def _(pool):
            step = [0]

            def link(ins, name="pool_step"):
                step[0] += name == "pool_step"
                ins.then_inc(sem(name), 1)
                pool.wait_ge(sem(name), step[0] if name == "pool_step" else 1)

            def keep(o, op, base, pattern, mult, fill=0.0):
                link(pool.affine_select(out=o, in_=o, compare_op=op, fill=fill, base=base, pattern=pattern,
                                        channel_multiplier=mult))

            def within(o, size):
                n = P // size
                keep(o, ALU.is_ge, 0, [[-size, n], [0, size]], 1)
                keep(o, ALU.is_ge, size - 1, [[size, n], [0, size]], -1)

            link(pool.memset(ident[:, :], 0.0))
            keep(ident[:, :], ALU.not_equal, 0, [[-1, P]], 1, fill=1.0)
            link(pool.memset(ones[:, :], 1.0))
            link(pool.memset(blk[:, :], 1.0))
            within(blk[:, :], HD)
            link(pool.memset(blk64[:, :], 1.0 / HD))
            within(blk64[:, :], HD)
            link(pool.memset(o256[:, :], 1.0 / X_HD))
            link(pool.memset(before[:, :], 1.0))
            keep(before[:, :], ALU.is_gt, 0, [[1, P]], -1)
            link(pool.memset(masks4[:, :, :], 1.0))
            for i, (size, op) in enumerate(((16, ALU.is_gt), (CH, ALU.is_ge), (CH, ALU.is_gt), (CH, ALU.is_ge))):
                keep(masks4[:, i, :], op, 0, [[1, P]], -1)
                within(masks4[:, i, :], size)
            link(pool.memset(masks3[:, 0, :], 1.0))
            link(pool.memset(lowers[:, :, :], 1.0))
            for o, size in ((masks3[:, 0, :], 16), (lowers[:, 0, :], 32), (lowers[:, 1, :], CH)):
                keep(o, ALU.is_gt, 0, [[-1, P]], 1)
                within(o, size)
            link(pool.tensor_tensor(masks3[:, 1, :], lowers[:, 0, :], masks3[:, 0, :], ALU.subtract))
            link(pool.tensor_tensor(masks3[:, 2, :], lowers[:, 1, :], lowers[:, 0, :], ALU.subtract))
            link(pool.memset(mreset[:, :], 1.0))
            link(pool.memset(mreset[:, 0:T:CH], 0.0))
            link(pool.iota(dist[:, 0:T], [[1, T]], base=-P, channel_multiplier=-1,
                           allow_small_or_imprecise_dtypes=True))
            keep(dist[:, 0:T], ALU.is_ge, P, [[-1, T]], 1, fill=NEG)
            for tt in range(TT):
                o = distc[:, tt, :]
                link(pool.iota(o, [[STRIDE, 16]], base=CMP - 1 - P * tt, channel_multiplier=-1,
                               allow_small_or_imprecise_dtypes=True))
                keep(o, ALU.is_ge, P * tt - CMP + 1, [[-STRIDE, 16]], 1, fill=NEG)
                link(pool.memset(maskc[:, tt, :], 1.0))
                keep(maskc[:, tt, :], ALU.is_ge, P * tt - CMP + 1, [[-STRIDE, 16]], 1)
            link(pool.iota(iotas[:, :], [[0, 2], [1, SLOTS]], base=0, channel_multiplier=0,
                           allow_small_or_imprecise_dtypes=True))
            link(pool.iota(reve[:, :], [[-1, NE]], base=64, channel_multiplier=0,
                           allow_small_or_imprecise_dtypes=True))
            link(pool.memset(sc_c[:, :, :, :], 0.0))
            link(pool.memset(eps_col[:, 0:1], EPS))
            link(pool.memset(eps_col[:, 1:2], GN_EPS))
            link(pool.memset(h1T[:, :, :], 0.0), "consts")
            for tt in range(TT):
                for i in range(NSA_H):
                    ins = pool.tensor_scalar(sc_c[:, tt, i, :], distc[:, tt, :], 8.0 * SLOPE[i], None, ALU.mult)
            ins.then_inc(sem("cmp_bias"), 1)

            for j in range(J_V + 2):
                pool.wait_ge(sem("job_taken"), j + 1)
                if j >= 2:
                    pool.wait_ge(sem("mixed"), j - 1)
                pool.tensor_tensor(diff[:, j % 2, :, :], shifted[:, j % 2, :, 0:T], shifted[:, j % 2, :, 1:T + 1],
                                   ALU.subtract).then_inc(sem("differenced"), 1)
            def turnp_step(u):
                tt, i = units[u]
                nk = P * (tt + 1)
                pool.wait_ge(sem("coef"), u + 1)
                s = S2[:, u % 2, :, 0:nk]
                c = st[:, 36 + 2 * (u % 2):38 + 2 * (u % 2)].unsqueeze(2)
                pool.tensor_tensor(s, s, bcast(c, P, 2, nk), ALU.mult).then_inc(sem("probs"), 1)

            for step, *args in order:
                if step == "turnp":
                    turnp_step(*args)
            pool.wait_ge(sem("ox"), 8)
            pool.iota(it1, [[1, EXTRA], [0, NE]], base=0, channel_multiplier=0,
                      allow_small_or_imprecise_dtypes=True).then_inc(sem("item_iota"), 1)

            pool.wait_ge(sem("tabled"), 1)
            n_items = pool.value_load(tabi[0:1, 0:1], min_val=NE, max_val=ITEMS)

            def bias_in(e):
                pool.dma_start(bias[0:1, 0:2 * DE], a["mlp1_b"][0, bass.ds(e, 1), :]).then_inc(sem("bias_in"), 16)
                pool.dma_start(bias[0:1, 2 * DE:3 * DE], a["mlp2_b"][0, bass.ds(e, 1), :]) \
                    .then_inc(sem("bias_in"), 16)

            bias_in(0)
            with pool.Fori(1, n_items) as i:
                e = pool.value_load(tabi[0:1, bass.ds(i + 1, 1)], min_val=0, max_val=NE - 1)
                pool.wait_ge(sem("piece_used"), i * 12 - 3)
                bias_in(e)

        @block.sync
        def _(sp):
            def rows(name):
                return a[name]

            sp.dma_start(h[:, :, :], a["x"][0].rearrange("(t p) d -> p t d", p=P)).then_inc(sem("x_in"), 16)

            def job_in(j):
                name, c = JOBS[j]
                if j >= WSLOTS:
                    sp.wait_ge(sem("tile_ready"), last_tile(j - WSLOTS) + 1)
                if name == "q":
                    o = slot(j)[:, 0:2048].rearrange("p (k i g d) -> p g i k d", k=8, i=2, g=2)
                    for g in range(NSA_G):
                        for i in range(2):
                            c0 = C_Q + 256 * g + 128 * c + HD * i
                            sp.dma_start(o[:, g, i], a["w_in"][0, :, c0:c0 + HD].rearrange("(k p) n -> p k n", p=P)) \
                              .then_inc(sem(f"weights_in_{j % WSLOTS}"), 16)
                    return
                if name.startswith("cmp"):
                    o = slot(j)[:, 0:2048].rearrange("p (l e) -> p l e", l=CMP)
                    for g in range(NSA_G):
                        sp.dma_start(o[64 * g:64 * g + 64], a[name][0].rearrange("(l d) e -> d l e", d=HD)) \
                          .then_inc(sem(f"weights_in_{j % WSLOTS}"), 16)
                    return
                if name == "gl":
                    sp.dma_start(wjob(j, 24), a["w_in"][0, :, c:c + 24].rearrange("(k p) n -> p k n", p=P)) \
                      .then_inc(sem(f"weights_in_{j % WSLOTS}"), 16)
                    return
                sp.dma_start(wjob(j), a[name][0, :, c:c + T].rearrange("(k p) n -> p k n", p=P)) \
                  .then_inc(sem(f"weights_in_{j % WSLOTS}"), 16)

            LAST = {J_KC: ("kc",), J_KS: ("kv", 0), J_KW: ("kv", 1), J_Q: ("q", 0), J_Q + 1: ("q", 1),
                    J_GL: ("gl",), J_CK: ("cmp", 0), J_CV: ("cmp", 1)}

            def last_tile(j):
                if j in LAST:
                    return tiles[LAST[j]][1]
                for base, name in ((J_XO, "xout"), (J_XQ, "xq"), (J_OUT, "wout"), (J_XV, "xv"), (J_XK, "xk")):
                    if j >= base:
                        return tiles[name, j - base][1]
                return tiles["job", j][1]

            for j in range(WSLOTS):
                job_in(j)
                if j == 0:
                    for name, n in VROWS:
                        src = a[name][0]
                        r0 = VCOL[name]
                        if name == "rwkv_r_k":
                            src = src.rearrange("(a b) c -> a (b c)", b=2)
                            o = vrows[r0:r0 + n, :]
                        elif n > 1 or name in ("x",):
                            src = src.rearrange("(a b) -> a b", b=P)
                            o = vrows[r0:r0 + n, :]
                        else:
                            sp.dma_start(vrows[r0:r0 + 1, 0:HD], a[name][0:1, :]).then_inc(sem("rows_in"), 16)
                            sp.dma_start(vrows[r0:r0 + 1, HD:P], a[name][0:1, :]).then_inc(sem("rows_in"), 16)
                            continue
                        sp.dma_start(o, src).then_inc(sem("rows_in"), 16)
                    for kind, name in enumerate(("cmp_pe_k", "cmp_pe_v")):
                        for g in range(2):
                            sp.dma_start(perow[0:CMP, kind, 64 * g:64 * g + 64], a[name][0]) \
                              .then_inc(sem("rows_in"), 16)
                    sp.dma_start(memx, a["mem"][0].rearrange("(t p) d -> p t d", p=P)).then_inc(sem("mem_in"), 16)
                    sp.dma_start(lora[0:64, 0, :], a["rwkv_w_up"][0]).then_inc(sem("small_in"), 16)
                    sp.dma_start(lora[64:128, 0, :], a["rwkv_a_up"][0]).then_inc(sem("small_in"), 16)
                    sp.dma_start(lora[:, 1, :], a["rwkv_g_up"][0]).then_inc(sem("small_in"), 16)
                    for kind, name in enumerate(("cmp_k_w2", "cmp_v_w2")):
                        for g in range(2):
                            sp.dma_start(cw2[64 * g:64 * g + 64, kind, :], a[name][0]).then_inc(sem("small_in"), 16)
                    sp.dma_start(rw[:, :, :], a["router_w"][0].rearrange("(k p) n -> p k n", p=P)) \
                      .then_inc(sem("small_in"), 16)
                    sp.dma_start(rb[0:1, :], a["router_b"][0:1, :]).then_inc(sem("small_in"), 16)

            w1_src = a["mlp1_w"][0].rearrange("e (k p) (h n c) -> e n h p k c", p=P, h=2, n=2)
            w2_src = a["mlp2_w"][0].rearrange("e (k p) n -> e p k n", p=P)
            w1_dst = w1.rearrange("p k (h n c) -> p n k h c", h=2, n=2)

            def piece(e, c):
                if c < 8:
                    n, k, half = c // 4, 4 * (c // 2 % 2), c % 2
                    sp.dma_start(w1_dst[:, n, k:k + 4, half], w1_src[bass.ds(e, 1), n, half, :, k:k + 4]
                                 .rearrange("e p k c -> p (e k) c")).then_inc(sem(f"w1_in_{c}"), 16)
                else:
                    n, q = (c - 8) // 2, c % 2
                    k = 4 * q + 2 * n
                    sp.dma_start(w2[:, k:k + 2, :], w2_src[bass.ds(e, 1), :, k:k + 2, :]
                                 .rearrange("e p k n -> p (e k) n")).then_inc(sem(f"w2_in_{c - 8}"), 16)

            left = list(range(12))
            for j in range(WSLOTS, len(JOBS)):
                job_in(j)
                if j == J_OUT + 2:
                    sp.wait_ge(sem("rwkv_out"), 2)
                if j >= J_OUT + 2:
                    for c in left[:2]:
                        piece(0, c)
                    left = left[2:]
            sp.wait_ge(sem("tabled"), 1)
            n_items = sp.value_load(tabi[0:1, 0:1], min_val=NE, max_val=ITEMS)
            with sp.Fori(1, n_items) as i:
                e = sp.value_load(tabi[0:1, bass.ds(i + 1, 1)], min_val=0, max_val=NE - 1)
                for c in range(12):
                    sp.wait_ge(sem("piece_used"), i * 12 + (c - 11))
                    piece(e, c)
            for tt in range(TT):
                sp.wait_ge(sem("out_ready"), 2 * tt + 2)
                sp.dma_start(out[0, tt * P:(tt + 1) * P, :], h[:, tt, :]).then_inc(sem("out_done"), 16)
            sp.wait_ge(sem("out_done"), 32)


_INS = ["x", "mem", "norm_mix_g", "w_in", "q_norm_g", "k_cmp_norm_g", "k_slc_norm_g", "k_win_norm_g",
        "cmp_pe_k", "cmp_pe_v", "cmp_k_w1", "cmp_k_w2", "cmp_v_w1", "cmp_v_w2",
        "rwkv_mu", "rwkv_w0", "rwkv_w_up", "rwkv_a0", "rwkv_a_up", "rwkv_g_up", "rwkv_k_k", "rwkv_k_a",
        "rwkv_r_k", "rwkv_ln_w", "rwkv_ln_b", "w_out", "norm_x_g", "norm_mem_g", "xq_w", "xk_w", "xv_w",
        "xq_norm_g", "xk_norm_g", "xo_w", "norm_ffn_g", "router_w", "router_b",
        "mlp1_w", "mlp1_b", "mlp2_w", "mlp2_b"]


def kernel(**inputs):
    import concourse.bacc as bacc
    from concourse.bass_utils import run_bass_kernel_spmd

    nc = bacc.Bacc("TRN2", target_bir_lowering=False, num_devices=1)
    arrays, args = {}, {}
    for name in _INS:
        arr = np.ascontiguousarray(inputs[name])
        arrays[f"in_{name}"] = arr
        args[name] = nc.dram_tensor(f"in_{name}", arr.shape, mybir.dt.from_np(arr.dtype),
                                    kind="ExternalInput").ap()
    out = nc.dram_tensor("out_h", (1, T, D), F32, kind="ExternalOutput").ap()
    build(nc, args, out)
    r = run_bass_kernel_spmd(nc, [arrays], core_ids=[0])
    return r.results[0]["out_h"]
```

```python
from contextlib import ExitStack

import numpy as np

import concourse.bass as bass
from concourse import mybir

P = 128
F32 = mybir.dt.float32
I32 = mybir.dt.int32
ALU = mybir.AluOpType
ACT = mybir.ActivationFunctionType
AX = mybir.AxisListType.X

T = 256
TT = T // P
D = 1024
KD = D // P
MEM = 256
HD = 64
NSA_H, NSA_G = 8, 2
RW_H = 8
CMP, STRIDE = 32, 16
NCMP = T // STRIDE - CMP // STRIDE + 1
X_H, X_HD = 4, 256
NE, TOPK = 32, 4
DE = 1024
SLOTS = 64
EXTRA = (T * TOPK) // (SLOTS + 1)
ITEMS = NE + EXTRA
ICOLS = ITEMS + 1
CH = 64
EPS = 1e-6
GN_EPS = HD * 1e-5
NEG = -1e30
KAPPA = float(np.exp(-0.5))

C_Q, C_KC, C_VC, C_KS, C_VS, C_KW, C_VW, C_GL = 0, 512, 640, 768, 896, 1024, 1152, 1280
C_R, C_K, C_V, C_WD = 1304, 1816, 2328, 2840

JOBS = [("w_in", C_WD), ("w_in", C_K), ("w_in", C_K + 256), ("w_in", C_R), ("w_in", C_R + 256),
        ("w_in", C_V), ("w_in", C_V + 256),
        ("w_in", C_KC), ("w_in", C_KS), ("w_in", C_KW), ("q", 0), ("q", 1), ("gl", C_GL),
        *[("xk_w", 256 * j) for j in range(4)], ("cmp", 0)] + \
    [("xv_w", 256 * j) for j in range(4)] + \
    [("w_out", 256 * j) for j in range(4)] + [("xq_w", 256 * j) for j in range(4)] + \
    [("xo_w", 256 * j) for j in range(4)]
WSLOTS = 3
J_LORA, J_K, J_R, J_V, J_KC, J_KS, J_KW, J_Q, J_GL, J_CMP, J_XK, J_XV, J_OUT, J_XQ, J_XO = \
    0, 1, 3, 5, 7, 8, 9, 10, 12, 17, 13, 18, 22, 26, 30

VROWS = [("norm_mix_g", 8), ("norm_x_g", 8), ("norm_mem_g", 8), ("norm_ffn_g", 8), ("rwkv_mu", 14),
         ("rwkv_w0", 4), ("rwkv_a0", 4), ("rwkv_k_k", 4), ("rwkv_k_a", 4), ("rwkv_r_k", 4),
         ("rwkv_ln_w", 4), ("rwkv_ln_b", 4), ("xq_norm_g", 2), ("xk_norm_g", 2),
         ("q_norm_g", 1), ("k_slc_norm_g", 1), ("k_win_norm_g", 1), ("k_cmp_norm_g", 1)]
VCOL = {}
for _name, _rows in VROWS:
    VCOL[_name] = sum(r for n, r in VROWS[:len(VCOL)])
NV = sum(r for _, r in VROWS)


def view(buf, off, *dims):
    n = int(np.prod(dims))
    flat = buf[:, off:off + n]
    if len(dims) == 1:
        return flat
    names = "abcd"[:len(dims)]
    return flat.rearrange(f"p ({' '.join(names)}) -> p {' '.join(names)}",
                          **{c: d for c, d in zip(names[1:], dims[1:])})


def bcast(ap, *shape):
    return ap.to_broadcast(list(shape))


def build(nc, a, out):
    ctx = ExitStack()
    with ctx:
        sems = {}

        def sem(name):
            if name not in sems:
                sems[name] = ctx.enter_context(nc.semaphore(name))
            return sems[name]

        def sb(name, *dims, dt=F32, rows=P):
            return ctx.enter_context(nc.sbuf_tensor("sb_" + name, [rows, *dims], dt))

        ring = sb("ring", 24576)
        h = sb("h", TT, D)
        hnT = sb("hnT", KD, T)
        hn = sb("hn", 2048)
        wsl = sb("wsl", WSLOTS * 2048)
        kxT = sb("kxT", KD, T)
        vx = sb("vx", 2048)
        qx = sb("qx", 2048)
        ox = sb("ox", 2048)
        mixT = sb("mixT", KD, T)
        onT, orT = mixT[:, 0:4, :], mixT[:, 4:8, :]
        ident = sb("ident", P)
        blk = sb("blk", P)
        blk64 = sb("blk64", P)
        o256 = sb("o256", P)
        before = sb("before", P)
        ones = sb("ones", P)
        masks4 = sb("masks4", 4, CH)
        masks3 = sb("masks3", 3, CH)
        identc = sb("identc", CH)
        dist = sb("dist", T)
        distc = sb("distc", TT, 16)
        maskc = sb("maskc", TT, 16)
        mreset = sb("mreset", T)
        vrows = sb("vrows", P)
        vecs = sb("vecs", P)
        omka = sb("omka", 4)
        eps_col = sb("eps_col", 2)
        perow = sb("perow", 2, P)
        peT = sb("peT", 2, CMP // 2)
        cw2 = sb("cw2", HD)
        rw = sb("rw", KD, NE)
        rb = sb("rb", 3 * NE)
        rbb = sb("rbb", NE)
        psq = sb("psq", TT, 4)
        wend = sb("wend", 4, 4)
        kcmpT = sb("kcmpT", 16)
        vcmp = sb("vcmp", 2, HD)
        h1T = sb("h1T", NSA_G, NCMP)
        csq = sb("csq", 2 * NCMP)
        crs = sb("crs", 16)
        gates = sb("gates", TT, 24)
        sc_c = sb("sc_c", TT, 8, 16)
        ptc = sb("ptc", 2, 2, P)
        st = sb("st", 96)
        rank = sb("rank", TT, ICOLS)
        gate = sb("gate", TT, ICOLS)
        tabi = sb("tabi", 64, dt=I32)
        psum = ctx.enter_context(nc.psum_tensor("ps", [P, 8, 512], F32))

        GM = view(ring, 0, 4, 16, CH)
        DT3 = view(ring, 4096, 3, 16, CH)
        B1, B2, B3, B4, PP = (view(ring, 7168 + 1024 * i, 16, CH) for i in range(5))
        QT = view(ring, 12288, 2, 8, CH)
        AKV, Z, U = (view(ring, 4096 + 1024 * i, 16, CH) for i in range(3))
        AR = view(ring, 14336, 4, 2, 2, P)
        bhT = view(ring, 16384, 4, T)
        khT = view(ring, 17408, 4, T)
        gT = view(ring, 18432, 4, T)
        bonus = view(ring, 19456, 4, T)
        vT = view(ring, 20480, 4, T)
        tokA, tokV = view(ring, 21504, TT, 512), view(ring, 22528, TT, 512)
        tokB, tokK = view(ring, 7168, TT, 512), view(ring, 10240, TT, 512)
        SH = view(ring, 23552, 4, 4, HD)
        (kT, rT, sig, cum, W, Wi, Wp, kkr, sqr, kk, aT, k2, tmp) = \
            (view(ring, 1024 * i, 4, T) for i in range(13))
        wdad = view(ring, 13312, T)
        gd = view(ring, 13568, T)
        Y = [view(ring, 8192 + 512 * tt, 512) for tt in range(TT)]
        YC = [view(ring, 9216 + 512 * tt, 512) for tt in range(TT)]
        SQ = view(ring, 13312, 512)
        mfull = view(ring, 0, 7, P)
        shifted = view(kxT[:, :, :].rearrange("p a b -> p (a b)"), 0, 2, 2, 257)
        diff = view(vx, 0, 2, 2, T)
        lora = view(vx, 1024, 2, 512)
        qT = view(hn, 0, 4, T)
        ksT, kwT = view(hn, 1024, T), view(hn, 1280, T)
        vs, vw = view(hn, 1536, TT, P), view(hn, 1792, TT, P)
        kcT = view(onT[:, :, :].rearrange("p a b -> p (a b)"), 0, 4, P)
        nsq = view(onT[:, :, :].rearrange("p a b -> p (a b)"), 512, 2, T)
        orf = orT[:, :, :].rearrange("p a b -> p (a b)")
        XC = view(orf, 0, 2, CMP // 2, NSA_G, NCMP)
        nrs = view(orf, 512, 2, T)
        memx = view(qx, 0, TT, D)
        S2 = view(qx, 0, 2, 4, T)
        PT = view(hnT[:, :, :].rearrange("p a b -> p (a b)"), 0, 2, 2, 4, P)
        memT = view(ox, 0, KD, T)
        qxT = view(qx, 0, KD, T)
        oxT = view(qx, 0, KD, T)
        vxm = view(vx, 0, TT, D)

        xsq = sb("xsq", 2, T)
        xrs = sb("xrs", T)
        rsB = view(hn, 1024, T)
        diag = view(hn, 1280, TT, P)
        junk = view(hn, 1536, 512)
        xs = view(hn, 0, 2, MEM)
        xpt = view(hn, 512, 2, 2, P)
        hf = hnT[:, :, :].rearrange("p a b -> p (a b)")
        xgT, actv, actT, yb = view(hf, 0, KD, SLOTS), view(hf, 512, 512), view(hf, 1024, 4, P), view(hf, 1536, 512)
        gl, ll, sg = (view(wsl, 512 * i, 2, 256) for i in range(3))
        selg, sel, selgT = view(wsl, 1536, TT, P), view(wsl, 1792, TT, SLOTS), view(wsl, 1920, TT, P)
        bias = view(wsl, 2176, 3 * DE)
        kf = kxT[:, :, :].rearrange("p a b -> p (a b)")
        lw, le, key, pick = (view(kf, 64 * i, TT, NE) for i in range(4))
        chosen, place = view(kf, 256, TT, NE), view(kf, 320, TT, NE)
        gsm, best = view(kf, 384, TT, NE), view(kf, 448, TT, 8)
        extra, upto, off = (view(kf, 512 + NE * i, NE) for i in range(3))
        top = view(kf, 640, TT)
        it1, it2, it3 = (view(hn, 512 * i, EXTRA, NE) for i in range(3))
        blk_of, exp_of, it4 = (view(kf, 704 + EXTRA * i, EXTRA) for i in range(3))
        tabf = view(kf, 768, 64)
        iotas = sb("iotas", P)
        of_expert = sb("of_expert", ICOLS)
        hot = sb("hot", SLOTS)
        reve = sb("reve", NE)
        w1 = view(ring, 0, KD, 2 * DE)
        w2 = view(ring, 16384, KD, D)
        ahead = [view(buf, 0, 4, 512) for buf in (ox, mixT[:, :, :].rearrange("p a b -> p (a b)"), vx, qx)]

        def vec(name, i=0, n=1):
            return vecs[:, VCOL[name] + i:VCOL[name] + i + n]

        def slot(j):
            return wsl[:, (j % WSLOTS) * 2048:(j % WSLOTS + 1) * 2048]

        def wjob(j, n=256):
            return slot(j)[:, 0:8 * n].rearrange("p (k n) -> p k n", k=8)

        INV = [("D2", "copy", "DT", "D", "B1"), ("D2T", "copy", "D", "DT", "B2"),
               ("D4", "copy", "B2", "B1", "B3"), ("D4T", "copy", "B1", "B2", "B4"),
               ("P2", "add", "B2", "PP", "PP"), ("D8T", "copy", "B3", "B4", "B1"),
               ("P4", "add", "B4", "PP", "PP"), ("P8", "add", "B1", "PP", "PP"),
               ("P8T", "turn", "PP", None, "B2"), ("T1", "copy", "E1T", "PP", "B3"),
               ("M1", "add", "B2", "B3", "PP"), ("M1T", "turn", "PP", None, "B2"),
               ("T2", "copy", "E2T", "PP", "B3"), ("M2", "add", "B2", "B3", "PP")]
        COPIES = [n for n, kind, *_ in INV if kind != "add"]
        ADDS = [n for n, kind, *_ in INV if kind == "add"]
        NEEDS = {"D2": ["G"], "D2T": ["G"], "D4": ["D2", "D2T"], "D4T": ["D2T"], "P2": ["P1", "D2T"],
                 "D8T": ["D4", "D4T"], "P4": ["P2", "D4T"], "P8": ["P4", "D8T"], "P8T": ["P8"],
                 "T1": ["P8"], "M1": ["P8T", "T1"], "M1T": ["M1"], "T2": ["M1"], "M2": ["M1T", "T2"]}
        BUF = {"D": GM[:, 0], "DT": DT3[:, 0], "E1T": DT3[:, 1], "E2T": DT3[:, 2],
               "B1": B1, "B2": B2, "B3": B3, "B4": B4, "PP": PP}

        def inv_done(name, q):
            if name in ("G", "P1"):
                return "p1_made", q + 1
            own, group = ("inv_added", ADDS) if name in ADDS else ("inv_copied", COPIES)
            return own, 2 * group.index(name) + q + 1

        def matrix(q, tt, p):
            return 8 * q + 4 * tt + p

        core = [("tok", 0), ("xk", 0), ("tok", 3), ("xk", 1), ("xkn", 0), ("parts", 0), ("xkn", 1), ("xk", 2),
                ("parts", 1), ("xkn", 2), ("g3",), ("xk", 3)]
        start = len(core) + 1
        XV_AT = (18, 24, 25, 34)
        for s, (name, *_) in enumerate(INV):
            core.append(("inv", s))
            if name == "T1":
                core += [("tok", 1), ("tok", 2)]
        core += [("qt",), ("akv",), ("z",)]
        core += [("chunk", 0), ("chunk", 1), ("y", 0), ("chunk", 2), ("ymean", 0), ("chunk", 3), ("yvar", 0),
                 ("y", 1), ("ymean", 1), ("yvar", 1)]
        for j, at in enumerate(XV_AT):
            core.insert(at + j, ("xv", j))
        units = [(tt, j) for tt in range(TT) for j in range(4)]
        fill = [("xkn", 3), ("cmp",), ("cmpout",), ("cmpsc",)]
        for u in range(len(units) + 2):
            if u < len(units):
                fill.append(("score", u))
            if u >= 2:
                fill.append(("pv", u - 2))
            if 1 <= u <= len(units):
                fill.append(("turnp", u - 1))
        EARLY = 11
        order = []
        for i, step in enumerate(core):
            order.append(step)
            if i >= start:
                n, of = i - start, len(core) - start - EARLY
                order += fill[n * len(fill) // of:(n + 1) * len(fill) // of]
        CROSS = [("project", 0), ("project", 1), ("norm", 0), ("project", 2), ("norm", 1), ("score", 0), ("score", 1),
                 ("project", 3), ("norm", 2), ("turn", 0), ("turn", 1), ("norm", 3)]
        for n in range(0, 2 * X_H, 2):
            if n:
                CROSS += [("turn", n), ("turn", n + 1)]
            if n + 2 < 2 * X_H:
                CROSS += [("score", n + 2), ("score", n + 3)]
            CROSS += [("pv", n), ("pv", n + 1)]
        SLOPE = [float(2.0 ** (-8.0 * (i + 1) / NSA_H)) for i in range(NSA_H)]

        TOKS = [0, 3, 1, 2]
        tiles = {}
        block = ctx.enter_context(nc.Block())

        def ready(eng, *name):
            bank, number = tiles[name]
            eng.wait_ge(sem("tile_ready"), number + 1)
            return bank

        NORMS = ["x", "mem"]

        @block.tensor
        def _(pe):
            owners = {}

            def tile(*name, freed, bank=None):
                n = sum(1 for b, _ in tiles.values() if b != 7)
                if bank is None:
                    bank = n % 7
                if bank in owners:
                    own, value = owners[bank]
                    pe.wait_ge(sem(own), value)
                owners[bank] = freed
                tiles[name] = (bank, n)
                return psum[:, bank, :]

            def loaded(j):
                transfers = sum({"q": 4, "cmp": 2, "w_out": 3}.get(JOBS[i][0], 1)
                                for i in range(j % WSLOTS, j + 1, WSLOTS))
                pe.wait_ge(sem(f"weights_in_{j % WSLOTS}"), 16 * transfers)

            def turn_norm(which, src, freed):
                for tt in range(TT):
                    pe.wait_ge(sem("rows_normed"), 2 * NORMS.index(which) + tt + 1)
                    for half in range(2):
                        t = tile("turn", which, tt, half, freed=(freed, 2 * tt + half + 1))
                        for k in range(4):
                            c = (4 * half + k) * P
                            mm = pe.transpose(t[:, k * P:(k + 1) * P], src[:, tt, c:c + P], ident[:, :])
                        mm.then_inc(sem("tile_ready"), 1)

            def project(t, w, act, cols=2):
                for g in range(cols):
                    for k in range(KD):
                        mm = pe.matmul(t[:, g * T:(g + 1) * T], w[:, k, g * P:(g + 1) * P], act[:, k, :],
                                       start=k == 0, stop=k == KD - 1)
                return mm

            pe.wait_ge(sem("ident_set"), 1)
            pe.wait_ge(sem("gain_in"), 16)
            t = tile("gain", freed=("gain", 1))
            pe.transpose(t[:, 0:8], vrows[0:8, :], ident[0:8, 0:8]).then_inc(sem("tile_ready"), 1)
            hn3 = view(hn, 0, TT, D)
            turn_norm("x", hn3, "xT")
            def rwkv_job(j):
                loaded(j)
                t = tile("job", j, freed=("job_taken", j + 1))
                project(t, wjob(j), hnT).then_inc(sem("tile_ready"), 1)

            pe.wait_ge(sem("xT"), 4)
            pe.wait_ge(sem("consts"), 1)
            for j in range(J_LORA, J_R + 2):
                rwkv_job(j)
                if j == J_LORA:
                    pe.wait_ge(sem("rows_in"), 16 * (len(VROWS) - 1) + 16 * 6)
                    t = tile("vecs", freed=("vecs", 1))
                    pe.transpose(t[:, 0:NV], vrows[0:NV, :], ident[0:NV, 0:NV])
                    for kind in range(2):
                        mm = pe.transpose(t[:, P + CMP // 2 * kind:P + CMP // 2 * (kind + 1)],
                                          perow[0:CMP // 2, kind, :], ident[0:CMP // 2, 0:CMP // 2])
                    mm.then_inc(sem("tile_ready"), 1)
                    turn_norm("mem", memx, "memT")
            pe.wait_ge(sem("small_in"), 16 * 7)
            pe.wait_ge(sem("lora_in"), 2)
            pe.wait_ge(sem("mixed"), 1)
            for name, rows, w, act in (("zw", slice(0, 64), 0, wdad), ("az", slice(64, 128), 0, wdad),
                                       ("gg", slice(0, 128), 1, gd)):
                for i in range(2):
                    t = tile(name, i, freed=(name, i + 1))
                    for p in (2 * i, 2 * i + 1):
                        mm = pe.matmul(t[:, (p % 2) * T:(p % 2 + 1) * T], lora[rows, w, p * P:(p + 1) * P],
                                       act[rows, :], start=True, stop=True)
                    mm.then_inc(sem("tile_ready"), 1)
            rwkv_job(J_V)
            rwkv_job(J_V + 1)
            loaded(J_KC)
            t = tile("kc", freed=("kc_copied", 1))
            w = wjob(J_KC)
            for b in range(4):
                for k in range(KD):
                    for par in range(2):
                        mm = pe.matmul(t[64 * par:64 * par + 64, b * P:(b + 1) * P], w[:, k, 64 * b:64 * b + 64],
                                       hnT[:, k, par:T:2], start=k == 0, stop=k == KD - 1)
            mm.then_inc(sem("tile_ready"), 1)

            for i in range(2):
                pe.wait_ge(sem("key_squares"), i + 1)
                t = tile("kks", i, freed=("key_norms", i + 1))
                pe.matmul(t, blk[:, :], sqr[:, 2 * i:2 * i + 2, :], start=True, stop=True) \
                  .then_inc(sem("tile_ready"), 1)

            def keys_job(n):
                loaded(J_KS + n)
                t = tile("kv", n, freed=("keys_taken", n + 1))
                w = wjob(J_KS + n)
                project(t, w, hnT, cols=1)
                for tt in range(TT):
                    for k in range(KD):
                        mm = pe.matmul(t[:, T + tt * P:T + (tt + 1) * P], hnT[:, k, tt * P:(tt + 1) * P],
                                       w[:, k, P:2 * P], start=k == 0, stop=k == KD - 1)
                mm.then_inc(sem("tile_ready"), 1)

            def keys_norm(n):
                pe.wait_ge(sem("nsa_squares"), n + 1)
                t = tile("kvn", n, freed=("nsa_rs", n + 1))
                pe.matmul(t[:, 0:T], blk64[:, :], nsq[:, n, :], start=True, stop=True) \
                  .then_inc(sem("tile_ready"), 1)

            def queries_job(n):
                loaded(J_Q + n)
                t = tile("q", n, freed=("queries_taken", n + 1))
                project(t, wjob(J_Q + n), hnT).then_inc(sem("tile_ready"), 1)

            def queries_norm(n):
                pe.wait_ge(sem("nsa_squares"), n + 3)
                t = tile("qn", n, freed=("nsa_rs", n + 3))
                pe.matmul(t, blk64[:, :], (xsq, nsq)[n][:, :, :], start=True, stop=True) \
                  .then_inc(sem("tile_ready"), 1)

            keys_job(0)
            keys_job(1)
            keys_norm(0)
            queries_job(0)
            keys_norm(1)
            queries_job(1)
            queries_norm(0)
            loaded(J_GL)
            t = tile("gl", freed=("gates_taken", 1))
            w = wjob(J_GL, 24)
            for tt in range(TT):
                for k in range(KD):
                    mm = pe.matmul(t[:, tt * 24:(tt + 1) * 24], hnT[:, k, tt * P:(tt + 1) * P], w[:, k, :],
                                   start=k == 0, stop=k == KD - 1)
            mm.then_inc(sem("tile_ready"), 1)
            queries_norm(1)

            for i in range(2):
                pe.wait_ge(sem("bonus_in"), i + 1)
                t = tile("bo", i, freed=("bonus", i + 1))
                pe.matmul(t, blk[:, :], tmp[:, 2 * i:2 * i + 2, :], start=True, stop=True) \
                  .then_inc(sem("tile_ready"), 1)

            def cmp_step():
                loaded(J_CMP)
                pe.wait_ge(sem("cmp_in"), 1)
                t = tile("cmp", freed=("cmp_hidden", 1))
                w = view(slot(J_CMP), 0, 2, CMP // 2, HD)
                for m in range(CMP // 2):
                    for kind in range(2):
                        mm = pe.matmul(t[64 * kind:64 * kind + 64, 0:2 * NCMP], w[:, kind, m, :],
                                       XC[:, kind, m, :, :], start=m == 0, stop=m == CMP // 2 - 1)
                mm.then_inc(sem("tile_ready"), 1)

            def cmpout_step():
                pe.wait_ge(sem("cmp_hidden"), 1)
                t = tile("kcmp", freed=("kcmp", 1))
                for g in range(NSA_G):
                    mm = pe.matmul(t[64 * g:64 * g + 64, 0:NCMP], cw2[0:HD, :], h1T[0:HD, g, :],
                                   start=True, stop=True)
                mm.then_inc(sem("tile_ready"), 1)
                t = tile("vcmp", freed=("vcmp", 1))
                for g in range(NSA_G):
                    mm = pe.matmul(t[0:NCMP, g * HD:(g + 1) * HD], h1T[HD:P, g, :], cw2[HD:P, :],
                                   start=True, stop=True)
                mm.then_inc(sem("tile_ready"), 1)
                pe.wait_ge(sem("kcmp_squares"), 1)
                t = tile("kcn", freed=("kcmp_rs", 1))
                pe.matmul(t[:, 0:NCMP], blk64[:, :], csq[:, 0:NCMP], start=True, stop=True) \
                  .then_inc(sem("tile_ready"), 1)

            def tok_step(kind):
                if kind == 0:
                    pe.wait_ge(sem("rwkv_ready"), 1)
                for tt in range(TT):
                    t = tile("tok", kind, tt, freed=("tok", TOKS.index(kind) * 2 + tt + 1))
                    for p in range(4):
                        src = AR[:, p, tt, 0, :] if kind == 0 else \
                            (bhT, khT, vT)[kind - 1][:, p, tt * P:(tt + 1) * P]
                        mm = pe.transpose(t[:, p * P:(p + 1) * P], src, ident[:, :])
                    mm.then_inc(sem("tile_ready"), 1)

            def parts_step(tt):
                for pp in range(2):
                    both = [tile("gm", tt, pp, q, freed=("gm_masked", 4 * tt + 2 * pp + q + 1))
                            for q in range(2)]
                    for n in range(2):
                        p = 2 * pp + n
                        for w, lhs in enumerate((bhT, khT)):
                            for c in range(2):
                                for q in range(2):
                                    r, now = slice(64 * q, 64 * q + 64), slice(64 * c, 64 * c + 64)
                                    o = both[q][now, 256 * n + 128 * w:256 * n + 128 * w + 128]
                                    at = tt * P + 64 * c
                                    mm = pe.matmul(o, lhs[r, p, at:at + 64], AR[r, p, tt, :, now],
                                                   start=True, stop=True)
                                    if n == 1 and w == 1 and c == 1:
                                        mm.then_inc(sem("tile_ready"), 1)

            def g3_step():
                both = [tile("g3", q, freed=("parts_masked", q + 1)) for q in range(2)]
                for tt in range(TT):
                    for p in range(4):
                        for c in range(2):
                            for q in range(2):
                                r, now = slice(64 * q, 64 * q + 64), slice(64 * c, 64 * c + 64)
                                at = tt * P + 64 * c
                                mm = pe.matmul(both[q][now, (4 * tt + p) * CH:(4 * tt + p + 1) * CH],
                                               AR[r, p, tt, 0, now], bhT[r, p, at:at + 64],
                                               start=True, stop=True)
                                if tt == 1 and p == 3 and c == 1:
                                    mm.then_inc(sem("tile_ready"), 1)

            def inv_step(s):
                name, kind, lhs, rhs, _ = INV[s]
                for q in range(2):
                    own, value = inv_done(name, q)
                    for need in NEEDS[name]:
                        own_need, at = inv_done(need, q)
                        pe.wait_ge(sem(own_need), at)
                    t = tile("inv", s, q, freed=(own, value))
                    for n in range(8):
                        m = 8 * q + n
                        for c in range(2):
                            r = slice(64 * c, 64 * c + 64)
                            moving = identc[r, :] if kind == "turn" else BUF[rhs][r, m, :]
                            mm = pe.matmul(t[r, n * CH:(n + 1) * CH], BUF[lhs][r, m, :], moving,
                                           start=True, stop=True)
                    mm.then_inc(sem("tile_ready"), 1)

            def qt_step():
                pe.wait_ge(sem("inv_added"), 2 * len(ADDS))
                both = [tile("qt", c, freed=("qt", c + 1)) for c in range(2)]
                for tt in range(TT):
                    for p in range(4):
                        for q in range(2):
                            for c in range(2):
                                r = slice(64 * c, 64 * c + 64)
                                mm = pe.matmul(both[c][64 * q:64 * q + 64, (4 * tt + p) * CH:(4 * tt + p + 1) * CH],
                                               tokA[r, tt, (2 * p + q) * HD:(2 * p + q + 1) * HD],
                                               PP[r, matrix(q, tt, p), :], start=True, stop=True)
                                if tt == 1 and p == 3 and q == 1:
                                    mm.then_inc(sem("tile_ready"), 1)

            def akv_step():
                for q in range(2):
                    t = tile("akv", q, freed=("akv", q + 1))
                    for n in range(8):
                        tt, p = n // 4, n % 4
                        for c in range(2):
                            r = slice(64 * c, 64 * c + 64)
                            mm = pe.matmul(t[r, n * CH:(n + 1) * CH], GM[r, 2, 8 * q + n, :],
                                           tokV[r, tt, (2 * p + q) * HD:(2 * p + q + 1) * HD],
                                           start=True, stop=True)
                    mm.then_inc(sem("tile_ready"), 1)

            def z_step():
                for q in range(2):
                    pe.wait_ge(sem("akv"), q + 1)
                    t = tile("z", q, freed=("z", q + 1))
                    for n in range(8):
                        for c in range(2):
                            r = slice(64 * c, 64 * c + 64)
                            mm = pe.matmul(t[r, n * CH:(n + 1) * CH], PP[r, 8 * q + n, :], AKV[r, 8 * q + n, :],
                                           start=True, stop=True)
                    mm.then_inc(sem("tile_ready"), 1)

            def chunk_step(c):
                tt, cc, rows = c // 2, c % 2, slice(64 * (c % 2), 64 * (c % 2) + 64)
                if c > 0:
                    pe.wait_ge(sem("state"), c)
                    pe.wait_ge(sem("qt"), 2)
                    both = [tile("u", c, q, freed=("u", 2 * c + q + 1)) for q in range(2)]
                    for p in range(4):
                        for q in range(2):
                            r = slice(64 * q, 64 * q + 64)
                            mm = pe.matmul(both[q][rows, p * HD:(p + 1) * HD], QT[r, cc, 4 * tt + p, :],
                                           SH[r, c, p, :], start=True, stop=True)
                            if p == 3:
                                mm.then_inc(sem("tile_ready"), 1)
                if c < 3:
                    t = tile("ds", c, freed=("state", c + 1))
                    for p in range(4):
                        for q in range(2):
                            cols = slice((2 * p + q) * HD, (2 * p + q + 1) * HD)
                            o = t[64 * q:64 * q + 64, p * HD:(p + 1) * HD]
                            if p == 0:
                                pe.wait_ge(sem("u"), 2 * c + q + 1)
                            pe.matmul(o, tokK[rows, tt, cols], tokV[rows, tt, cols], start=True, stop=False)
                            mm = pe.matmul(o, tokB[rows, tt, cols], U[rows, matrix(q, tt, p), :],
                                           start=False, stop=True)
                    mm.then_inc(sem("tile_ready"), 1)

            def y_step(tt):
                pe.wait_ge(sem("u"), 4 * tt + 4)
                both = [tile("y", tt, c, freed=("y", 2 * tt + c + 1)) for c in range(2)]
                for p in range(4):
                    for q in range(2):
                        m, cols = matrix(q, tt, p), slice((2 * p + q) * HD, (2 * p + q + 1) * HD)
                        for c in range(2):
                            r = slice(64 * c, 64 * c + 64)
                            pe.matmul(both[c][64 * q:64 * q + 64, p * CH:(p + 1) * CH], tokV[r, tt, cols],
                                      GM[r, 3, m, :], start=True, stop=False)
                        for c in range(2):
                            r = slice(64 * c, 64 * c + 64)
                            mm = pe.matmul(both[c][64 * q:64 * q + 64, p * CH:(p + 1) * CH], U[r, m, :],
                                           GM[r, 1, m, :], start=False, stop=True)
                            if p == 3 and q == 1:
                                mm.then_inc(sem("tile_ready"), 1)
                t = tile("ys", tt, freed=("y_state", tt + 1))
                for p in range(4):
                    for c in range(2):
                        for q in range(2):
                            r = slice(64 * q, 64 * q + 64)
                            mm = pe.matmul(t[r, p * P + 64 * c:p * P + 64 * c + 64], SH[r, 2 * tt + c, p, :],
                                           AR[r, p, tt, 1, 64 * c:64 * c + 64], start=True, stop=True)
                mm.then_inc(sem("tile_ready"), 1)

            def ymean_step(tt):
                pe.wait_ge(sem("y"), 2 * tt + 2)
                t = tile("ymean", tt, freed=("y_centred", tt + 1))
                pe.matmul(t, blk64[:, :], Y[tt], start=True, stop=True).then_inc(sem("tile_ready"), 1)

            def yvar_step(tt):
                pe.wait_ge(sem("y_squared"), tt + 1)
                t = tile("yvar", tt, freed=("y_rs", tt + 1))
                pe.matmul(t, blk64[:, :], SQ, start=True, stop=True).then_inc(sem("tile_ready"), 1)

            def xk_step(j):
                if j == 0:
                    pe.wait_ge(sem("memT"), 4)
                loaded(J_XK + j)
                t = tile("xk", j, freed=("kx_taken", j + 1))
                project(t, wjob(J_XK + j), memT).then_inc(sem("tile_ready"), 1)

            def xkn_step(j):
                xnorm("xk", j, "kx_squares", "kx_rs")

            def xnorm(name, j, squares, freed):
                pe.wait_ge(sem(squares), j + 1)
                t = tile(name + "n", j, freed=(freed, j + 1))
                pe.matmul(t[:, 0:T], o256[:, :], xsq[:, 0, :], start=True, stop=False)
                pe.matmul(t[:, 0:T], o256[:, :], xsq[:, 1, :], start=False, stop=True) \
                  .then_inc(sem("tile_ready"), 1)

            def rows_job(t, j, lhs, before=None):
                w = wjob(j)
                for tt in range(TT):
                    if before is not None:
                        before(tt)
                    for k in range(KD):
                        mm = pe.matmul(t[:, tt * T:(tt + 1) * T], lhs(k, tt), w[:, k, :],
                                       start=k == 0, stop=k == KD - 1)
                return mm

            def xv_step(j):
                loaded(J_XV + j)
                t = tile("xv", j, freed=("vx", j + 1))
                rows_job(t, J_XV + j, lambda k, tt: memT[:, k, tt * P:(tt + 1) * P]) \
                    .then_inc(sem("tile_ready"), 1)

            def cmpsc_step():
                pe.wait_ge(sem("queries_normed"), 2)
                pe.wait_ge(sem("kcmp"), 1)
                for tt in range(TT):
                    both = [tile("cmpsc", tt, g, freed=("cmp_scores", 2 * tt + g + 1)) for g in range(NSA_G)]
                    for i in range(4):
                        for g in range(NSA_G):
                            r = slice(64 * g, 64 * g + 64)
                            mm = pe.matmul(both[g][:, i * 16:i * 16 + NCMP], qT[r, i, tt * P:(tt + 1) * P],
                                           kcmpT[r, 0:NCMP], start=True, stop=True)
                            if i == 3:
                                mm.then_inc(sem("tile_ready"), 1)

            def score_step(u):
                tt, j = units[u]
                nk = P * (tt + 1)
                if u == 0:
                    pe.wait_ge(sem("keys_normed"), 2)
                both = [tile("score", u, g, freed=("scores", 2 * u + g + 1)) for g in range(NSA_G)]
                for b, keys in enumerate((ksT, kwT)):
                    for g in range(NSA_G):
                        r = slice(64 * g, 64 * g + 64)
                        mm = pe.matmul(both[g][:, b * T:b * T + nk], qT[r, j, tt * P:(tt + 1) * P],
                                       keys[r, 0:nk], start=True, stop=True)
                        if b == 1:
                            mm.then_inc(sem("tile_ready"), 1)

            def turnp_step(u):
                tt, j = units[u]
                if j == 0:
                    pe.wait_ge(sem("cmp_probs"), tt + 1)
                t = tile("pc", u, freed=("ptc", u + 1))
                for g in range(NSA_G):
                    mm = pe.transpose(t[0:NCMP, g * P:(g + 1) * P], sc_c[:, tt, 4 * g + j, 0:NCMP], ident[:, :])
                mm.then_inc(sem("tile_ready"), 1)
                pe.wait_ge(sem("probs"), u + 1)
                for g in range(NSA_G):
                    t = tile("pt", u, g, freed=("pt", 2 * u + g + 1))
                    for b in range(2):
                        for kt in range(tt + 1):
                            n = b * (tt + 1) + kt
                            mm = pe.transpose(t[:, n * P:(n + 1) * P],
                                              S2[:, u % 2, 2 * g + b, kt * P:(kt + 1) * P], ident[:, :])
                    mm.then_inc(sem("tile_ready"), 1)

            def pv_step(u):
                tt, j = units[u]
                if u == 0:
                    pe.wait_ge(sem("vcmp"), 1)
                if j == 0:
                    out_tile[0] = tile("o", tt, freed=("on", tt + 1), bank=7)
                pe.wait_ge(sem("ptc"), u + 1)
                pe.wait_ge(sem("pt"), 2 * u + 2)
                for g in range(NSA_G):
                    pe.matmul(out_tile[0][64 * g:64 * g + 64, j * P:(j + 1) * P], vcmp[0:NCMP, g, :],
                              ptc[0:NCMP, u % 2, g, :], start=True, stop=False)
                for b, values in enumerate((vs, vw)):
                    for kt in range(tt + 1):
                        for g in range(NSA_G):
                            mm = pe.matmul(out_tile[0][64 * g:64 * g + 64, j * P:(j + 1) * P],
                                           values[:, kt, g * HD:(g + 1) * HD],
                                           PT[:, u % 2, g, b * (tt + 1) + kt, :],
                                           start=False, stop=b == 1 and kt == tt)
                mm.then_inc(sem("pv_done"), 1)

            out_tile = [None]
            steps = {"cmp": cmp_step, "cmpout": cmpout_step, "tok": tok_step,
                     "parts": parts_step, "g3": g3_step, "inv": inv_step, "qt": qt_step, "akv": akv_step,
                     "z": z_step, "chunk": chunk_step, "y": y_step, "ymean": ymean_step, "yvar": yvar_step, "xk": xk_step, "xkn": xkn_step,
                     "xv": xv_step, "cmpsc": cmpsc_step, "score": score_step, "turnp": turnp_step,
                     "pv": pv_step}
            for step, *args in order:
                steps[step](*args)

            def turn_block(which, j):
                pe.wait_ge(sem("h_" + which), j + 1)
                t = tile("turn", which, j, freed=("turned_" + which, j + 1))
                for k in range(2):
                    for tt in range(TT):
                        mm = pe.transpose(t[:, k * T + tt * P:k * T + (tt + 1) * P],
                                          h[:, tt, (2 * j + k) * P:(2 * j + k + 1) * P], ident[:, :])
                mm.then_inc(sem("tile_ready"), 1)

            def mixed_rows(tt):
                pe.wait_ge(sem("on"), tt + 1)
                pe.wait_ge(sem("rwkv_out"), tt + 1)

            for j in range(4):
                loaded(J_OUT + j)
                t = tile("wout", j, freed=("h_mixed", j + 1))
                rows_job(t, J_OUT + j, lambda k, tt: (onT if k < 4 else orT)[:, k % 4, tt * P:(tt + 1) * P],
                         before=mixed_rows if j == 0 else None) \
                    .then_inc(sem("tile_ready"), 1)
                if j:
                    turn_block("mixed", j - 1)
            turn_block("mixed", 3)
            pe.wait_ge(sem("turned_mixed"), 4)

            def xproject(j):
                loaded(J_XQ + j)
                t = tile("xq", j, freed=("qx_scaled", j + 1))
                project(t, wjob(J_XQ + j), hnT).then_inc(sem("tile_ready"), 1)
                if j == 0:
                    pe.wait_ge(sem("diag"), 2)
                    t = tile("rsB", freed=("rsB", 1))
                    pe.matmul(t[:, 0:T], ones[:, :], diag[:, :, :], start=True, stop=True) \
                      .then_inc(sem("tile_ready"), 1)

            def xscore(n):
                tt, i = n % 2, n // 2
                pe.wait_ge(sem("qx_normed"), i + 1)
                t = tile("xs", n, freed=("xscores", n + 1))
                for c in range(2):
                    mm = pe.matmul(t[:, 0:MEM], qxT[:, 2 * i + c, tt * P:(tt + 1) * P], kxT[:, 2 * i + c, :],
                                   start=c == 0, stop=c == 1)
                mm.then_inc(sem("tile_ready"), 1)

            def xturn(n):
                pe.wait_ge(sem("xprobs"), n + 1)
                t = tile("xp", n, freed=("xpt", n + 1))
                for m in range(2):
                    mm = pe.transpose(t[:, m * P:(m + 1) * P], xs[:, n % 2, m * P:(m + 1) * P], ident[:, :])
                mm.then_inc(sem("tile_ready"), 1)

            def xpv(n):
                tt, i = n % 2, n // 2
                pe.wait_ge(sem("xpt"), n + 1)
                t = tile("xo", n, freed=("ox", n + 1))
                for c in range(2):
                    for m in range(2):
                        mm = pe.matmul(t[:, c * P:(c + 1) * P], vxm[:, m, i * X_HD + c * P:i * X_HD + (c + 1) * P],
                                       xpt[:, n % 2, m, :], start=m == 0, stop=m == 1)
                mm.then_inc(sem("tile_ready"), 1)

            for step, n in CROSS:
                {"project": xproject, "norm": lambda j: xnorm("xq", j, "qx_squares", "qx_rs"),
                 "score": xscore, "turn": xturn, "pv": xpv}[step](n)
            pe.wait_ge(sem("ox"), 8)
            logits = psum[:, 7, :]

            def router_step(j):
                pe.wait_ge(sem("turned_crossed"), j + 1)
                for tt in range(TT):
                    for k in (2 * j, 2 * j + 1):
                        mm = pe.matmul(logits[:, tt * NE:(tt + 1) * NE], hnT[:, k, tt * P:(tt + 1) * P], rw[:, k, :],
                                       start=False, stop=k == KD - 1 and tt == 1)
                if j == 3:
                    mm.then_inc(sem("logits_made"), 1)

            for j in range(4):
                loaded(J_XO + j)
                t = tile("xout", j, freed=("h_crossed", j + 1))
                rows_job(t, J_XO + j, lambda k, tt: oxT[:, k, tt * P:(tt + 1) * P]).then_inc(sem("tile_ready"), 1)
                if j == 0:
                    pe.wait_ge(sem("small_in"), 16 * 7)
                    pe.matmul(logits[:, 0:3 * NE], ones[0:1, :], rb[0:1, :], start=True, stop=False)
                if j >= 1:
                    turn_block("crossed", j - 1)
                if j >= 2:
                    router_step(j - 2)
            turn_block("crossed", 3)
            router_step(2)
            router_step(3)
            pe.wait_ge(sem("chosen"), 1)
            t = tile("places", freed=("places", 1))
            pe.matmul(t[:, 0:NE], before[:, :], chosen[:, 0, :], start=True, stop=True)
            pe.matmul(t[:, NE:2 * NE], ones[:, :], chosen[:, 0, :], start=True, stop=False)
            pe.matmul(t[:, NE:2 * NE], before[:, :], chosen[:, 1, :], start=False, stop=True)
            pe.matmul(t[:, 2 * NE:3 * NE], ones[:, :], chosen[:, 0, :], start=True, stop=False)
            pe.matmul(t[:, 2 * NE:3 * NE], ones[:, :], chosen[:, 1, :], start=False, stop=True) \
              .then_inc(sem("tile_ready"), 1)

            def gather():
                for k in range(KD):
                    for tt in range(TT):
                        mm = pe.matmul(psum[:, 4, k * SLOTS:(k + 1) * SLOTS], h[:, tt, k * P:(k + 1) * P],
                                       sel[:, tt, :], start=tt == 0, stop=tt == 1)
                mm.then_inc(sem("gathered"), 1)

            def item(i, first=False, second=False):
                pe.wait_ge(sem("slots_in"), i + 1)
                pe.wait_ge(sem("hot"), i + 1)
                pe.wait_ge(sem("swiglu"), i * 2 + 1)
                for n in range(2):
                    for half in range(2):
                        o = psum[64 * half:64 * half + 64, 4 + n, :]
                        c = half * DE + n * 512
                        mm = pe.matmul(o, hot[0:NE, :], bias[0:NE, c:c + 512], start=True, stop=False)
                    for kq in range(2):
                        for half in range(2):
                            c = 4 * n + 2 * kq + half
                            if second and n == 0:
                                pe.wait_ge(sem(f"ahead_in_{c}"), 16)
                            else:
                                pe.wait_ge(sem(f"w1_in_{c}"), (i + 1) * 16 if first or n else i * 16)
                        for k in range(4 * kq, 4 * kq + 4):
                            for half in range(2):
                                o = psum[64 * half:64 * half + 64, 4 + n, :]
                                c = half * DE + n * 512
                                w = ahead[2 * kq + half][:, k % 4, :] if second and n == 0 else w1[:, k, c:c + 512]
                                mm = pe.matmul(o, xgT[:, k, :], w,
                                               start=False, stop=k == KD - 1)
                                if k % 4 == 3:
                                    mm.then_inc(sem("piece_used"), 1)
                pe.wait_ge(sem("gated"), i + 1)
                pe.wait_ge(sem("y_out"), i + 1)
                for tt in range(TT):
                    mm = pe.transpose(psum[:, 7, tt * P:(tt + 1) * P], selg[:, tt, :], ident[:, :])
                mm.then_inc(sem("gated_turned"), 1)
                pe.wait_ge(sem("selected"), i + 2)
                pe.wait_ge(sem("swiglu"), i * 2 + 2)
                gather()
                for n in range(2):
                    pe.wait_ge(sem("swiglu"), i * 2 + 2 + n)
                    if n == 0:
                        pe.wait_ge(sem("act_out"), i * 2 + 1)
                    for m in (2 * n, 2 * n + 1):
                        mm = pe.transpose(psum[:, 6, m * P:(m + 1) * P], actv[:, m * P:(m + 1) * P], ident[:, :])
                    mm.then_inc(sem("act_turned"), 1)
                    if n == 0:
                        pe.wait_ge(sem("selgT"), i + 1)
                        for o2 in range(2):
                            pe.matmul(psum[64 * o2:64 * o2 + 64, 7, :], hot[0:NE, :],
                                      bias[0:NE, 2 * DE + o2 * 512:2 * DE + (o2 + 1) * 512],
                                      start=True, stop=False)
                    pe.wait_ge(sem("act_out"), i * 2 + 2 + n)
                    for q in range(2):
                        pe.wait_ge(sem(f"w2_in_{2 * n + q}"), (i + 1) * 16)
                        for m in (2 * n, 2 * n + 1):
                            for o2 in range(2):
                                mm = pe.matmul(psum[64 * o2:64 * o2 + 64, 7, :],
                                               actT[:, m, 64 * q:64 * q + 64],
                                               w2[:, 4 * q + m, o2 * 512:(o2 + 1) * 512],
                                               start=False, stop=(n == 1 and q == 1 and m == 3))
                        mm.then_inc(sem("piece_used"), 1)
                pe.wait_ge(sem("y_out"), i + 2)
                for tt in range(TT):
                    for o2 in range(2):
                        r = slice(64 * o2, 64 * o2 + 64)
                        mm = pe.matmul(psum[:, 2 * tt + o2, :], selgT[r, tt, :], yb[r, :],
                                       start=first, stop=False, skip_group_check=True)
                mm.then_inc(sem("scattered"), 1)

            pe.wait_ge(sem("selected"), 1)
            pe.wait_ge(sem("bias_in"), 32)
            gather()
            item(0, first=True)
            item(1, second=True)
            pe.wait_ge(sem("tabled"), 1)
            n_items = pe.value_load(tabi[0:1, 0:1], min_val=NE, max_val=ITEMS)
            with pe.Fori(2, n_items) as i:
                item(i)


        def unit_stat(kind, u):
            at = 48 + 8 * kind + 4 * (u % 2)
            return st[:, at:at + 4]

        @block.vector
        def _(dve):
            counts = {}

            def link(ins, name="vector_step"):
                counts[name] = counts.get(name, 0) + 1
                ins.then_inc(sem(name), 1)
                dve.wait_ge(sem(name), counts[name])

            def stt(o, x, s, y, op0, op1):
                return dve.scalar_tensor_tensor(out=o, in0=x, scalar=s, in1=y, op0=op0, op1=op1)

            def norm_rows(which, src, dst):
                n = 2 * NORMS.index(which)
                for tt in range(TT):
                    dve.wait_ge(sem("row_rs"), n // 2 + 1)
                    c = st[:, n + tt:n + tt + 1]
                    link(dve.tensor_scalar(dst[:, tt, :], src[:, tt, :], c, None, ALU.mult), "rows_normed")

            def turned(which, dst, gain, name):
                for tt in range(TT):
                    for half in range(2):
                        b = ready(dve, "turn", which, tt, half)
                        g = vec(gain, 4 * half, 4).unsqueeze(2)
                        link(dve.tensor_tensor(dst[:, 4 * half:4 * half + 4, tt * P:(tt + 1) * P],
                                               view(psum[:, b, :], 0, 4, P), bcast(g, P, 4, P), ALU.mult), name)

            hn3 = view(hn, 0, TT, D)
            norm_rows("x", h, hn3)
            b = ready(dve, "gain")
            link(dve.tensor_copy(vecs[:, 0:8], psum[:, b, 0:8]), "gain")
            turned("x", hnT, "norm_mix_g", "xT")
            norm_rows("mem", memx, memx)
            link(dve.memset(shifted[:, :, :, 0:1], 0.0), "shift_zeroed")
            b = ready(dve, "vecs")
            link(dve.tensor_copy(vecs[:, 8:NV], psum[:, b, 8:NV]))
            link(dve.tensor_copy(peT[:, :, :], view(psum[:, b, P:P + CMP], 0, 2, CMP // 2)), "vecs")
            link(dve.tensor_scalar(omka[:, :], vec("rwkv_k_a", 0, 4), -1.0, 1.0, ALU.mult, ALU.add))
            turned("mem", memT, "norm_mem_g", "memT")

            MIXED = {J_LORA: (12, lambda g: (wdad, gd)[g])}
            for jj in range(2):
                MIXED[J_K + jj] = (4 + 2 * jj, lambda g, jj=jj: kT[:, 2 * jj + g, :])
                MIXED[J_R + jj] = (2 * jj, lambda g, jj=jj: rT[:, 2 * jj + g, :])
                MIXED[J_V + jj] = (8 + 2 * jj, lambda g, jj=jj: vT[:, 2 * jj + g, :])

            def mix(j):
                at, dst = MIXED[j]
                dve.wait_ge(sem("differenced"), j + 1)
                stt(dst(0), diff[:, j % 2, 0, :], vec("rwkv_mu", at), shifted[:, j % 2, 0, 1:T + 1],
                    ALU.mult, ALU.add)
                link(stt(dst(1), diff[:, j % 2, 1, :], vec("rwkv_mu", at + 1), shifted[:, j % 2, 1, 1:T + 1],
                         ALU.mult, ALU.add), "mixed")

            mix(J_LORA)
            mix(J_K)
            mix(J_K + 1)
            for i in range(2):
                for p in (2 * i, 2 * i + 1):
                    link(dve.tensor_scalar(kkr[:, p, :], kT[:, p, :], vec("rwkv_k_k", p), None, ALU.mult),
                         "kkr" if p % 2 else "vector_step")
            mix(J_R)
            mix(J_R + 1)
            dve.wait_ge(sem("zw"), 2)
            for p in range(4):
                link(dve.tensor_tensor_scan(cum[:, p, :], mreset[:, :], sig[:, p, :], 0.0, ALU.mult, ALU.add))
            link(dve.tensor_tensor(tmp[:, :, :], cum[:, :, :], sig[:, :, :], ALU.subtract), "cum")
            dve.wait_ge(sem("az"), 2)
            for p in range(4):
                link(dve.tensor_scalar(k2[:, p, :], aT[:, p, :], vec("rwkv_k_a", p), omka[:, p:p + 1],
                                       ALU.mult, ALU.add))
            link(dve.tensor_tensor(k2[:, :, :], k2[:, :, :], kT[:, :, :], ALU.mult))
            mix(J_V)
            mix(J_V + 1)
            dve.wait_ge(sem("decays"), 3)
            for i in range(2):
                for p in (2 * i, 2 * i + 1):
                    link(stt(tmp[:, p, :], rT[:, p, :], vec("rwkv_r_k", p), k2[:, p, :], ALU.mult, ALU.mult),
                         "bonus_in" if p % 2 else "vector_step")
            for i in range(2):
                b = ready(dve, "kks", i)
                link(dve.tensor_scalar(kk[:, 2 * i:2 * i + 2, :], view(psum[:, b, :], 0, 2, T), 1e-24, None,
                                       ALU.max), "key_norms")
            dve.wait_ge(sem("key_roots"), 2)
            link(dve.reciprocal(kk[:, :, :], kk[:, :, :]))
            link(dve.tensor_tensor(kk[:, :, :], kk[:, :, :], kkr[:, :, :], ALU.mult))

            def halves(x):
                return x.rearrange("p a (b c) -> p a b c", b=2)

            link(stt(AR[:, :, :, 0, :], halves(kk), -1.0, halves(Wp), ALU.mult, ALU.mult))
            link(dve.tensor_tensor(AR[:, :, :, 1, :], halves(rT), halves(W), ALU.mult))
            link(dve.tensor_tensor(bhT[:, :, :], kk[:, :, :], aT[:, :, :], ALU.mult))
            link(dve.tensor_tensor(bhT[:, :, :], bhT[:, :, :], Wi[:, :, :], ALU.mult))
            link(dve.tensor_copy(wend[:, :, :], W.rearrange("p a (c t) -> p a c t", c=4)[:, :, :, CH - 1]))
            link(dve.tensor_tensor(khT[:, :, :], k2[:, :, :], Wi[:, :, :], ALU.mult), "rwkv_ready")

            for n in range(2):
                dve.wait_ge(sem("nsa_rs"), n + 1)
                link(dve.reciprocal(nrs[:, n, :], nrs[:, n, :]))
                link(stt((ksT, kwT)[n], (ksT, kwT)[n], vec(("k_slc_norm_g", "k_win_norm_g")[n]), nrs[:, n, :],
                         ALU.mult, ALU.mult), "keys_normed")
            for n in range(2):
                dve.wait_ge(sem("nsa_rs"), n + 3)
                link(dve.reciprocal(nrs[:, :, :], nrs[:, :, :]))
                for j in range(2):
                    link(stt(qT[:, 2 * n + j, :], qT[:, 2 * n + j, :], vec("q_norm_g"), nrs[:, j, :],
                             ALU.mult, ALU.mult), "queries_normed" if j else "vector_step")
            for i in range(2):
                b = ready(dve, "bo", i)
                link(dve.tensor_tensor(bonus[:, 2 * i:2 * i + 2, :], view(psum[:, b, :], 0, 2, T),
                                       vT[:, 2 * i:2 * i + 2, :], ALU.mult), "bonus")

            link(dve.memset(SH[:, 0, :, :], 0.0), "state_zeroed")

            def cmp_step():
                dve.wait_ge(sem("kc_copied"), 1)
                half = STRIDE // 2
                for kind in range(2):
                    kc = kcT[:, 2 * kind:2 * kind + 2, :].rearrange("p g (c m) -> p m g c", m=half)
                    for l1 in range(2):
                        pos = peT[:, kind, half * l1:half * (l1 + 1)].unsqueeze(2)
                        for g in range(NSA_G):
                            link(dve.tensor_tensor(XC[:, kind, half * l1:half * (l1 + 1), g, :],
                                                   kc[:, :, g, l1:l1 + NCMP], bcast(pos, P, half, NCMP), ALU.add),
                                 "cmp_in" if kind and l1 and g else "vector_step")

            def cmpout_step():
                b = ready(dve, "cmp")
                dve.wait_ge(sem("cmp_exped"), 1)
                link(dve.tensor_scalar(csq[:, :], csq[:, :], 1.0, None, ALU.add))
                link(dve.reciprocal(csq[:, :], csq[:, :]))
                link(dve.tensor_tensor(h1T[:, :, :], view(psum[:, b, 0:2 * NCMP], 0, NSA_G, NCMP),
                                       view(csq, 0, NSA_G, NCMP), ALU.mult), "cmp_hidden")
                dve.wait_ge(sem("kcmp_rs"), 1)
                b = tiles["kcmp",][0]
                link(stt(kcmpT[:, 0:NCMP], psum[:, b, 0:NCMP], vec("k_cmp_norm_g"), crs[:, 0:NCMP],
                         ALU.mult, ALU.mult), "kcmp")

            def parts_step(tt):
                dve.wait_ge(sem("masks"), 1)
                gm5 = GM[:, :, :, :].rearrange("p a (q t n) c -> p q t n a c", q=2, t=TT)
                for pp in range(2):
                    for q in range(2):
                        b = ready(dve, "gm", tt, pp, q)
                        for n in range(2):
                            ins = dve.tensor_tensor(gm5[:, q, tt, 2 * pp + n],
                                                    view(psum[:, b, 256 * n:256 * n + 256], 0, 4, CH),
                                                    masks4[:, :, :], ALU.mult)
                            link(ins, "gm_masked" if n else "vector_step")

            def g3_step():
                for q in range(2):
                    b = ready(dve, "g3", q)
                    for k in range(3):
                        link(dve.tensor_tensor(DT3[:, k, 8 * q:8 * q + 8, :], view(psum[:, b, :], 0, 8, CH),
                                               bcast(masks3[:, k, :].unsqueeze(1), P, 8, CH), ALU.mult),
                             "parts_masked" if k == 2 else "vector_step")
                    link(dve.tensor_tensor(PP[:, 8 * q:8 * q + 8, :], GM[:, 0, 8 * q:8 * q + 8, :],
                                           bcast(identc[:, :].unsqueeze(1), P, 8, CH), ALU.add), "p1_made")

            def inv_step(s):
                if INV[s][1] != "add":
                    return
                for q in range(2):
                    b = ready(dve, "inv", s, q)
                    part = PP[:, 8 * q:8 * q + 8, :]
                    link(dve.tensor_tensor(part, view(psum[:, b, :], 0, 8, CH), part, ALU.add), "inv_added")

            def akv_step():
                for q in range(2):
                    b = ready(dve, "akv", q)
                    link(dve.tensor_copy(AKV[:, 8 * q:8 * q + 8, :], view(psum[:, b, :], 0, 8, CH)), "akv")

            def chunk_step(c):
                tt, rows = c // 2, slice(64 * (c % 2), 64 * (c % 2) + 64)
                dve.wait_ge(sem("z"), 2)
                for q in range(2):
                    at = slice(8 * q + 4 * tt, 8 * q + 4 * tt + 4)
                    if c == 0:
                        link(dve.tensor_copy(U[rows, at, :], Z[rows, at, :]), "u")
                    else:
                        b = ready(dve, "u", c, q)
                        link(dve.tensor_tensor(U[rows, at, :], view(psum[rows, b, 0:256], 0, 4, HD),
                                               Z[rows, at, :], ALU.add), "u")
                if c < 3:
                    b = ready(dve, "ds", c)
                    grown = view(psum[:, b, 0:256], 0, 4, HD)
                    if c > 0:
                        link(dve.tensor_tensor(AKV[:, 0:4, :], grown, SH[:, c, :, :], ALU.add))
                        grown = AKV[:, 0:4, :]
                    link(dve.tensor_tensor(SH[:, c + 1, :, :], grown, bcast(wend[:, :, c:c + 1], P, 4, HD),
                                           ALU.mult), "state")

            def y_step(tt):
                y4 = Y[tt].rearrange("p (a c t) -> p c a t", a=4, c=2)
                dve.wait_ge(sem("y_state"), tt + 1)
                for c in range(2):
                    b = ready(dve, "y", tt, c)
                    link(dve.tensor_tensor(y4[:, c], view(psum[:, b, 0:256], 0, 4, CH), y4[:, c], ALU.add), "y")

            def ymean_step(tt):
                b = ready(dve, "ymean", tt)
                link(dve.tensor_tensor(YC[tt], Y[tt], psum[:, b, :], ALU.subtract), "y_centred")

            def yvar_step(tt):
                dve.wait_ge(sem("y_rs"), tt + 1)
                link(dve.tensor_tensor(YC[tt], YC[tt], Y[tt], ALU.mult))
                for p in range(4):
                    c = slice(p * P, (p + 1) * P)
                    link(dve.tensor_scalar(YC[tt][:, c], YC[tt][:, c], vec("rwkv_ln_w", p), vec("rwkv_ln_b", p),
                                           ALU.mult, ALU.add))
                yc = view(YC[tt], 0, 4, P)
                now = slice(tt * P, (tt + 1) * P)
                link(dve.tensor_tensor(yc, yc, bonus[:, :, now], ALU.add))
                link(dve.tensor_tensor(orT[:, :, now], yc, gT[:, :, now], ALU.mult), "rwkv_out")

            def xkn_step(j):
                xnormed("xk", j, "kx_squares", "kx_rs", kxT, "xk_norm_g", "kx_normed")

            def xnormed(name, j, squares, rs, dst, gain, done):
                dve.wait_ge(sem(rs), j + 1)
                link(dve.reciprocal(xrs[:, :], xrs[:, :]))
                for c in range(2):
                    link(stt(dst[:, 2 * j + c, :], dst[:, 2 * j + c, :], vec(gain, c), xrs[:, :],
                             ALU.mult, ALU.mult), done if c else "vector_step")

            def cmpsc_step():
                dve.wait_ge(sem("gates_exp"), 1)
                link(dve.tensor_scalar(gates[:, :, :], gates[:, :, :], 1.0, None, ALU.add))
                link(dve.reciprocal(gates[:, :, :], gates[:, :, :]), "gates")
                dve.wait_ge(sem("cmp_bias"), 1)
                for tt in range(TT):
                    s = sc_c[:, tt, :, 0:NCMP]
                    for g in range(NSA_G):
                        b = ready(dve, "cmpsc", tt, g)
                        part = sc_c[:, tt, 4 * g:4 * g + 4, 0:NCMP]
                        link(dve.tensor_tensor(part, view(psum[:, b, :], 0, 4, 16)[:, :, 0:NCMP], part, ALU.add),
                             "cmp_scores")
                    link(dve.reduce_max(st[:, 8:16], s, AX))
                    link(dve.tensor_tensor(s, s, bcast(st[:, 8:16].unsqueeze(2), P, 8, NCMP), ALU.subtract),
                         "cmp_shifted")
                    dve.wait_ge(sem("cmp_exp"), tt + 1)
                    link(dve.reduce_sum(st[:, 16:24], s, AX))
                    link(dve.reciprocal(st[:, 16:24], st[:, 16:24]))
                    link(dve.tensor_tensor(st[:, 16:24], gates[:, tt, 0:24:3], st[:, 16:24], ALU.mult))
                    link(dve.tensor_tensor(s, s, bcast(maskc[:, tt, 0:NCMP].unsqueeze(1), P, 8, NCMP), ALU.mult))
                    link(dve.tensor_tensor(s, s, bcast(st[:, 16:24].unsqueeze(2), P, 8, NCMP), ALU.mult),
                         "cmp_probs")

            def score_step(u):
                tt, j = units[u]
                nk = P * (tt + 1)
                if u >= 2:
                    ready(dve, "pt", u - 2, 1)
                d = dist[:, T - nk:T].unsqueeze(1)
                for g in range(NSA_G):
                    b = ready(dve, "score", u, g)
                    link(stt(S2[:, u % 2, 2 * g:2 * g + 2, 0:nk], bcast(d, P, 2, nk), 8.0 * SLOPE[4 * g + j],
                             view(psum[:, b, :], 0, 2, T)[:, :, 0:nk], ALU.mult, ALU.add), "scores")
                m = unit_stat(0, u)
                link(dve.reduce_max(m, S2[:, u % 2, :, 0:nk], AX))
                link(dve.tensor_scalar(unit_stat(1, u), m, -0.125, None, ALU.mult), "score_max")

            def turnp_step(u):
                tt, j = units[u]
                dve.wait_ge(sem("exped"), u + 1)
                if u >= 2:
                    dve.wait_ge(sem("probs"), u - 1)
                c = unit_stat(3, u)
                link(dve.reciprocal(c, unit_stat(2, u)))
                g4 = gates[:, tt, :].rearrange("p (g j b) -> p j g b", g=2, j=4)
                link(dve.tensor_tensor(view(c, 0, 2, 2), g4[:, j, :, 1:3], view(c, 0, 2, 2), ALU.mult), "coef")

            steps = {"cmp": cmp_step, "cmpout": cmpout_step, "y": y_step,
                     "parts": parts_step, "g3": g3_step, "inv": inv_step, "akv": akv_step, "chunk": chunk_step,
                     "ymean": ymean_step, "yvar": yvar_step, "xkn": xkn_step, "cmpsc": cmpsc_step, "score": score_step,
                     "turnp": turnp_step}
            for step, *args in order:
                if step in steps:
                    steps[step](*args)

            def residual(name, which, gain):
                for j in range(5):
                    if j < 4:
                        b = ready(dve, name, j)
                        cols = h[:, :, j * T:(j + 1) * T]
                        link(dve.tensor_tensor(cols, view(psum[:, b, :], 0, 2, T), cols, ALU.add), "h_" + which)
                    if j:
                        b = ready(dve, "turn", which, j - 1)
                        g = vec(gain, 2 * (j - 1), 2).unsqueeze(2)
                        link(dve.tensor_tensor(hnT[:, 2 * (j - 1):2 * j, :], view(psum[:, b, :], 0, 2, T),
                                               bcast(g, P, 2, T), ALU.mult), "turned_" + which)

            def roots(which):
                n = ("mixed", "crossed").index(which)
                dve.wait_ge(sem("part_squares"), 8 * (n + 1))
                link(dve.reduce_sum(st[:, 4 + 2 * n:6 + 2 * n], psq[:, :, :], AX), "squares_summed")
                dve.wait_ge(sem("token_rs"), n + 1)

            residual("wout", "mixed", "norm_x_g")
            roots("mixed")
            for tt in range(TT):
                link(dve.tensor_scalar(diag[:, tt, :], ident[:, :], st[:, 4 + tt:5 + tt], None, ALU.mult), "diag")
            for step, n in CROSS:
                if step == "project":
                    b = ready(dve, "xq", n)
                    dve.wait_ge(sem("rsB"), 1)
                    link(dve.tensor_tensor(qxT[:, 2 * n:2 * n + 2, :], view(psum[:, b, :], 0, 2, T),
                                           bcast(rsB.unsqueeze(1), P, 2, T), ALU.mult), "qx_scaled")
                if step == "norm":
                    dve.wait_ge(sem("qx_rs"), n + 1)
                    for c in range(2):
                        o = qxT[:, 2 * n + c, :]
                        link(stt(o, o, vec("xq_norm_g", c), xrs[:, :], ALU.mult, ALU.mult),
                             "qx_normed" if c else "vector_step")
                if step == "score":
                    b = ready(dve, "xs", n)
                    link(dve.reduce_max(st[:, 40 + n % 2:41 + n % 2], psum[:, b, 0:MEM], AX))
                    link(dve.tensor_scalar(st[:, 42 + n % 2:43 + n % 2], st[:, 40 + n % 2:41 + n % 2],
                                           -float(X_HD) ** -0.5, None, ALU.mult), "xmax")
                if step == "turn":
                    q = n % 2
                    dve.wait_ge(sem("xscores"), n + 1)
                    link(dve.reciprocal(st[:, 46 + q:47 + q], st[:, 44 + q:45 + q]))
                    link(dve.tensor_scalar(xs[:, q, :], xs[:, q, :], st[:, 46 + q:47 + q], None, ALU.mult), "xprobs")
            link(dve.memset(rank[:, :, :], -1.0))
            link(dve.memset(gate[:, :, :], 0.0))
            link(dve.memset(of_expert[:, :], 0.0))
            link(dve.tensor_copy(of_expert[:, 0:NE], ident[:, 0:NE]))
            residual("xout", "crossed", "norm_ffn_g")
            roots("crossed")

            def choose(i):
                for tt in range(TT):
                    ins = dve.tensor_scalar(sel[:, tt, :], iotas[:, 0:SLOTS], rank[:, tt, bass.ds(i, 1)],
                                            st[:, 6 + tt:7 + tt], ALU.is_equal, ALU.mult)
                ins.then_inc(sem("selected"), 1)

            def wide(x):
                return bcast(x.unsqueeze(2), P, TT, NE)

            dve.wait_ge(sem("logits_made"), 1)
            link(dve.tensor_copy(rbb[:, :], psum[:, 7, 2 * NE:3 * NE]))
            for tt in range(TT):
                link(stt(lw[:, tt, :], psum[:, 7, tt * NE:(tt + 1) * NE], st[:, 6 + tt:7 + tt], rbb[:, :],
                         ALU.mult, ALU.add))
            for tt in range(TT):
                link(dve.max(best[:, tt, :], lw[:, tt, :]))
            fourth = bcast(best[:, :, TOPK - 1:TOPK], P, TT, NE)
            link(dve.tensor_tensor(pick, lw, fourth, ALU.is_gt))
            link(dve.tensor_tensor(key, lw, fourth, ALU.is_equal))
            link(dve.reduce_sum(top, pick, AX))
            for tt in range(TT):
                link(dve.tensor_tensor_scan(gsm[:, tt, :], ones[:, 0:NE], key[:, tt, :], 0.0, ALU.mult, ALU.add))
            link(dve.tensor_tensor(gsm, gsm, wide(top), ALU.add))
            link(stt(key, gsm, float(TOPK), key, ALU.is_le, ALU.mult))
            link(dve.tensor_tensor(chosen, pick, key, ALU.add), "chosen")
            link(dve.tensor_tensor(le, lw, bcast(best[:, :, 0:1], P, TT, NE), ALU.subtract), "logits_shifted")
            dve.wait_ge(sem("logits_exp"), 1)
            link(dve.tensor_tensor(gsm, le, chosen, ALU.mult))
            link(dve.reduce_sum(top, gsm, AX))
            link(dve.reciprocal(top, top))
            link(dve.tensor_tensor(gate[:, :, 0:NE], gsm, wide(top), ALU.mult))
            b = ready(dve, "places")
            pl = psum[:, b, 0:3 * NE]
            link(stt(place, view(pl, 0, TT, NE), 1.0, chosen, ALU.add, ALU.mult))
            link(dve.tensor_scalar(rank[:, :, 0:NE], place, -1.0, None, ALU.add))
            choose(0)
            count = pl[:, 2 * NE:3 * NE]
            link(dve.tensor_scalar(extra, count, float(SLOTS), None, ALU.is_gt))
            for m in range(2, T // SLOTS):
                link(stt(extra, count, float(SLOTS * m), extra, ALU.is_gt, ALU.add))
            link(dve.tensor_tensor_scan(upto, ones[:, 0:NE], extra, 0.0, ALU.mult, ALU.add), "places")
            def items(x):
                return bcast(x.unsqueeze(1), P, EXTRA, NE)

            def first_tables():
                link(dve.tensor_tensor(off, upto, extra, ALU.subtract))
                dve.wait_ge(sem("item_iota"), 1)

                link(dve.tensor_tensor(it2, items(off), it1, ALU.is_le))
                link(dve.tensor_tensor(it3, items(upto), it1, ALU.is_gt))
                link(dve.tensor_tensor(it2, it2, it3, ALU.mult))
                link(dve.tensor_tensor(it3, it2, items(ident[:, 0:NE]), ALU.mult))
                link(dve.reduce_sum(of_expert[:, NE:ITEMS], it3, AX))
                link(dve.tensor_tensor(it3, it2, items(off), ALU.mult))
                link(dve.reduce_sum(blk_of, it3, AX))
                link(dve.tensor_tensor(blk_of, it1[:, :, 0], blk_of, ALU.subtract))
                link(dve.tensor_scalar(blk_of, blk_of, float(SLOTS), float(SLOTS), ALU.mult, ALU.add))
                link(dve.tensor_tensor(it3, it2, items(reve[:, :]), ALU.mult))
                link(dve.reduce_sum(exp_of, it3, AX))
                link(dve.tensor_scalar(exp_of, exp_of, -1.0, 64.0, ALU.mult, ALU.add))

            def second_tables():
                for tt in range(TT):
                    link(dve.tensor_tensor(it3, it2, items(rank[:, tt, 0:NE]), ALU.mult))
                    link(dve.reduce_sum(it4, it3, AX))
                    link(dve.tensor_tensor(rank[:, tt, NE:ITEMS], it4, blk_of, ALU.subtract))
                    link(dve.tensor_tensor(it3, it2, items(gate[:, tt, 0:NE]), ALU.mult))
                    link(dve.reduce_sum(gate[:, tt, NE:ITEMS], it3, AX))
                link(dve.tensor_scalar(tabf[:, 0:1], upto[:, NE - 1:NE], float(NE), None, ALU.add))
                link(dve.tensor_scalar(tabf[:, 1:1 + NE], reve[:, :], -1.0, 64.0, ALU.mult, ALU.add))
                link(dve.tensor_scalar(tabf[:, 1 + NE:1 + ITEMS], exp_of, float(NE - 1), None, ALU.min))
                link(dve.memset(tabf[:, 1 + ITEMS:64], 0.0))
                link(dve.tensor_copy(tabi[:, :], tabf), "tabled")

            def light(i):
                dve.tensor_scalar(hot[0:NE, :], ones[0:NE, 0:SLOTS], of_expert[0:NE, bass.ds(i, 1)], None, ALU.mult) \
                   .then_inc(sem("hot"), 1)

            def fill_slots():
                g = vec("norm_ffn_g", 0, KD).unsqueeze(2)
                dve.tensor_tensor(xgT, view(psum[:, 4, :], 0, KD, SLOTS), bcast(g, P, KD, SLOTS), ALU.mult) \
                   .then_inc(sem("slots_in"), 1)

            dve.sem_inc(sem("swiglu"), 1)
            dve.sem_inc(sem("gated_turned"), 1)
            light(0)
            first_tables()
            dve.wait_ge(sem("gathered"), 1)
            fill_slots()

            def item(i, first=False):
                dve.wait_ge(sem("gated_turned"), i + 1)
                for tt in range(TT):
                    ins = dve.tensor_scalar(selg[:, tt, :], iotas[:, :], rank[:, tt, bass.ds(i, 1)],
                                            gate[:, tt, bass.ds(i, 1)], ALU.is_equal, ALU.mult)
                ins.then_inc(sem("gated"), 1)
                dve.wait_ge(sem("gathered"), i + 1)
                choose(i + 1)
                if first:
                    second_tables()
                for n in range(2):
                    dve.wait_ge(sem("piece_used"), i * 12 + 4 + 4 * n)
                    if n == 1:
                        dve.wait_ge(sem("gated_turned"), i + 2)
                        dve.tensor_copy(selgT, view(psum[:, 7, 0:256], 0, TT, P)).then_inc(sem("selgT"), 1)
                    hid = view(psum[:, 4 + n, :], 0, 256, 2)
                    dve.tensor_scalar(gl[:, n, :], hid[:, :, 0], 7.0, None, ALU.min).then_inc(sem("glu"), 1)
                    dve.tensor_scalar(ll[:, n, :], hid[:, :, 1], 7.0, -7.0, ALU.min, ALU.max) \
                       .then_inc(sem("lin"), 1)
                    dve.wait_ge(sem("lin"), i * 2 + n + 1)
                    stt(ll[:, n, :], ll[:, n, :], 1.0, gl[:, n, :], ALU.add, ALU.mult).then_inc(sem("glin"), 1)
                    dve.wait_ge(sem("glin"), i * 2 + n + 1)
                    dve.wait_ge(sem("sig"), i * 2 + n + 1)
                    dve.tensor_tensor(actv[:, n * 256:(n + 1) * 256], ll[:, n, :], sg[:, n, :], ALU.mult) \
                       .then_inc(sem("swiglu"), 1)
                dve.wait_ge(sem("gathered"), i + 2)
                fill_slots()
                dve.wait_ge(sem("act_turned"), i * 2 + 2)
                light(i + 1)

            item(0, first=True)
            n_items = dve.value_load(tabi[0:1, 0:1], min_val=NE, max_val=ITEMS)
            with dve.Fori(1, n_items) as i:
                item(i)
            dve.wait_ge(sem("scattered"), n_items)
            for tt in range(TT):
                for o2 in range(2):
                    cols = h[:, tt, o2 * 512:(o2 + 1) * 512]
                    link(dve.tensor_tensor(cols, psum[:, 2 * tt + o2, :], cols, ALU.add), "out_ready")

        @block.scalar
        def _(act):
            counts = {}

            def link(ins, name="scalar_step"):
                counts[name] = counts.get(name, 0) + 1
                ins.then_inc(sem(name), 1)
                act.wait_ge(sem(name), counts[name])

            def f(o, x, func, **kw):
                return act.activation(o, x, func, **kw)

            hn3 = view(hn, 0, TT, D)
            def inv_root(dst, src, name, scale=1.0, eps=EPS):
                link(f(dst, src, ACT.Ln, scale=scale, bias=eps_col[:, 0:1] if eps == EPS else eps_col[:, 1:2]))
                link(f(dst, dst, ACT.Exp, scale=-0.5), name)

            def root(dst, src, name):
                link(f(dst, src, ACT.Sqrt, bias=eps_col[:, 0:1]), name)

            def squares(which, src, dst):
                n = 2 * NORMS.index(which)
                for tt in range(TT):
                    if which == "x":
                        act.wait_ge(sem(f"x_in_{tt}"), 16)
                    link(f(dst[:, tt, :], src[:, tt, :], ACT.Square, accum_out=st[:, n + tt:n + tt + 1]))
                inv_root(st[:, n:n + 2], st[:, n:n + 2], "row_rs", scale=1.0 / D)

            LOGEXP, SIGMOID = "natural_log_exp_and_others", "sigmoid_and_others"
            act.preload_act_table_set(LOGEXP)
            act.wait_ge(sem("eps_set"), 1)
            squares("x", h, hn3)
            act.wait_ge(sem("mem_in"), 16)
            squares("mem", memx, view(kxT[:, :, :].rearrange("p a b -> p (a b)"), 0, TT, D))
            act.preload_act_table_set(SIGMOID)
            act.wait_ge(sem("shift_zeroed"), 1)

            def take(j):
                if j >= 2:
                    act.wait_ge(sem("mixed"), j - 1)
                b = ready(act, "job", j)
                link(f(shifted[:, j % 2, :, 1:T + 1], view(psum[:, b, :], 0, 2, T), ACT.Copy), "job_taken")

            take(J_LORA)
            act.wait_ge(sem("mixed"), 1)
            link(f(wdad[0:64, :], wdad[0:64, :], ACT.Tanh), "lora_in")
            link(f(gd, gd, ACT.Sigmoid), "lora_in")
            take(J_K)
            take(J_K + 1)
            take(J_R)
            take(J_R + 1)
            for name, dst in (("zw", sig), ("az", aT), ("gg", gT)):
                for i in range(2):
                    b = ready(act, name, i)
                    for p in (2 * i, 2 * i + 1):
                        src = psum[:, b, (p % 2) * T:(p % 2 + 1) * T]
                        if name == "gg":
                            ins = f(dst[:, p, :], src, ACT.Copy)
                        else:
                            ins = f(dst[:, p, :], src, ACT.Sigmoid,
                                    bias=vec("rwkv_w0" if name == "zw" else "rwkv_a0", p))
                        link(ins, name if p % 2 else "scalar_step")
            take(J_V)
            take(J_V + 1)
            act.preload_act_table_set(LOGEXP)
            for i in range(2):
                act.wait_ge(sem("kkr"), i + 1)
                link(f(sqr[:, 2 * i:2 * i + 2, :], kkr[:, 2 * i:2 * i + 2, :], ACT.Square), "key_squares")
            act.wait_ge(sem("cum"), 1)
            link(f(W[:, :, :], cum[:, :, :], ACT.Exp, scale=-KAPPA), "decays")
            link(f(Wi[:, :, :], cum[:, :, :], ACT.Exp, scale=KAPPA), "decays")
            link(f(Wp[:, :, :], tmp[:, :, :], ACT.Exp, scale=-KAPPA), "decays")
            act.preload_act_table_set("sqrt_and_others")
            act.wait_ge(sem("key_norms"), 2)
            for i in range(2):
                part = kk[:, 2 * i:2 * i + 2, :]
                link(f(part, part, ACT.Sqrt), "key_roots")
            b = ready(act, "kc")
            link(f(kcT[:, :, :], view(psum[:, b, :], 0, 4, P), ACT.Copy), "kc_copied")

            def keys_job(n):
                b = ready(act, "kv", n)
                link(f((vs, vw)[n], view(psum[:, b, T:2 * T], 0, TT, P), ACT.Copy))
                link(f((ksT, kwT)[n], psum[:, b, 0:T], ACT.Copy), "keys_taken")
                link(f(nsq[:, n, :], (ksT, kwT)[n], ACT.Square), "nsa_squares")

            def keys_norm(n):
                b = ready(act, "kvn", n)
                root(nrs[:, n, :], psum[:, b, 0:T], "nsa_rs")

            def queries_job(n):
                b = ready(act, "q", n)
                part = qT[:, 2 * n:2 * n + 2, :]
                link(f(part, view(psum[:, b, :], 0, 2, T), ACT.Copy), "queries_taken")
                if n:
                    ready(act, "kvn", 1)
                link(f((xsq, nsq)[n][:, :, :], part, ACT.Square), "nsa_squares")

            def queries_norm(n):
                b = ready(act, "qn", n)
                act.wait_ge(sem("queries_normed" if n else "keys_normed"), 1 if n else 2)
                root(nrs[:, :, :], view(psum[:, b, :], 0, 2, T), "nsa_rs")

            keys_job(0)
            keys_job(1)
            keys_norm(0)
            queries_job(0)
            keys_norm(1)
            queries_job(1)
            queries_norm(0)
            b = ready(act, "gl")
            link(f(gates[:, :, :], view(psum[:, b, 0:48], 0, 2, 24), ACT.Copy), "gates_taken")
            queries_norm(1)

            def cmpout_step():
                act.preload_act_table_set(LOGEXP)
                link(f(gates[:, :, :], gates[:, :, :], ACT.Exp, scale=-1.0), "gates_exp")
                b = ready(act, "cmp")
                link(f(csq[:, :], psum[:, b, 0:2 * NCMP], ACT.Exp, scale=-1.0), "cmp_exped")
                act.wait_ge(sem("cmp_hidden"), 1)
                b = ready(act, "kcmp")
                link(f(csq[:, 0:NCMP], psum[:, b, 0:NCMP], ACT.Square), "kcmp_squares")
                b = ready(act, "vcmp")
                link(f(vcmp[0:NCMP, :, :], view(psum[0:NCMP, b, 0:P], 0, NSA_G, HD), ACT.Copy), "vcmp")
                b = ready(act, "kcn")
                inv_root(crs[:, 0:NCMP], psum[:, b, 0:NCMP], "kcmp_rs")

            def tok_step(kind):
                dst = (tokA, tokB, tokK, tokV)[kind]
                for tt in range(TT):
                    b = ready(act, "tok", kind, tt)
                    link(f(dst[:, tt, :], psum[:, b, :], ACT.Copy), "tok")

            def inv_step(s):
                name, kind, _, _, dst = INV[s]
                if kind == "add":
                    return
                for q in range(2):
                    b = ready(act, "inv", s, q)
                    link(f(BUF[dst][:, 8 * q:8 * q + 8, :], view(psum[:, b, :], 0, 8, CH), ACT.Copy), "inv_copied")

            def qt_step():
                for c in range(2):
                    b = ready(act, "qt", c)
                    link(f(QT[:, c, :, :], view(psum[:, b, :], 0, 8, CH), ACT.Copy), "qt")

            def z_step():
                for q in range(2):
                    b = ready(act, "z", q)
                    link(f(Z[:, 8 * q:8 * q + 8, :], view(psum[:, b, :], 0, 8, CH), ACT.Copy), "z")

            def y_step(tt):
                b = ready(act, "ys", tt)
                link(f(Y[tt], psum[:, b, :], ACT.Copy), "y_state")

            def ymean_step(tt):
                act.wait_ge(sem("y_centred"), tt + 1)
                if tt:
                    ready(act, "yvar", 0)
                link(f(SQ, YC[tt], ACT.Square), "y_squared")

            def yvar_step(tt):
                b = ready(act, "yvar", tt)
                inv_root(Y[tt], psum[:, b, :], "y_rs", eps=GN_EPS)

            def xk_step(j):
                b = ready(act, "xk", j)
                part = kxT[:, 2 * j:2 * j + 2, :]
                link(f(part, view(psum[:, b, :], 0, 2, T), ACT.Copy), "kx_taken")
                if j:
                    ready(act, "xkn", j - 1)
                link(f(xsq[:, :, :], part, ACT.Square), "kx_squares")

            def xkn_step(j):
                xroots("xk", j, "kx_rs", "kx_normed")

            def xroots(name, j, rs, used):
                b = ready(act, name + "n", j)
                if j:
                    act.wait_ge(sem(used), j)
                if name == "xk":
                    root(xrs[:, :], psum[:, b, 0:T], rs)
                else:
                    inv_root(xrs[:, :], psum[:, b, 0:T], rs)

            def xv_step(j):
                b = ready(act, "xv", j)
                link(f(vxm[:, :, j * T:(j + 1) * T], view(psum[:, b, :], 0, 2, T), ACT.Copy), "vx")

            def cmpsc_step():
                for tt in range(TT):
                    act.wait_ge(sem("cmp_shifted"), tt + 1)
                    s = sc_c[:, tt, :, 0:NCMP]
                    link(f(s, s, ACT.Exp, scale=0.125), "cmp_exp")

            def score_step(u):
                tt, j = units[u]
                nk = P * (tt + 1)
                act.wait_ge(sem("score_max"), u + 1)
                if u >= 2:
                    act.wait_ge(sem("coef"), u - 1)
                for n in range(4):
                    s = S2[:, u % 2, n, 0:nk]
                    ins = f(s, s, ACT.Exp, bias=unit_stat(1, u)[:, n:n + 1], scale=0.125,
                            accum_out=unit_stat(2, u)[:, n:n + 1])
                    if n == 3:
                        link(ins, "exped")

            def turnp_step(u):
                tt, j = units[u]
                n = 2 * (tt + 1)
                b = ready(act, "pc", u)
                if u >= 2:
                    act.wait_ge(sem("pv_done"), u - 1)
                link(f(ptc[0:NCMP, u % 2, :, :], view(psum[0:NCMP, b, 0:2 * P], 0, 2, P), ACT.Copy), "ptc")
                for g in range(NSA_G):
                    b = ready(act, "pt", u, g)
                    link(f(PT[:, u % 2, g, 0:n, :], view(psum[:, b, 0:n * P], 0, n, P), ACT.Copy), "pt")

            def pv_step(u):
                tt, j = units[u]
                if j == 3:
                    act.wait_ge(sem("pv_done"), 4 * (tt + 1))
                    link(f(onT[:, :, tt * P:(tt + 1) * P], view(psum[:, 7, :], 0, 4, P), ACT.Copy), "on")

            steps = {"cmpout": cmpout_step, "tok": tok_step, "inv": inv_step, "qt": qt_step, "z": z_step,
                     "y": y_step,
                     "ymean": ymean_step, "yvar": yvar_step, "xk": xk_step, "xkn": xkn_step, "xv": xv_step, "cmpsc": cmpsc_step,
                     "score": score_step, "turnp": turnp_step, "pv": pv_step}
            for step, *args in order:
                if step in steps:
                    steps[step](*args)

            def block_squares(which):
                for j in range(4):
                    act.wait_ge(sem("h_" + which), j + 1)
                    for tt in range(TT):
                        link(f(junk[:, 0:T], h[:, tt, j * T:(j + 1) * T], ACT.Square, accum_out=psq[:, tt, j:j + 1]),
                             "part_squares")
                n = ("mixed", "crossed").index(which)
                act.wait_ge(sem("squares_summed"), n + 1)
                c = st[:, 4 + 2 * n:6 + 2 * n]
                inv_root(c, c, "token_rs", scale=1.0 / D)

            block_squares("mixed")
            for step, n in CROSS:
                if step == "project":
                    if n == 0:
                        b = ready(act, "rsB")
                        link(f(rsB, psum[:, b, 0:T], ACT.Copy), "rsB")
                    act.wait_ge(sem("qx_scaled"), n + 1)
                    if n:
                        ready(act, "xqn", n - 1)
                    link(f(xsq[:, :, :], qxT[:, 2 * n:2 * n + 2, :], ACT.Square), "qx_squares")
                if step == "norm":
                    xroots("xq", n, "qx_rs", "qx_normed")
                if step == "score":
                    b = ready(act, "xs", n)
                    act.wait_ge(sem("xmax"), n + 1)
                    if n >= 2:
                        ready(act, "xp", n - 2)
                    link(f(xs[:, n % 2, :], psum[:, b, 0:MEM], ACT.Exp, bias=st[:, 42 + n % 2:43 + n % 2],
                           scale=float(X_HD) ** -0.5, accum_out=st[:, 44 + n % 2:45 + n % 2]), "xscores")
                if step == "turn":
                    b = ready(act, "xp", n)
                    if n >= 2:
                        ready(act, "xo", n - 2)
                    link(f(xpt[:, n % 2, :, :], view(psum[:, b, 0:256], 0, 2, P), ACT.Copy), "xpt")
                if step == "pv":
                    tt, i = n % 2, n // 2
                    b = ready(act, "xo", n)
                    link(f(oxT[:, 2 * i:2 * i + 2, tt * P:(tt + 1) * P], view(psum[:, b, 0:256], 0, 2, P),
                           ACT.Copy), "ox")
            block_squares("crossed")
            act.wait_ge(sem("logits_shifted"), 1)
            link(f(le, le, ACT.Exp), "logits_exp")

            act.preload_act_table_set(SIGMOID)
            act.sem_inc(sem("act_out"), 1)
            act.sem_inc(sem("y_out"), 1)

            def item(i):
                for n in range(2):
                    act.wait_ge(sem("glu"), i * 2 + n + 1)
                    f(sg[:, n, :], gl[:, n, :], ACT.Sigmoid, scale=1.702).then_inc(sem("sig"), 1)
                for n in range(2):
                    act.wait_ge(sem("act_turned"), i * 2 + n + 1)
                    f(actT[:, 2 * n:2 * n + 2, :], view(psum[:, 6, n * 256:(n + 1) * 256], 0, 2, P),
                      ACT.Copy).then_inc(sem("act_out"), 1)
                act.wait_ge(sem("piece_used"), i * 12 + 12)
                f(yb, psum[:, 7, :], ACT.Copy).then_inc(sem("y_out"), 1)

            item(0)
            act.wait_ge(sem("tabled"), 1)
            n_items = act.value_load(tabi[0:1, 0:1], min_val=NE, max_val=ITEMS)
            with act.Fori(1, n_items) as i:
                item(i)

        @block.gpsimd
        def _(pool):
            step = [0]

            def link(ins, name="pool_step"):
                step[0] += name == "pool_step"
                ins.then_inc(sem(name), 1)
                pool.wait_ge(sem(name), step[0] if name == "pool_step" else 1)

            def keep(o, op, base, pattern, mult, fill=0.0):
                link(pool.affine_select(out=o, in_=o, compare_op=op, fill=fill, base=base, pattern=pattern,
                                        channel_multiplier=mult))

            def within(o, size):
                n = P // size
                keep(o, ALU.is_ge, 0, [[-size, n], [0, size]], 1)
                keep(o, ALU.is_ge, size - 1, [[size, n], [0, size]], -1)

            link(pool.memset(eps_col[:, 0:1], EPS))
            link(pool.memset(eps_col[:, 1:2], GN_EPS), "eps_set")
            link(pool.memset(rb[:, :], 0.0), "rb_zeroed")
            link(pool.memset(ident[:, :], 0.0))
            keep(ident[:, :], ALU.not_equal, 0, [[-1, P]], 1, fill=1.0)
            link(pool.tensor_tensor(identc[:, :], ident[:, 0:CH], ident[:, CH:P], ALU.add), "ident_set")
            link(pool.memset(mreset[:, :], 1.0))
            link(pool.memset(mreset[:, 0:T:CH], 0.0))
            link(pool.memset(blk[:, :], 1.0))
            within(blk[:, :], HD)
            link(pool.memset(blk64[:, :], 1.0 / HD))
            within(blk64[:, :], HD)
            link(pool.memset(o256[:, :], 1.0 / X_HD), "consts")
            link(pool.memset(mfull, 1.0))
            for i, (size, op) in enumerate(((16, ALU.is_gt), (CH, ALU.is_ge), (CH, ALU.is_gt), (CH, ALU.is_ge))):
                keep(mfull[:, i, :], op, 0, [[1, P]], -1)
                within(mfull[:, i, :], size)
            for i, size in ((4, 16), (5, 32), (6, CH)):
                keep(mfull[:, i, :], ALU.is_gt, 0, [[-1, P]], 1)
                within(mfull[:, i, :], size)
            link(pool.tensor_tensor(masks4[:, :, :], mfull[:, 0:4, 0:CH], mfull[:, 0:4, CH:P], ALU.add))
            link(pool.tensor_tensor(masks3[:, :, :], mfull[:, 4:7, 0:CH], mfull[:, 4:7, CH:P], ALU.add))
            link(pool.tensor_tensor(masks3[:, 2, :], masks3[:, 2, :], masks3[:, 1, :], ALU.subtract))
            link(pool.tensor_tensor(masks3[:, 1, :], masks3[:, 1, :], masks3[:, 0, :], ALU.subtract), "masks")
            link(pool.iota(dist[:, :], [[1, T]], base=-P, channel_multiplier=-1,
                           allow_small_or_imprecise_dtypes=True))
            keep(dist[:, :], ALU.is_ge, P, [[-1, T]], 1, fill=NEG)
            for tt in range(TT):
                o = distc[:, tt, :]
                link(pool.iota(o, [[STRIDE, 16]], base=CMP - 1 - P * tt, channel_multiplier=-1,
                               allow_small_or_imprecise_dtypes=True))
                keep(o, ALU.is_ge, P * tt - CMP + 1, [[-STRIDE, 16]], 1, fill=NEG)
                link(pool.memset(maskc[:, tt, :], 1.0))
                keep(maskc[:, tt, :], ALU.is_ge, P * tt - CMP + 1, [[-STRIDE, 16]], 1)
            link(pool.iota(iotas[:, :], [[0, 2], [1, SLOTS]], base=0, channel_multiplier=0,
                           allow_small_or_imprecise_dtypes=True))
            link(pool.iota(reve[:, :], [[-1, NE]], base=64, channel_multiplier=0,
                           allow_small_or_imprecise_dtypes=True))
            link(pool.memset(ones[:, :], 1.0))
            link(pool.memset(before[:, :], 1.0))
            keep(before[:, :], ALU.is_gt, 0, [[1, P]], -1)
            link(pool.memset(sc_c[:, :, :, :], 0.0), "late_consts")
            for tt in range(TT):
                for i in range(NSA_H):
                    ins = pool.tensor_scalar(sc_c[:, tt, i, :], distc[:, tt, :], 8.0 * SLOPE[i], None, ALU.mult)
            ins.then_inc(sem("cmp_bias"), 1)

            for j in range(J_V + 2):
                pool.wait_ge(sem("job_taken"), j + 1)
                if j >= 2:
                    pool.wait_ge(sem("mixed"), j - 1)
                pool.tensor_tensor(diff[:, j % 2, :, :], shifted[:, j % 2, :, 0:T], shifted[:, j % 2, :, 1:T + 1],
                                   ALU.subtract).then_inc(sem("differenced"), 1)

            def turnp_step(u):
                tt, j = units[u]
                nk = P * (tt + 1)
                pool.wait_ge(sem("coef"), u + 1)
                s = S2[:, u % 2, :, 0:nk]
                c = unit_stat(3, u).unsqueeze(2)
                pool.tensor_tensor(s, s, bcast(c, P, 4, nk), ALU.mult).then_inc(sem("probs"), 1)

            for step, *args in order:
                if step == "turnp":
                    turnp_step(*args)
            pool.wait_ge(sem("ox"), 8)
            pool.iota(it1, [[1, EXTRA], [0, NE]], base=0, channel_multiplier=0,
                      allow_small_or_imprecise_dtypes=True).then_inc(sem("item_iota"), 1)

            pool.wait_ge(sem("h_crossed"), 4)
            pool.dma_start(bias[0:NE, 0:2 * DE], a["mlp1_b"][0]).then_inc(sem("bias_in"), 16)
            pool.dma_start(bias[0:NE, 2 * DE:3 * DE], a["mlp2_b"][0]).then_inc(sem("bias_in"), 16)

        @block.sync
        def _(sp):
            for tt in range(TT):
                sp.dma_start(h[:, tt, :], a["x"][0, tt * P:(tt + 1) * P, :]).then_inc(sem(f"x_in_{tt}"), 16)
            sp.dma_start(vrows[0:8, :], a["norm_mix_g"][0].rearrange("(a b) -> a b", b=P)) \
              .then_inc(sem("gain_in"), 16)

            def job_in(j):
                name, c = JOBS[j]
                if j >= WSLOTS:
                    sp.wait_ge(sem("tile_ready"), last_tile(j - WSLOTS) + 1)
                if name == "q":
                    o = slot(j)[:, 0:2048].rearrange("p (k i g d) -> p g i k d", k=8, i=2, g=2)
                    for g in range(NSA_G):
                        for i in range(2):
                            c0 = C_Q + 256 * g + 128 * c + HD * i
                            sp.dma_start(o[:, g, i], a["w_in"][0, :, c0:c0 + HD].rearrange("(k p) n -> p k n", p=P)) \
                              .then_inc(sem(f"weights_in_{j % WSLOTS}"), 16)
                    return
                if name == "cmp":
                    o = view(slot(j), 0, 2, CMP // 2, HD)
                    for kind, w in enumerate(("cmp_k_w1", "cmp_v_w1")):
                        sp.dma_start(o[:, kind], a[w][0].rearrange("(m p) e -> p m e", p=P)) \
                          .then_inc(sem(f"weights_in_{j % WSLOTS}"), 16)
                    return
                if name == "w_out":
                    o = wjob(j)
                    for g in range(NSA_G):
                        src = a["w_out"][0, 256 * g:256 * g + 256, c:c + T]
                        sp.dma_start(o[64 * g:64 * g + 64, 0:4, :], src.rearrange("(j d) n -> d j n", d=HD)) \
                          .then_inc(sem(f"weights_in_{j % WSLOTS}"), 16)
                    sp.dma_start(o[:, 4:8, :], a["w_out"][0, 512:1024, c:c + T]
                                 .rearrange("(k p) n -> p k n", p=P)) \
                      .then_inc(sem(f"weights_in_{j % WSLOTS}"), 16)
                    return
                if name == "gl":
                    sp.dma_start(wjob(j, 24), a["w_in"][0, :, c:c + 24].rearrange("(k p) n -> p k n", p=P)) \
                      .then_inc(sem(f"weights_in_{j % WSLOTS}"), 16)
                    return
                sp.dma_start(wjob(j), a[name][0, :, c:c + T].rearrange("(k p) n -> p k n", p=P)) \
                  .then_inc(sem(f"weights_in_{j % WSLOTS}"), 16)

            LAST = {J_KC: ("kc",), J_KS: ("kv", 0), J_KW: ("kv", 1), J_Q: ("q", 0), J_Q + 1: ("q", 1),
                    J_GL: ("gl",), J_CMP: ("cmp",)}

            def last_tile(j):
                if j in LAST:
                    return tiles[LAST[j]][1]
                for base, name in ((J_XO, "xout"), (J_XQ, "xq"), (J_OUT, "wout"), (J_XV, "xv"), (J_XK, "xk")):
                    if j >= base:
                        return tiles[name, j - base][1]
                return tiles["job", j][1]

            for j in range(WSLOTS):
                job_in(j)
                if j == 0:
                    for name, n in VROWS[1:]:
                        src = a[name][0]
                        r0 = VCOL[name]
                        if name == "rwkv_r_k":
                            src = src.rearrange("(a b) c -> a (b c)", b=2)
                            o = vrows[r0:r0 + n, :]
                        elif n > 1:
                            src = src.rearrange("(a b) -> a b", b=P)
                            o = vrows[r0:r0 + n, :]
                        else:
                            sp.dma_start(vrows[r0:r0 + 1, 0:HD], a[name][0:1, :]).then_inc(sem("rows_in"), 16)
                            sp.dma_start(vrows[r0:r0 + 1, HD:P], a[name][0:1, :]).then_inc(sem("rows_in"), 16)
                            continue
                        sp.dma_start(o, src).then_inc(sem("rows_in"), 16)
                    for kind, name in enumerate(("cmp_pe_k", "cmp_pe_v")):
                        sp.dma_start(perow[0:CMP // 2, kind, :], a[name][0].rearrange("(m two) d -> m (two d)", two=2)) \
                          .then_inc(sem("rows_in"), 16)
                    sp.dma_start(memx, a["mem"][0].rearrange("(t p) d -> p t d", p=P)).then_inc(sem("mem_in"), 16)
                    sp.dma_start(lora[0:64, 0, :], a["rwkv_w_up"][0]).then_inc(sem("small_in"), 16)
                    sp.dma_start(lora[64:128, 0, :], a["rwkv_a_up"][0]).then_inc(sem("small_in"), 16)
                    sp.dma_start(lora[:, 1, :], a["rwkv_g_up"][0]).then_inc(sem("small_in"), 16)
                    for kind, name in enumerate(("cmp_k_w2", "cmp_v_w2")):
                        sp.dma_start(cw2[HD * kind:HD * kind + HD, :], a[name][0]).then_inc(sem("small_in"), 16)
                    sp.dma_start(rw[:, :, :], a["router_w"][0].rearrange("(k p) n -> p k n", p=P)) \
                      .then_inc(sem("small_in"), 16)
                    sp.wait_ge(sem("rb_zeroed"), 1)
                    sp.dma_start(rb[0:1, 2 * NE:3 * NE], a["router_b"][0:1, :]).then_inc(sem("small_in"), 16)

            w1_src = a["mlp1_w"][0].rearrange("e (k p) (h n c) -> e n h p k c", p=P, h=2, n=2)
            w2_src = a["mlp2_w"][0].rearrange("e (k p) n -> e p k n", p=P)
            w1_dst = w1.rearrange("p k (h n c) -> p n k h c", h=2, n=2)

            def piece(e, c):
                if c < 8:
                    n, k, half = c // 4, 4 * (c // 2 % 2), c % 2
                    sp.dma_start(w1_dst[:, n, k:k + 4, half], w1_src[bass.ds(e, 1), n, half, :, k:k + 4]
                                 .rearrange("e p k c -> p (e k) c")).then_inc(sem(f"w1_in_{c}"), 16)
                else:
                    n, q = (c - 8) // 2, c % 2
                    k = 4 * q + 2 * n
                    sp.dma_start(w2[:, k:k + 2, :], w2_src[bass.ds(e, 1), :, k:k + 2, :]
                                 .rearrange("e p k n -> p (e k) n")).then_inc(sem(f"w2_in_{c - 8}"), 16)

            def piece_ahead(c):
                if c < 2:
                    sp.wait_ge(sem("tile_ready"), tiles[(("xv", 3), ("wout", 3))[c]][1] + 1)
                elif c == 2:
                    sp.wait_ge(sem("ox"), 8)
                else:
                    sp.wait_ge(sem("tile_ready"), tiles["xout", 3][1] + 1)
                k, half = 4 * (c // 2), c % 2
                sp.dma_start(ahead[c], w1_src[1:2, 0, half, :, k:k + 4].rearrange("e p k c -> p (e k) c")) \
                  .then_inc(sem(f"ahead_in_{c}"), 16)

            left = list(range(12))
            for j in range(WSLOTS, len(JOBS)):
                job_in(j)
                if j == J_OUT + 2:
                    sp.wait_ge(sem("rwkv_out"), 2)
                if j >= J_OUT + 2:
                    for c in left[:2]:
                        piece(0, c)
                    left = left[2:]

            for c in range(4):
                piece_ahead(c)

            def item(i, e, pieces=range(12)):
                for c in pieces:
                    sp.wait_ge(sem("piece_used"), i * 12 + (c - 11))
                    piece(e, c)

            for c in range(4):
                sp.wait_ge(sem("piece_used"), c + 1)
                piece(2, c)
            item(1, 1, range(4, 12))
            item(2, 2, range(4, 12))
            with sp.Fori(3, NE - 1) as i:
                item(i, i)
            sp.wait_ge(sem("tabled"), 1)
            n_items = sp.value_load(tabi[0:1, 0:1], min_val=NE, max_val=ITEMS)
            with sp.Fori(NE - 1, n_items) as i:
                e = sp.value_load(tabi[0:1, bass.ds(i + 1, 1)], min_val=0, max_val=NE - 1)
                item(i, e)
            for tt in range(TT):
                sp.wait_ge(sem("out_ready"), 2 * tt + 2)
                sp.dma_start(out[0, tt * P:(tt + 1) * P, :], h[:, tt, :]).then_inc(sem("out_done"), 16)
            sp.wait_ge(sem("out_done"), 32)


_INS = ["x", "mem", "norm_mix_g", "w_in", "q_norm_g", "k_cmp_norm_g", "k_slc_norm_g", "k_win_norm_g",
        "cmp_pe_k", "cmp_pe_v", "cmp_k_w1", "cmp_k_w2", "cmp_v_w1", "cmp_v_w2",
        "rwkv_mu", "rwkv_w0", "rwkv_w_up", "rwkv_a0", "rwkv_a_up", "rwkv_g_up", "rwkv_k_k", "rwkv_k_a",
        "rwkv_r_k", "rwkv_ln_w", "rwkv_ln_b", "w_out", "norm_x_g", "norm_mem_g", "xq_w", "xk_w", "xv_w",
        "xq_norm_g", "xk_norm_g", "xo_w", "norm_ffn_g", "router_w", "router_b",
        "mlp1_w", "mlp1_b", "mlp2_w", "mlp2_b"]


def kernel(**inputs):
    import concourse.bacc as bacc
    from concourse.bass_utils import run_bass_kernel_spmd

    nc = bacc.Bacc("TRN2", target_bir_lowering=False, num_devices=1)
    arrays, args = {}, {}
    for name in _INS:
        arr = np.ascontiguousarray(inputs[name])
        arrays[f"in_{name}"] = arr
        args[name] = nc.dram_tensor(f"in_{name}", arr.shape, mybir.dt.from_np(arr.dtype),
                                    kind="ExternalInput").ap()
    out = nc.dram_tensor("out_h", (1, T, D), F32, kind="ExternalOutput").ap()
    build(nc, args, out)
    r = run_bass_kernel_spmd(nc, [arrays], core_ids=[0])
    return r.results[0]["out_h"]
```
